# Optimizing a Trainium2 kernel written in Bass

```python
import jax, jax.numpy as jnp
from jax import lax
import numpy as np

D_MODEL = 2048
BATCH = 1
SEQ = 256
DEPTH = 1

MIX_WIDTH = D_MODEL
HGRN_HEADS = 8
HGRN_KDIM = 128
HGRN_VDIM = MIX_WIDTH // 2 // HGRN_HEADS
HGRN_CHUNK = 64
ATTN_HEADS = 8
ATTN_HEAD_DIM = MIX_WIDTH // 2 // ATTN_HEADS
IDX_HEADS = 16
IDX_DIM = 64
DSA_TOPK = 256
DSA_QBLOCK = 64
N_MEM = 256
CROSS_HEADS = 4
CROSS_HEAD_DIM = 128
CROSS_WIDTH = CROSS_HEADS * CROSS_HEAD_DIM
D_FF = 4 * D_MODEL
EPS = 1e-6

HG_K = HGRN_HEADS * HGRN_KDIM
HG_V = HGRN_HEADS * HGRN_VDIM
ATT_W = ATTN_HEADS * ATTN_HEAD_DIM
SPLIT_SIZES = (HG_K, HG_K, HG_V, HG_V, ATT_W, ATT_W, ATT_W, IDX_HEADS * IDX_DIM, IDX_DIM, IDX_HEADS)
SPLIT_POINTS = tuple(int(p) for p in np.cumsum(SPLIT_SIZES)[:-1])
IN_WIDTH = int(sum(SPLIT_SIZES))
OUT_WIDTH = HG_V + ATT_W


def rms_norm(x, gain):
    xf = x.astype(jnp.float32)
    y = xf * lax.rsqrt(jnp.mean(xf * xf, axis=-1, keepdims=True) + EPS)
    return (y * gain.astype(jnp.float32)).astype(x.dtype)

def chunk_gated_recurrence(q, k, v, log_f):
    B, S, H, K = q.shape
    V = v.shape[-1]
    C = HGRN_CHUNK
    n = S // C

    def to_chunks(t):
        return t.reshape(B, n, C, H, t.shape[-1]).transpose(1, 0, 3, 2, 4)

    causal = jnp.tril(jnp.ones((C, C), dtype=bool))[:, :, None]

    def step(state, inp):
        qb, kb, vb, gb = inp
        A = jnp.cumsum(gb, axis=2)
        o_inter = jnp.einsum('bhtk,bhkv->bhtv', qb * jnp.exp(A), state)
        diff = A[:, :, :, None, :] - A[:, :, None, :, :]
        decay = jnp.exp(jnp.where(causal, diff, -jnp.inf))
        scores = jnp.einsum('bhtk,bhtsk,bhsk->bhts', qb, decay, kb)
        o_intra = jnp.einsum('bhts,bhsv->bhtv', scores, vb)
        A_last = A[:, :, -1:, :]
        new_state = state * jnp.exp(A_last[:, :, 0, :])[..., None] + jnp.einsum(
            'bhsk,bhsv->bhkv', kb * jnp.exp(A_last - A), vb)
        return new_state, o_inter + o_intra

    state0 = jnp.zeros((B, H, K, V), jnp.float32)
    _, ys = lax.scan(step, state0, (to_chunks(q), to_chunks(k), to_chunks(v), to_chunks(log_f)))
    return ys.transpose(1, 0, 3, 2, 4).reshape(B, S, H, V)

def hgrn2_group(q, f_pre, i, g, lb, onorm):
    B, S, _ = q.shape
    f32 = jnp.float32
    q = jax.nn.silu(q.reshape(B, S, HGRN_HEADS, HGRN_KDIM).astype(f32)) * (HGRN_KDIM ** -0.5)
    lb = lb.reshape(HGRN_HEADS, HGRN_KDIM).astype(f32)
    f = lb + (1.0 - lb) * jax.nn.sigmoid(f_pre.reshape(B, S, HGRN_HEADS, HGRN_KDIM).astype(f32))
    v = i.reshape(B, S, HGRN_HEADS, HGRN_VDIM).astype(f32)
    o = chunk_gated_recurrence(q, 1.0 - f, v, jnp.log(f))
    o = rms_norm(o, onorm) * jax.nn.silu(g.reshape(B, S, HGRN_HEADS, HGRN_VDIM).astype(f32))
    return o.reshape(B, S, HG_V).astype(i.dtype)

def dsa_group(q, k, v, q_idx, k_idx, w_idx, qnorm, knorm):
    B, S, _ = q.shape
    f32 = jnp.float32
    H, Dh = ATTN_HEADS, ATTN_HEAD_DIM
    q = rms_norm(q.reshape(B, S, H, Dh), qnorm)
    k = rms_norm(k.reshape(B, S, H, Dh), knorm)
    v = v.reshape(B, S, H, Dh)
    q_idx = q_idx.reshape(B, S, IDX_HEADS, IDX_DIM).astype(f32)
    k_idx = k_idx.astype(f32)
    w_idx = w_idx.astype(f32) * (IDX_HEADS ** -0.5 * IDX_DIM ** -0.5)
    top = min(DSA_TOPK, S // 4)
    n_blocks = S // DSA_QBLOCK
    s_pos = jnp.arange(S)
    scale = Dh ** -0.5
    gather = jax.vmap(lambda kv, ix: kv[ix])

    def block(bi):
        start = bi * DSA_QBLOCK
        qb = lax.dynamic_slice_in_dim(q, start, DSA_QBLOCK, axis=1)
        qib = lax.dynamic_slice_in_dim(q_idx, start, DSA_QBLOCK, axis=1)
        wb = lax.dynamic_slice_in_dim(w_idx, start, DSA_QBLOCK, axis=1)
        t_pos = start + jnp.arange(DSA_QBLOCK)
        logits = jnp.einsum('bthd,bsd->bths', qib, k_idx)
        idx_score = jnp.einsum('bth,bths->bts', wb, jax.nn.relu(logits))
        visible = s_pos[None, :] <= t_pos[:, None]
        idx_score = jnp.where(visible[None], idx_score, -jnp.inf)
        _, sel = lax.top_k(idx_score, top)
        valid = sel <= t_pos[None, :, None]
        kg = gather(k, sel)
        vg = gather(v, sel)
        s = jnp.einsum('bthd,btkhd->bthk', qb, kg).astype(f32) * scale
        s = jnp.where(valid[:, :, None, :], s, -jnp.inf)
        p = jax.nn.softmax(s, axis=-1).astype(vg.dtype)
        return jnp.einsum('bthk,btkhd->bthd', p, vg)

    out = lax.map(block, jnp.arange(n_blocks))
    return out.transpose(1, 0, 2, 3, 4).reshape(B, S, ATT_W)

def hybrid_mixer(xn, w_in, lb, hgrn_onorm, attn_qnorm, attn_knorm, w_out):
    proj = xn @ w_in
    (hq, hf, hi, hg, aq, ak, av, iq, ik, iw) = jnp.split(proj, SPLIT_POINTS, axis=-1)
    y_h = hgrn2_group(hq, hf, hi, hg, lb, hgrn_onorm)
    y_a = dsa_group(aq, ak, av, iq, ik, iw, attn_qnorm, attn_knorm)
    return jnp.concatenate([y_h, y_a], axis=-1) @ w_out

def memory_cross_attention(hn, memn, wq, wk, wv, wo, qnorm, knorm):
    B, S, _ = hn.shape
    M = memn.shape[1]
    q = rms_norm((hn @ wq).reshape(B, S, CROSS_HEADS, CROSS_HEAD_DIM), qnorm)
    k = rms_norm((memn @ wk).reshape(B, M, CROSS_HEADS, CROSS_HEAD_DIM), knorm)
    v = (memn @ wv).reshape(B, M, CROSS_HEADS, CROSS_HEAD_DIM)
    s = jnp.einsum('bthd,bmhd->bhtm', q, k).astype(jnp.float32) * (CROSS_HEAD_DIM ** -0.5)
    p = jax.nn.softmax(s, axis=-1).astype(v.dtype)
    o = jnp.einsum('bhtm,bmhd->bthd', p, v).reshape(B, S, CROSS_WIDTH)
    return o @ wo

def sqrelu_mlp(hn, w_up, w_down):
    return jnp.square(jax.nn.relu(hn @ w_up)) @ w_down

def first_inputs(seed: int = 0) -> dict:
    key = jax.random.key(seed)
    ks = jax.random.split(key, 20)
    f32 = jnp.float32
    nrm = lambda k, shape, fan_in: jax.random.normal(k, shape, f32) * (fan_in ** -0.5)
    gain = lambda k, shape: 1.0 + 0.02 * jax.random.normal(k, shape, f32)
    L = DEPTH
    return {
        "x": jax.random.normal(ks[0], (BATCH, SEQ, D_MODEL), f32),
        "mem": jax.random.normal(ks[1], (BATCH, N_MEM, D_MODEL), f32),
        "norm_mix": gain(ks[2], (L, D_MODEL)),
        "w_in": nrm(ks[3], (L, D_MODEL, IN_WIDTH), D_MODEL),
        "hgrn_lb_logits": 0.1 * jax.random.normal(ks[4], (L + 1, HG_K), f32),
        "hgrn_onorm": gain(ks[5], (L, HGRN_VDIM)),
        "attn_qnorm": gain(ks[6], (L, ATTN_HEAD_DIM)),
        "attn_knorm": gain(ks[7], (L, ATTN_HEAD_DIM)),
        "w_out": nrm(ks[8], (L, OUT_WIDTH, D_MODEL), OUT_WIDTH),
        "norm_cross": gain(ks[9], (L, D_MODEL)),
        "mem_norm": gain(ks[10], (L, D_MODEL)),
        "wq_x": nrm(ks[11], (L, D_MODEL, CROSS_WIDTH), D_MODEL),
        "wk_x": nrm(ks[12], (L, D_MODEL, CROSS_WIDTH), D_MODEL),
        "wv_x": nrm(ks[13], (L, D_MODEL, CROSS_WIDTH), D_MODEL),
        "wo_x": nrm(ks[14], (L, CROSS_WIDTH, D_MODEL), CROSS_WIDTH),
        "xq_norm": gain(ks[15], (L, CROSS_HEAD_DIM)),
        "xk_norm": gain(ks[16], (L, CROSS_HEAD_DIM)),
        "norm_mlp": gain(ks[17], (L, D_MODEL)),
        "w_up": nrm(ks[18], (L, D_MODEL, D_FF), D_MODEL),
        "w_down": nrm(ks[19], (L, D_FF, D_MODEL), D_FF),
    }

def first_block(x, mem, norm_mix, w_in, hgrn_lb_logits, hgrn_onorm, attn_qnorm, attn_knorm, w_out,
              norm_cross, mem_norm, wq_x, wk_x, wv_x, wo_x, xq_norm, xk_norm,
              norm_mlp, w_up, w_down):
    lb_all = jnp.cumsum(jax.nn.softmax(hgrn_lb_logits.astype(jnp.float32), axis=0), axis=0)
    h = x
    for l in range(DEPTH):
        h = h + hybrid_mixer(rms_norm(h, norm_mix[l]), w_in[l], lb_all[l], hgrn_onorm[l],
                             attn_qnorm[l], attn_knorm[l], w_out[l])
        h = h + memory_cross_attention(rms_norm(h, norm_cross[l]), rms_norm(mem, mem_norm[l]),
                                       wq_x[l], wk_x[l], wv_x[l], wo_x[l], xq_norm[l], xk_norm[l])
        h = h + sqrelu_mlp(rms_norm(h, norm_mlp[l]), w_up[l], w_down[l])
    return h


DEPTH_2 = 2

MEM_LEN = 256
HEAD_DIM = 128
MIX_W = D_MODEL
MEM_HEADS = 4
MEM_W = MEM_HEADS * HEAD_DIM
POOL_W = MIX_W - MEM_W
POOL_WINDOWS = (2, 4, 8, 16)
POOL_GROUPS = len(POOL_WINDOWS)
POOL_GC = POOL_W // POOL_GROUPS
NSA_W = MIX_W - MEM_W
NSA_HEADS = NSA_W // HEAD_DIM
NSA_KV_HEADS = 4
NSA_GROUP = NSA_HEADS // NSA_KV_HEADS
NSA_KV_W = NSA_KV_HEADS * HEAD_DIM
CMP_LEN = 32
CMP_STRIDE = 16
CMP_HID = 256
SEL_LEN = 64
SEL_TOPK = 16
WINDOW = 512
Q_CHUNK = 32
ROT_DIM = HEAD_DIM // 4
ROPE_THETA = 500000.0
NORM_EPS = 1e-6
FORCE_SCORE = 1e4
NEG_INF = -1e30


def rmsnorm(x, g):
    xf = x.astype(jnp.float32)
    y = xf * lax.rsqrt(jnp.mean(xf * xf, axis=-1, keepdims=True) + NORM_EPS)
    return (y * g.astype(jnp.float32)).astype(x.dtype)

def rope(x, pos):
    half = ROT_DIM // 2
    inv = ROPE_THETA ** (-jnp.arange(half, dtype=jnp.float32) * 2.0 / ROT_DIM)
    ang = pos.astype(jnp.float32)[..., None] * inv
    cos = jnp.cos(ang)[:, :, None, :]
    sin = jnp.sin(ang)[:, :, None, :]
    xr = x[..., :ROT_DIM].astype(jnp.float32)
    x1, x2 = xr[..., :half], xr[..., half:]
    rot = jnp.concatenate([x1 * cos - x2 * sin, x2 * cos + x1 * sin], axis=-1)
    return jnp.concatenate([rot.astype(x.dtype), x[..., ROT_DIM:]], axis=-1)

def masked_softmax(s, mask):
    s = jnp.where(mask, s.astype(jnp.float32), NEG_INF)
    p = jax.nn.softmax(s, axis=-1)
    return jnp.where(mask, p, 0.0)

def memory_attention(q, mem, mem_g, w_mem_kv):
    b, m, _ = mem.shape
    mn = rmsnorm(mem, mem_g)
    kv = (mn @ w_mem_kv).reshape(b, m, 2, MEM_HEADS, HEAD_DIM)
    k, v = kv[:, :, 0], kv[:, :, 1]
    s = jnp.einsum('bshd,bmhd->bhsm', q, k).astype(jnp.float32)
    p = jax.nn.softmax(s, axis=-1).astype(v.dtype)
    o = jnp.einsum('bhsm,bmhd->bshd', p, v)
    return o.reshape(q.shape[0], q.shape[1], MEM_W)

def multiscale_pool(u, w_pool, scale):
    b, s, _ = u.shape
    ug = u.reshape(b, s, POOL_GROUPS, POOL_GC)
    t1 = jnp.arange(1, s + 1, dtype=jnp.float32)[None, :, None]
    outs = []
    for gi, win in enumerate(POOL_WINDOWS):
        v = ug[:, :, gi].astype(jnp.float32)
        c = jnp.cumsum(v, axis=1)
        c_lag = jnp.pad(c, ((0, 0), (win, 0), (0, 0)))[:, :s]
        outs.append((c - c_lag) / jnp.minimum(t1, float(win)) - v)
    pooled = jnp.stack(outs, axis=2).astype(u.dtype)
    mixed = jnp.einsum('bsgc,gcd->bsgd', pooled, w_pool).reshape(b, s, POOL_W)
    return mixed * scale

def nsa_shared_kv(h, kv_norm_g, w_kv, cmp_pe, cmp_w1, cmp_w2, positions):
    b, s, _ = h.shape
    hn = rmsnorm(h, kv_norm_g)
    kv = (hn @ w_kv).reshape(b, s, 6, NSA_KV_HEADS, HEAD_DIM)
    k_c, v_c, k_s, v_s, k_w, v_w = [kv[:, :, i] for i in range(6)]
    k_s = rope(k_s, positions)
    k_w = rope(k_w, positions)
    n_cmp = (s - CMP_LEN) // CMP_STRIDE + 1
    blk = jnp.arange(n_cmp)[:, None] * CMP_STRIDE + jnp.arange(CMP_LEN)[None, :]

    def compress(z, pe, w1, w2):
        zb = z[:, blk] + pe[None, None, :, None, :]
        zb = zb.transpose(0, 1, 3, 2, 4).reshape(b, n_cmp, NSA_KV_HEADS, CMP_LEN * HEAD_DIM)
        return jax.nn.silu(zb @ w1) @ w2

    k_cmp = compress(k_c, cmp_pe[0], cmp_w1[0], cmp_w2[0])
    v_cmp = compress(v_c, cmp_pe[1], cmp_w1[1], cmp_w2[1])
    k_cmp = rope(k_cmp, positions[:, blk[:, -1]])
    n_sel = s // SEL_LEN
    k_blk = k_s.reshape(b, n_sel, SEL_LEN, NSA_KV_HEADS, HEAD_DIM).transpose(0, 3, 1, 2, 4)
    v_blk = v_s.reshape(b, n_sel, SEL_LEN, NSA_KV_HEADS, HEAD_DIM).transpose(0, 3, 1, 2, 4)
    pad = ((0, 0), (WINDOW, 0), (0, 0), (0, 0))
    return (k_cmp, v_cmp, k_blk, v_blk, jnp.pad(k_w, pad), jnp.pad(v_w, pad))

def nsa_attention(q, gates, k_cmp, v_cmp, k_blk, v_blk, k_win, v_win):
    b, s, _, _ = q.shape
    n_cmp = k_cmp.shape[1]
    n_sel = k_blk.shape[2]
    n_top = min(SEL_TOPK, n_sel)
    G, R, L = NSA_KV_HEADS, NSA_GROUP, SEL_LEN
    cmp_start = jnp.arange(n_cmp) * CMP_STRIDE
    cmp_end = cmp_start + CMP_LEN - 1
    sel_start = jnp.arange(n_sel) * SEL_LEN
    ov = (jnp.minimum(cmp_end[:, None], sel_start[None, :] + L - 1)
          - jnp.maximum(cmp_start[:, None], sel_start[None, :]) + 1)
    overlap = jnp.maximum(ov, 0).astype(jnp.float32) / CMP_LEN
    bi = jnp.arange(b)[:, None, None, None]
    gi = jnp.arange(G)[None, :, None, None]
    jsel = jnp.arange(n_sel)

    def chunk(c):
        t0 = c * Q_CHUNK
        t = t0 + jnp.arange(Q_CHUNK)
        qc = lax.dynamic_slice_in_dim(q, t0, Q_CHUNK, axis=1).reshape(b, Q_CHUNK, G, R, HEAD_DIM)
        gc = lax.dynamic_slice_in_dim(gates, t0, Q_CHUNK, axis=1).reshape(b, Q_CHUNK, G, R, 3)
        sc = jnp.einsum('bqgrd,bngd->bgrqn', qc, k_cmp)
        p_cmp = masked_softmax(sc, cmp_end[None, :] <= t[:, None])
        o_cmp = jnp.einsum('bgrqn,bngd->bqgrd', p_cmp.astype(v_cmp.dtype), v_cmp)
        imp = jnp.einsum('bgrqn,nj->bgqj', p_cmp, overlap)
        cur = t // L
        forced = (jsel[None, :] == 0) | (jsel[None, :] == cur[:, None]) | (jsel[None, :] == cur[:, None] - 1)
        ok = sel_start[None, :] <= t[:, None]
        score = jnp.where(ok, jnp.where(forced, FORCE_SCORE, imp), NEG_INF)
        _, idx = lax.top_k(score, n_top)
        k_sel = k_blk[bi, gi, idx].reshape(b, G, Q_CHUNK, n_top * L, HEAD_DIM)
        v_sel = v_blk[bi, gi, idx].reshape(b, G, Q_CHUNK, n_top * L, HEAD_DIM)
        key_pos = (idx[..., None] * L + jnp.arange(L)).reshape(b, G, 1, Q_CHUNK, n_top * L)
        ss = jnp.einsum('bqgrd,bgqmd->bgrqm', qc, k_sel)
        p_sel = masked_softmax(ss, key_pos <= t[None, None, None, :, None])
        o_sel = jnp.einsum('bgrqm,bgqmd->bqgrd', p_sel.astype(v_sel.dtype), v_sel)
        kw = lax.dynamic_slice_in_dim(k_win, t0, WINDOW + Q_CHUNK, axis=1)
        vw = lax.dynamic_slice_in_dim(v_win, t0, WINDOW + Q_CHUNK, axis=1)
        spos = t0 - WINDOW + jnp.arange(WINDOW + Q_CHUNK)
        dist = t[:, None] - spos[None, :]
        win_ok = (dist >= 0) & (dist < WINDOW) & (spos[None, :] >= 0)
        sw = jnp.einsum('bqgrd,bsgd->bgrqs', qc, kw)
        p_w = masked_softmax(sw, win_ok)
        o_win = jnp.einsum('bgrqs,bsgd->bqgrd', p_w.astype(vw.dtype), vw)
        return gc[..., 0:1] * o_cmp + gc[..., 1:2] * o_sel + gc[..., 2:3] * o_win

    out = lax.map(chunk, jnp.arange(s // Q_CHUNK))
    return jnp.moveaxis(out, 0, 1).reshape(b, s, NSA_W)

def pool_layer(x, mem, norm_g, w_in, w_pool, pool_scale, mem_g, w_mem_kv, w_out):
    b, s, _ = x.shape
    h = rmsnorm(x, norm_g)
    proj = h @ w_in
    u, zu, qm, zm = jnp.split(proj, [POOL_W, 2 * POOL_W, 2 * POOL_W + MEM_W], axis=-1)
    y_pool = multiscale_pool(u, w_pool, pool_scale) * jax.nn.silu(zu)
    qm = qm.reshape(b, s, MEM_HEADS, HEAD_DIM) * (HEAD_DIM ** -0.5)
    y_mem = memory_attention(qm, mem, mem_g, w_mem_kv) * jax.nn.silu(zm)
    return x + jnp.concatenate([y_pool, y_mem], axis=-1) @ w_out

def nsa_layer(x, mem, positions, norm_g, w_in, mem_g, w_mem_kv, w_out, shared):
    b, s, _ = x.shape
    h = rmsnorm(x, norm_g)
    proj = h @ w_in
    o1 = NSA_W
    o2 = o1 + 3 * NSA_HEADS
    o3 = o2 + NSA_W
    o4 = o3 + MEM_W
    q, gl, zq, qm, zm = jnp.split(proj, [o1, o2, o3, o4], axis=-1)
    q = rope(q.reshape(b, s, NSA_HEADS, HEAD_DIM), positions) * (HEAD_DIM ** -0.5)
    gates = jax.nn.sigmoid(gl.reshape(b, s, NSA_HEADS, 3))
    y_nsa = nsa_attention(q, gates, *shared) * jax.nn.silu(zq)
    qm = qm.reshape(b, s, MEM_HEADS, HEAD_DIM) * (HEAD_DIM ** -0.5)
    y_mem = memory_attention(qm, mem, mem_g, w_mem_kv) * jax.nn.silu(zm)
    return x + jnp.concatenate([y_nsa, y_mem], axis=-1) @ w_out

def second_inputs(seed: int = 0) -> dict:
    key = jax.random.key(seed)
    ks = jax.random.split(key, 20)
    n_a = DEPTH_2 // 2
    n_b = DEPTH_2 - n_a
    f32 = jnp.float32

    def w(k, shape, fan_in):
        return jax.random.normal(k, shape, f32) * (fan_in ** -0.5)

    def gain(k, shape):
        return 1.0 + 0.05 * jax.random.normal(k, shape, f32)

    x = jax.random.normal(ks[0], (BATCH, SEQ, D_MODEL), f32)
    mem = jax.random.normal(ks[1], (BATCH, MEM_LEN, D_MODEL), f32)
    offs = jax.random.randint(ks[2], (BATCH, 1), 0, 1024, dtype=jnp.int32)
    positions = (offs + jnp.arange(SEQ, dtype=jnp.int32)[None, :]).astype(jnp.int32)
    b_in_w = 2 * NSA_W + 3 * NSA_HEADS + 2 * MEM_W
    return {
        "x": x,
        "mem": mem,
        "positions": positions,
        "norm_g": gain(ks[3], (DEPTH_2, D_MODEL)),
        "mem_norm_g": gain(ks[4], (DEPTH_2, D_MODEL)),
        "w_mem_kv": w(ks[5], (DEPTH_2, D_MODEL, 2 * MEM_W), D_MODEL),
        "w_out": w(ks[6], (DEPTH_2, MIX_W, D_MODEL), MIX_W),
        "a_w_in": w(ks[7], (n_a, D_MODEL, 2 * POOL_W + 2 * MEM_W), D_MODEL),
        "a_w_pool": w(ks[8], (n_a, POOL_GROUPS, POOL_GC, POOL_GC), POOL_GC),
        "a_pool_scale": gain(ks[9], (n_a, POOL_W)),
        "b_w_in": w(ks[10], (n_b, D_MODEL, b_in_w), D_MODEL),
        "kv_norm_g": gain(ks[11], (D_MODEL,)),
        "w_kv": w(ks[12], (D_MODEL, 6 * NSA_KV_W), D_MODEL),
        "cmp_pe": 0.1 * jax.random.normal(ks[13], (2, CMP_LEN, HEAD_DIM), f32),
        "cmp_w1": w(ks[14], (2, CMP_LEN * HEAD_DIM, CMP_HID), CMP_LEN * HEAD_DIM),
        "cmp_w2": w(ks[15], (2, CMP_HID, HEAD_DIM), CMP_HID),
        "final_g": gain(ks[16], (D_MODEL,)),
    }

def second_block(x, mem, positions, norm_g, mem_norm_g, w_mem_kv, w_out, a_w_in, a_w_pool,
              a_pool_scale, b_w_in, kv_norm_g, w_kv, cmp_pe, cmp_w1, cmp_w2, final_g):
    n_a = DEPTH_2 // 2
    h = x
    shared = None
    for layer in range(DEPTH_2):
        if layer < n_a:
            h = pool_layer(h, mem, norm_g[layer], a_w_in[layer], a_w_pool[layer],
                           a_pool_scale[layer], mem_norm_g[layer], w_mem_kv[layer], w_out[layer])
        else:
            if layer == n_a:
                shared = nsa_shared_kv(h, kv_norm_g, w_kv, cmp_pe, cmp_w1, cmp_w2, positions)
            h = nsa_layer(h, mem, positions, norm_g[layer], b_w_in[layer - n_a],
                          mem_norm_g[layer], w_mem_kv[layer], w_out[layer], shared)
    return rmsnorm(h, final_g)


def setup_inputs(seed=0):
    out = dict(first_inputs(seed))
    for name, value in second_inputs(seed + 1).items():
        if name != "x":
            out[name + "_2"] = value
    return out


def reference(
    x, mem, norm_mix, w_in, hgrn_lb_logits, hgrn_onorm, attn_qnorm, attn_knorm, w_out,
    norm_cross, mem_norm, wq_x, wk_x, wv_x, wo_x, xq_norm, xk_norm, norm_mlp, w_up, w_down,
    mem_2, positions_2, norm_g_2, mem_norm_g_2, w_mem_kv_2, w_out_2, a_w_in_2, a_w_pool_2,
    a_pool_scale_2, b_w_in_2, kv_norm_g_2, w_kv_2, cmp_pe_2, cmp_w1_2, cmp_w2_2, final_g_2,
):
    x = first_block(
        x, mem, norm_mix, w_in, hgrn_lb_logits, hgrn_onorm, attn_qnorm, attn_knorm, w_out,
        norm_cross, mem_norm, wq_x, wk_x, wv_x, wo_x, xq_norm, xk_norm, norm_mlp, w_up, w_down,
    )
    return second_block(
        x, mem_2, positions_2, norm_g_2, mem_norm_g_2, w_mem_kv_2, w_out_2, a_w_in_2,
        a_w_pool_2, a_pool_scale_2, b_w_in_2, kv_norm_g_2, w_kv_2, cmp_pe_2, cmp_w1_2, cmp_w2_2,
        final_g_2,
    )


_drawn_inputs = setup_inputs


def setup_inputs(seed=0):
    import zlib

    import numpy as np

    out = dict(_drawn_inputs(seed))
    spreads = {}
    factors = {'hgrn_lb_logits': 8.0,
     'hgrn_onorm': 5.572,
     'attn_qnorm': 8.0,
     'attn_knorm': 8.0,
     'norm_cross': 8.0,
     'mem_norm': 8.0,
     'xq_norm': 8.0,
     'xk_norm': 8.0,
     'norm_mlp': 3.155,
     'norm_g_2': 2.871,
     'mem_norm_g_2': 8.0,
     'a_pool_scale_2': 4.517,
     'kv_norm_g_2': 8.0,
     'cmp_pe_2': 6.907}
    for name, (base, spread) in spreads.items():
        noise = np.random.default_rng([zlib.crc32(name.encode()), seed]).standard_normal(out[name].shape)
        drawn = base * np.exp(spread * noise) if base else spread * noise
        out[name] = __import__('jax').numpy.asarray(drawn.astype(out[name].dtype))
    for name, factor in factors.items():
        out[name] = (out[name] * factor).astype(out[name].dtype)
    return out
```

```python
from contextlib import ExitStack

import concourse.bass as bass
from concourse import mybir

F32 = mybir.dt.float32
I32 = mybir.dt.int32
ALU = mybir.AluOpType
ACT = mybir.ActivationFunctionType
AX = mybir.AxisListType.X

P = 128
D = 2048
KT = D // P
T = 256
TH = T // P
HD = 128
HALF_FF = 4096
EPS = 1e-6
ATT_SCALE = HD ** -0.5
RING = 8
CHUNK = 2048
NEG = -1e30
TAKEN = -3e38
TOPK = 64
IDX_HEADS = 16
IDX_SCALE = IDX_HEADS ** -0.5 * 64 ** -0.5
CMP_LEN, CMP_STRIDE = 32, 16
N_CMP = (T - CMP_LEN) // CMP_STRIDE + 1
ROPE_THETA = 500000.0
ROT = HD // 4
POOL_WINDOWS = (2, 4, 8, 16)
CHUNK_T = 64
LEVELS = (1, 2, 4, 8, 16, 32, 64)
TWO_PI_PARTS = (6.28125, 0.0019354820251464844, -1.7484556025237907e-07)


def spread(ap, dim, count):
    shape = list(ap.shape)
    shape[dim] = count
    return ap.broadcast_to(shape)


class Gemm:

    def __init__(self, b0, blocks, g0, groups):
        self.b0, self.blocks, self.g0, self.groups = b0, blocks, g0, groups
        self.chunks = 4 * blocks // groups

    def made(self, n=0):
        return 4 * self.b0 + self.chunks * (n + 1)


def plan_stream():
    order = [("hgrn_qf", 4, 4), ("hgrn_v", 2, 2), ("gate_q_k", 6, 6), ("attn_v", 2, 2), ("idx_q", 2, 2),
             ("idx_tail", 1, 1), ("mix_out", 4, 4),
             ("cross_q", 1, 1), ("cross_k", 1, 1), ("cross_v", 1, 1), ("cross_out", 1, 4),
             ("up0", 8, 8), ("down0", 8, 4), ("up1", 8, 8), ("down1", 8, 4),
             ("pool_in", 8, 8), ("mem_k0", 1, 1), ("mem_v0", 1, 1), ("pool_mix", 1, 4), ("out0", 4, 4),
             ("cmp_kv", 2, 2), ("sel_k", 1, 1), ("sel_v", 1, 1), ("win_k", 1, 1), ("win_v", 1, 1),
             ("cmp_hid_k", 1, 1), ("cmp_hid_v", 1, 1),
             ("nsa_q", 3, 3), ("nsa_gate", 1, 1), ("nsa_zq", 3, 3), ("nsa_qm", 1, 1), ("nsa_zm", 1, 1),
             ("mem_k1", 1, 1), ("mem_v1", 1, 1), ("out1", 4, 4)]
    plan, b, g = {}, 0, 0
    for name, blocks, groups in order:
        plan[name] = Gemm(b, blocks, g, groups)
        b += blocks
        g += groups
    return plan


def build_program(nc, a):
    PLAN = plan_stream()
    ctx = ExitStack()
    with ctx:
        def sb(name, shape, dt=F32):
            return ctx.enter_context(nc.sbuf_tensor(name, shape, dt))

        def sem(name):
            return ctx.enter_context(nc.semaphore(name))

        hT = sb("hT", [P, KT, T])
        xnT = sb("xnT", [P, KT, T])
        yT = sb("yT", [P, KT, T])
        proj = sb("proj", [P, 64, T])
        ring = sb("ring", [P, RING, CHUNK])
        scratch = sb("scratch", [P, 6144])
        ident = sb("ident", [P, P])
        ones = sb("ones", [P, P])
        gains = sb("gains", [P, 2, P])
        pe_cols = sb("pe_cols", [P, 2, CMP_LEN])
        lower = sb("lower", [P, 16])
        causal = sb("causal", [P, TH, T])
        cmp_mask = sb("cmp_mask", [P, TH, 16])
        rstd = sb("rstd", [P, 2, 2 * T])
        ikT = sb("ikT", [P, T])
        idx_w = sb("idx_w", [P, TH, 16])
        small = sb("small", [P, 64])
        stats = sb("stats", [P, 2, 16])
        best = sb("best", [P, TH, 8])
        nsa_gates = sb("nsa_gates", [P, TH, 36])
        rope_c = sb("rope_c", [ROT, T])
        rope_s = sb("rope_s", [ROT, T])
        swap = sb("swap", [ROT, ROT])
        inv_row = sb("inv_row", [1, ROT])
        eps_col = sb("eps_col", [P, 4])
        tok_rstd = sb("tok_rstd", [P, 8])
        kcmpT = sb("kcmpT", [P, 64])
        bank = [ctx.enter_context(nc.psum_tensor(f"bank{i}", [P, 512], F32)) for i in range(8)]

        landed = [sem(f"landed{i}") for i in range(RING)]
        chunks_used = sem("chunks_used")
        evac_a = sem("evac_a")
        evac_b = sem("evac_b")
        gains_in = sem("gains_in")
        tokens_in = sem("tokens_in")
        misc_in = sem("misc_in")
        out_stored = sem("out_stored")
        consts_ready = sem("consts_ready")
        pool_order = sem("pool_order")
        dve_order = sem("dve_order")
        act_order = sem("act_order")
        gains_turned = sem("gains_turned")
        gains_ready = sem("gains_ready")
        rows_scaled = sem("rows_scaled")
        rows_squared = sem("rows_squared")
        rows_turned = sem("rows_turned")
        rows_kept = sem("rows_kept")
        norm_squares = sem("norm_squares")
        norm_sums = sem("norm_sums")
        norm_root = sem("norm_root")
        xn_ready = sem("xn_ready")
        y_ready = sem("y_ready")
        head_squares = sem("head_squares")
        head_sums = sem("head_sums")
        head_root = sem("head_root")
        head_normed = sem("head_normed")
        scores_ready = sem("scores_ready")
        max_ready = sem("max_ready")
        exp_ready = sem("exp_ready")
        probs_ready = sem("probs_ready")
        probs_turned = sem("probs_turned")
        turned_kept = sem("turned_kept")
        values_summed = sem("values_summed")
        out_kept = sem("out_kept")
        hg_act = sem("hg_act")
        hg_dve = sem("hg_dve")
        hg_exp = sem("hg_exp")
        hg_pe = sem("hg_pe")
        hg_operands = sem("hg_operands")
        hg_scores = sem("hg_scores")
        hg_placed = sem("hg_placed")
        hg_out = sem("hg_out")
        hg_square = sem("hg_square")
        hg_sum = sem("hg_sum")
        hg_root = sem("hg_root")
        hg_done = sem("hg_done")
        idx_logits = sem("idx_logits")
        idx_relu = sem("idx_relu")
        idx_added = sem("idx_added")
        mask_ready = sem("mask_ready")
        silu_ready = sem("silu_ready")
        hidden_ready = sem("hidden_ready")
        pooled_ready = sem("pooled_ready")
        rope_pos = sem("rope_pos")
        rope_angle = sem("rope_angle")
        rope_sin = sem("rope_sin")
        rope_tables = sem("rope_tables")
        rope_swapped = sem("rope_swapped")
        rope_done = sem("rope_done")
        zpe_ready = sem("zpe_ready")
        hid_act = sem("hid_act")
        cmp_second = sem("cmp_second")
        cmp_ready = sem("cmp_ready")
        gates_ready = sem("gates_ready")
        pool_out = sem("pool_out")
        final_ready = sem("final_ready")
        final_turned = sem("final_turned")
        final_kept = sem("final_kept")

        G_MIX, G_CROSS, G_MEM, G_MLP, G_2A, G_2B, G_M2A, G_M2B = (slice(16 * i, 16 * i + 16) for i in range(8))
        G_KV, G_FINAL = slice(0, 16), slice(16, 32)
        G_POOL, G_LB = slice(32, 44), slice(44, 60)
        G_ONORM, G_QN, G_KN, G_XQ, G_XK = 60, 61, 62, 63, 64

        hgrn_v = proj[:, 48:56, :].rearrange("p a t -> p (a t)").rearrange("p (h n) -> p h n", h=TH)
        attn_v = proj[:, 56:64, :].rearrange("p a t -> p (a t)").rearrange("p (h n) -> p h n", h=TH)

        def values_at(tile):
            return proj[:, tile:tile + 4, :].rearrange("p a t -> p (a t)").rearrange("p (h n) -> p h n", h=TH)

        cross_v, mem_v0, sel_v, win_v, mem_v1 = (values_at(t) for t in (24, 52, 12, 20, 60))
        tokens = scratch[:, 0:TH * D].rearrange("p (h n) -> p h n", h=TH)
        gain_rows = scratch[:, 5120:5504].rearrange("p (s c) -> p s c", s=3)
        masked_scores = scratch[:, 0:1024].rearrange("p (b h s) -> p b h s", b=2, h=TH)
        probs = scratch[:, 1024:2048].rearrange("p (b h s) -> p b h s", b=2, h=TH)
        probsT = scratch[:, 2048:3072].rearrange("p (b n) -> p b n", b=2)
        sel_bias = scratch[:, 3072:3584].rearrange("p (h s) -> p h s", h=TH)
        idx_score = scratch[:, 3584:4096].rearrange("p (h s) -> p h s", h=TH)
        idx_relus = scratch[:, 4096:4096 + 768].rearrange("p (b n) -> p b n", b=2)
        head_sq = scratch[:, 5120:6144].rearrange("p (b n) -> p b n", b=2)

        vcmp = scratch[0:16, 4096:4608].rearrange("p (m d) -> p m d", m=4)
        pos_i = scratch[0:1, 5376:5632].bitcast(I32)
        cmp_w2 = scratch[:, 5632:6144].rearrange("p (i m d) -> p i m d", i=2, m=2)

        xflat = xnT[:, :, :].rearrange("p a t -> p (a t)")
        hg_logf = xflat[:, 0:1024]
        hg_cum = xflat[:, 1024:2048]
        hg_decay = xflat[:, 2048:3072]
        hg_keys = xflat[:, 3072:4096]
        hg_reset = scratch[:, 0:1024]
        hg_queries = scratch[:, 1024:1536]
        hg_diag = scratch[:, 1536:2560].rearrange("p (m t) -> p m t", t=P)
        hg_cross = scratch[:, 2560:3072].rearrange("p (m t) -> p m t", t=P)
        hg_osq = scratch[:, 3072:3584]
        hg_tmp = scratch[:, 3584:4608]
        level_mask = scratch[:, 4608:4608 + len(LEVELS) * CHUNK_T].rearrange("p (n t) -> p n t", t=CHUNK_T)

        hidT = scratch[:, 4608:4608 + 16 * N_CMP].rearrange("p (c m n) -> p c m n", c=2, m=2)

        def zpe(c):
            flat = proj[:, 24 + 8 * c:32 + 8 * c, :].rearrange("p a t -> p (a t)")
            return flat[:, 0:CMP_LEN * 4 * N_CMP].rearrange("p (l n) -> p l n", l=CMP_LEN)

        ROPE_TURNS = ([(proj[0:ROT, t:t + 2, :], 2, None) for t in (8, 10, 16, 18)]
                      + [(kcmpT[0:ROT, 0:4 * N_CMP].rearrange("p (m t) -> p m t", m=4), 4, CMP_LEN - 1)]
                      + [(proj[0:ROT, t:t + 2, :], 2, None) for t in range(24, 36, 2)])

        block = ctx.enter_context(nc.Block())

        norm_pairs = ([(24 + 2 * n, G_QN) for n in range(4)] + [(32 + 2 * n, G_KN) for n in range(4)]
                      + [(16 + 2 * n, G_XQ) for n in range(2)] + [(20 + 2 * n, G_XK) for n in range(2)])
        MIX_PAIRS, CROSS_PAIRS = range(0, 8), range(8, 12)

        class Item:
            def __init__(self, q, k, v, widths, out, mask=None, gate=None, first=True, last=True, times=None):
                self.q, self.k, self.v, self.widths, self.out = q, k, v, widths, out
                self.mask, self.gate, self.first, self.last, self.times = mask, gate, first, last, times

        CAUSAL, FULL, CMP = (P, T), (T, T), (N_CMP, N_CMP)
        items = []
        for h in range(8):
            items.append(Item(proj[:, 24 + h, :], proj[:, 32 + h, :], attn_v[:, :, h * HD:h * HD + HD],
                              CAUSAL, yT[:, 8 + h, :], mask=sel_bias))
        DSA = range(0, 8)
        for h in range(4):
            items.append(Item(proj[:, 16 + h, :], proj[:, 20 + h, :], cross_v[:, :, h * HD:h * HD + HD],
                              FULL, proj[:, 28 + h, :]))
        CROSS = range(8, 12)
        for h in range(4):
            items.append(Item(proj[:, 24 + h, :], proj[:, 48 + h, :], mem_v0[:, :, h * HD:h * HD + HD],
                              FULL, yT[:, 12 + h, :], times=proj[:, 28 + h, :]))
        MEM0 = range(12, 16)
        for h in range(12):
            kv = h // 3
            for branch in range(3):
                q = proj[:, 24 + h, :]
                gate = nsa_gates[:, :, 3 * h + branch]
                if branch == 0:
                    it = Item(q, kcmpT[:, kv * N_CMP:kv * N_CMP + N_CMP], vcmp[:, kv, :], CMP, None,
                              mask=cmp_mask, gate=gate, last=False)
                elif branch == 1:
                    it = Item(q, proj[:, 8 + kv, :], sel_v[:, :, kv * HD:kv * HD + HD], CAUSAL, None,
                              mask=causal, gate=gate, first=False, last=False)
                else:
                    it = Item(q, proj[:, 16 + kv, :], win_v[:, :, kv * HD:kv * HD + HD], CAUSAL, yT[:, h, :],
                              mask=causal, gate=gate, first=False, times=proj[:, 36 + h, :])
                items.append(it)
        NSA = range(16, 52)
        for h in range(4):
            items.append(Item(proj[:, 48 + h, :], proj[:, 56 + h, :], mem_v1[:, :, h * HD:h * HD + HD],
                              FULL, yT[:, 12 + h, :], times=proj[:, 52 + h, :]))
        MEM1 = range(52, 56)
        outs_before = [sum(it.last for it in items[:n]) for n in range(len(items) + 1)]

        Y_HGRN, Y_DSA, Y_CROSS = 8, 16, 20
        Y_POOLED = Y_CROSS + 12 + 4
        Y_NSA = Y_POOLED + 16
        def hg_tiles(hg):
            return (proj[:, 4 * hg:4 * hg + 4, :].rearrange("p a t -> p (a t)"),
                    proj[:, 8 + 4 * hg:12 + 4 * hg, :].rearrange("p a t -> p (a t)"))

        def pair_tile(n, step=2):
            return proj[:, n:n + step, :].rearrange("p a t -> p (a t)")

        HG_OPS, HG_SCORES = len(LEVELS) + 1, len(LEVELS) + 2

        def xn_made(norm):
            return KT * (norm + 1)

        @block.sync
        def _(sp):
            x_rows = a["x"].rearrange("a (h p) n -> p (a h) n", p=P)
            mem_rows = a["mem"].rearrange("a (h p) n -> p (a h) n", p=P)
            mem2_rows = a["mem_2"].rearrange("a (h p) n -> p (a h) n", p=P)
            sp.dma_start(tokens, x_rows).then_inc(tokens_in, 16)

            row = 0
            def gain(name, rows, view, slot):
                nonlocal row
                sp.dma_start(gain_rows[row:row + rows, slot, :], view).then_inc(gains_in, 16)
                row += rows

            for name, n in (("norm_mix", 16), ("norm_cross", 16), ("mem_norm", 16), ("norm_mlp", 16),
                            ("norm_g_2", 32), ("mem_norm_g_2", 32)):
                gain(name, n, a[name].rearrange("l (r c) -> (l r) c", c=P), 0)
            row = 0
            gain("kv_norm_g_2", 16, a["kv_norm_g_2"].rearrange("(r c) -> r c", c=P), 1)
            gain("final_g_2", 16, a["final_g_2"].rearrange("(r c) -> r c", c=P), 1)
            gain("a_pool_scale_2", 12, a["a_pool_scale_2"].rearrange("l (r c) -> (l r) c", c=P), 1)
            gain("hgrn_lb_logits", 16, a["hgrn_lb_logits"].rearrange("l (r c) -> (l r) c", c=P), 1)
            for name in ("hgrn_onorm", "attn_qnorm", "attn_knorm", "xq_norm", "xk_norm"):
                gain(name, 1, a[name], 1)
            row = 0
            gain("cmp_pe_2", 64, a["cmp_pe_2"].rearrange("i l d -> (i l) d"), 2)
            def free_slot(b, j, more=0):
                need = 4 * b + j - RING + 1
                if need > 0:
                    sp.wait_ge(chunks_used, need + more)

            def stream(name, source, per_body=2):
                g = PLAN[name]
                peel = g.blocks if g.blocks < 2 * per_body else (2 if g.b0 == 0 else 0)
                for n in range(peel):
                    for j in range(4):
                        free_slot(g.b0 + n, j)
                        slot = (4 * (g.b0 + n) + j) % RING
                        dst, src = source(n, j, slot)
                        sp.dma_start(dst, src).then_inc(landed[slot], 16)
                if peel < g.blocks:
                    with sp.Fori(0, (g.blocks - peel) // per_body) as i:
                        for q in range(per_body):
                            b = g.b0 + peel + q
                            for j in range(4):
                                slot = (4 * b + j) % RING
                                free_slot(b, j, i * (4 * per_body))
                                dst, src = source(i * per_body + (peel + q), j, slot)
                                sp.dma_start(dst, src).then_inc(landed[slot], 16)

            def slab(slot, width=512, rows=4):
                return ring[:, slot, 0:rows * width].rearrange("p (k n) -> p k n", k=rows)

            def columns(w, col0):
                w3 = w.rearrange("(k p) n -> p k n", p=P)

                def source(n, j, slot):
                    return slab(slot), w3[:, 4 * j:4 * j + 4, bass.ds(n * 512 + col0, 512)]
                return source

            w_in = a["w_in"].rearrange("l k n -> (l k) n")
            stream("hgrn_qf", columns(w_in, 0))
            stream("hgrn_v", columns(w_in, 2048))
            stream("gate_q_k", columns(w_in, 3072))
            stream("attn_v", columns(w_in, 6144))
            stream("idx_q", columns(w_in, 7168))

            w_in3 = w_in.rearrange("(k p) n -> p k n", p=P)
            stream("idx_tail", lambda n, j, slot: (slab(slot, 80), w_in3[:, 4 * j:4 * j + 4, 8192:8272]))

            stream("mix_out", columns(a["w_out"].rearrange("l k n -> (l k) n"), 0))
            sp.wait_ge(out_kept, outs_before[8])
            sp.dma_start(tokens, mem_rows).then_inc(tokens_in, 16)
            stream("cross_q", columns(a["wq_x"].rearrange("l k n -> (l k) n"), 0))
            stream("cross_k", columns(a["wk_x"].rearrange("l k n -> (l k) n"), 0))
            stream("cross_v", columns(a["wv_x"].rearrange("l k n -> (l k) n"), 0))
            wo3 = a["wo_x"].rearrange("l (k p) n -> p (l k) n", p=P)
            stream("cross_out", lambda n, j, slot: (slab(slot), wo3[:, :, 512 * j:512 * j + 512]))
            w_up = a["w_up"].rearrange("l k n -> (l k) n")
            w_down3 = a["w_down"].rearrange("l (k p) n -> p (l k) n", p=P)
            for half in range(2):
                stream(f"up{half}", columns(w_up, half * HALF_FF))
                g = PLAN[f"down{half}"]
                with sp.Fori(0, 2) as i:
                    for q in range(4):
                        for j in range(4):
                            b = g.b0 + q
                            slot = (4 * b + j) % RING
                            free_slot(b, j, i * 16)
                            k = 32 * half + 16 * (q % 2) + 4 * j
                            sp.dma_start(slab(slot), w_down3[:, k:k + 4, bass.ds(i * 1024 + 512 * (q // 2), 512)])\
                              .then_inc(landed[slot], 16)
            stream("pool_in", columns(a["a_w_in_2"].rearrange("l k n -> (l k) n"), 0))
            sp.wait_ge(norm_sums, 4)
            sp.dma_start(tokens, mem2_rows).then_inc(tokens_in, 16)
            w_mem = a["w_mem_kv_2"].rearrange("l k n -> (l k) n")
            stream("mem_k0", columns(w_mem[0:D, :], 0))
            stream("mem_v0", columns(w_mem[0:D, :], 512))
            w_pool = a["a_w_pool_2"].rearrange("l g (k p) n -> p (l g) k n", p=P)
            stream("pool_mix", lambda n, j, slot: (slab(slot, 384, 3), w_pool[:, j, :, :]))
            w_out2 = a["w_out_2"].rearrange("l k n -> (l k) n")
            stream("out0", columns(w_out2[0:D, :], 0))
            sp.wait_ge(norm_sums, 5)
            sp.dma_start(pos_i[:, :], a["positions_2"]).then_inc(misc_in, 16)
            sp.dma_start(cmp_w2[:, :, :, :], a["cmp_w2_2"].rearrange("i (k p) d -> p i k d", p=P)).then_inc(misc_in, 16)
            w_kv = a["w_kv_2"]
            stream("cmp_kv", columns(w_kv, 0))
            stream("sel_k", columns(w_kv, 1024))
            stream("sel_v", columns(w_kv, 1536))
            stream("win_k", columns(w_kv, 2048))
            stream("win_v", columns(w_kv, 2560))
            w1 = a["cmp_w1_2"].rearrange("i (l p) n -> p i l n", p=P)
            stream("cmp_hid_k", lambda n, j, slot: (slab(slot, 256, 8), w1[:, 0, 8 * j:8 * j + 8, :]))
            stream("cmp_hid_v", lambda n, j, slot: (slab(slot, 256, 8), w1[:, 1, 8 * j:8 * j + 8, :]))
            w_b = a["b_w_in_2"].rearrange("l k n -> (l k) n")
            w_b3 = w_b.rearrange("(k p) n -> p k n", p=P)
            stream("nsa_q", columns(w_b, 0))
            stream("nsa_gate", lambda n, j, slot: (slab(slot, 36), w_b3[:, 4 * j:4 * j + 4, 1536:1572]))
            stream("nsa_zq", columns(w_b, 1572))
            stream("nsa_qm", columns(w_b, 3108))
            stream("nsa_zm", columns(w_b, 3620))
            sp.wait_ge(norm_sums, 6)
            sp.dma_start(tokens, mem2_rows).then_inc(tokens_in, 16)
            stream("mem_k1", columns(w_mem[D:2 * D, :], 0))
            stream("mem_v1", columns(w_mem[D:2 * D, :], 512))
            stream("out1", columns(w_out2[D:2 * D, :], 0))
            sp.wait_ge(final_kept, 8)
            sp.dma_start(a["out"].rearrange("a (h p) n -> p (a h) n", p=P), tokens).then_inc(out_stored, 16)
            sp.wait_ge(out_stored, 16)

        @block.gpsimd
        def _(pool):
            count = [0]

            def then(ins):
                count[0] += 1
                ins.then_inc(pool_order, 1)
                pool.wait_ge(pool_order, count[0])

            def select(out, pattern, base, per_row, op=ALU.is_ge, fill=0.0):
                then(pool.affine_select(out=out, in_=out, compare_op=op, fill=fill, base=base,
                                        pattern=pattern, channel_multiplier=per_row))

            then(pool.memset(ident[:, :], 0.0))
            select(ident[:, :], [[-1, P]], 0, 1, ALU.not_equal, 1.0)
            pool.memset(ones[:, :], 1.0)
            pool.memset(eps_col[:, 0:1], EPS)
            pool.memset(eps_col[:, 1:2], 1.5707963267948966)
            pool.memset(eps_col[:, 2:3], 0.0).then_inc(consts_ready, 1)
            then(pool.memset(causal[:, :, :], 0.0))
            select(causal[:, :, :], [[P, TH], [-1, T]], 0, 1, fill=NEG)
            then(pool.memset(cmp_mask[:, :, :], 0.0))
            select(cmp_mask[:, :, :], [[P, TH], [-CMP_STRIDE, 16]], 1 - CMP_LEN, 1, fill=NEG)
            then(pool.memset(swap[:, :], 0.0))
            select(swap[:, :], [[-1, ROT]], -ROT // 2, 1, ALU.not_equal, -1.0)
            select(swap[:, :], [[-1, ROT]], ROT // 2, 1, ALU.not_equal, 1.0)
            for j in range(ROT):
                last = pool.memset(inv_row[:, j:j + 1], float(ROPE_THETA ** (-(j % (ROT // 2)) * 2.0 / ROT)))
            last.then_inc(consts_ready, 1)
            pool.wait_ge(norm_sums, 1)
            then(pool.memset(level_mask[:, :, :], 1.0))
            for n, w in enumerate(LEVELS):
                v = level_mask[:, n, :].rearrange("p (b w) -> p b w", w=w)
                select(v, [[-2 * w, CHUNK_T // w], [0, w]], 0, 1)
                select(v, [[2 * w, CHUNK_T // w], [0, w]], w - 1, -1)
            then(pool.memset(hg_reset, 1.0))
            v = hg_reset.rearrange("p (c t) -> p c t", t=CHUNK_T)
            pool.memset(v[:, :, 0], 0.0).then_inc(consts_ready, 1)

        @block.tensor
        def _(pe):
            def arrived(b, j, more=0):
                pe.wait_ge(landed[(4 * b + j) % RING], 16 * (b // 2 + 1) + more)

            def group_free(g, more=0):
                if g >= 2:
                    pe.wait_ge(evac_a, g - 1 + more)
                    pe.wait_ge(evac_b, g - 1 + more)

            def slab(slot, width=512, rows=4):
                return ring[:, slot, 0:rows * width].rearrange("p (k n) -> p k n", k=rows)

            def features(x, b, g, k0=0, of=KT, it=0, per_body=2, ready=0):
                pair = bank[2 * (g % 2)], bank[2 * (g % 2) + 1]
                for j in range(4):
                    arrived(b, j, it * (8 * per_body))
                    if ready:
                        pe.wait_ge(xn_ready, ready - KT + 4 * j + 4)
                    w = slab((4 * b + j) % RING)
                    for k in range(4):
                        kt = k0 + 4 * j + k
                        for f in range(4):
                            mm = pe.matmul(pair[f // 2][:, (f % 2) * T:(f % 2) * T + T],
                                           w[:, k, f * P:f * P + P], x(kt),
                                           start=(kt == 0 and f % 2 == 0), stop=(kt == of - 1),
                                           skip_group_check=True)
                    mm.then_inc(chunks_used, 1)
                return mm

            def token_rows(x, b, g, it=0, ready=0):
                pair = bank[2 * (g % 2)], bank[2 * (g % 2) + 1]
                for j in range(4):
                    arrived(b, j, it * 16)
                    if ready:
                        pe.wait_ge(xn_ready, ready - KT + 4 * j + 4)
                    w = slab((4 * b + j) % RING)
                    for k in range(4):
                        kt = 4 * j + k
                        for h in range(TH):
                            mm = pe.matmul(pair[h][:, :], x(kt)[:, h * P:h * P + P], w[:, k, :],
                                           start=(kt == 0), stop=(kt == KT - 1), skip_group_check=True)
                    mm.then_inc(chunks_used, 1)
                return mm

            def product(name, kind, x, ready=0):
                g = PLAN[name]
                peel = g.blocks if g.blocks < 4 else (2 if g.b0 == 0 else 0)
                for n in range(peel):
                    group_free(g.g0 + n)
                    kind(x, g.b0 + n, g.g0 + n, ready=ready if n == 0 else 0)
                if peel < g.blocks:
                    if peel == 0 and ready:
                        pe.wait_ge(xn_ready, ready)
                    with pe.Fori(0, (g.blocks - peel) // 2) as i:
                        for q in range(2):
                            group_free(g.g0 + peel + q, i * 2)
                            kind(x, g.b0 + peel + q, g.g0 + peel + q, it=i)

            xn = lambda kt: xnT[:, kt, :]
            yt = lambda kt: yT[:, kt, :]

            pe.wait_ge(consts_ready, 1)
            pe.wait_ge(gains_in, 16 * 16)
            pe.transpose(bank[4][:, 0:P], gain_rows[:, 0, :], ident[:, :])
            pe.transpose(bank[4][:, P:P + 65], gain_rows[0:65, 1, :], ident[0:65, 0:65])
            pe.transpose(bank[4][:, 2 * P:2 * P + 64], gain_rows[0:64, 2, :], ident[0:64, 0:64])\
              .then_inc(gains_turned, 1)

            turned = [0]

            def turn_rows():
                for n in range(KT // 2):
                    m = turned[0]
                    if m >= 3:
                        pe.wait_ge(rows_kept, m - 2)
                    for c in range(2):
                        for h in range(TH):
                            mm = pe.transpose(bank[5 + m % 3][:, c * T + h * P:c * T + h * P + P],
                                              tokens[:, h, (2 * n + c) * P:(2 * n + c) * P + P], ident[:, :])
                    mm.then_inc(rows_turned, 1)
                    turned[0] += 1

            pe.wait_ge(tokens_in, 16)
            turn_rows()

            normed = [0]

            def norm_sum():
                n = normed[0]
                for c in range(4):
                    pe.wait_ge(norm_squares, 4 * n + c + 1)
                    for k in range(4):
                        kt = 4 * c + k
                        mm = pe.matmul(bank[4][:, 0:T], ones[:, :], scratch[:, kt * T:kt * T + T],
                                       start=(kt == 0), stop=(kt == KT - 1))
                mm.then_inc(norm_sums, 1)
                normed[0] += 1

            def head_sum(pairs):
                for n in pairs:
                    pe.wait_ge(head_squares, n + 1)
                    if n >= 2:
                        pe.wait_ge(head_root, n - 1)
                    pe.matmul(bank[4 + n % 2][:, :], ones[:, :], head_sq[:, n % 2, :], start=True, stop=True)\
                      .then_inc(head_sums, 1)

            def scores(n):
                it = items[n]
                if n >= 2:
                    pe.wait_ge(exp_ready, n - 1)
                for h in range(TH):
                    w = it.widths[h]
                    mm = pe.matmul(bank[4 + n % 2][:, h * T:h * T + w], it.q[:, h * P:h * P + P],
                                   it.k[:, 0:w], start=True, stop=True)
                mm.then_inc(scores_ready, 1)

            def turned_col(s, h):
                return P + h * P if s == 0 else (0 if h == 0 else 3 * P)

            def turn_probs(n):
                it = items[n]
                pe.wait_ge(probs_ready, n + 1)
                if n >= 1:
                    pe.wait_ge(turned_kept, n)
                for h in range(TH):
                    for s in range(TH):
                        w = min(P, it.widths[h] - s * P)
                        if w > 0:
                            c = turned_col(s, h)
                            mm = pe.transpose(bank[6][0:w, c:c + P], probs[:, n % 2, h, s * P:s * P + w],
                                              ident[:, :])
                mm.then_inc(probs_turned, 1)

            def weigh_values(n):
                it = items[n]
                g = outs_before[n]
                pe.wait_ge(turned_kept, n + 1)
                if it.first and g:
                    pe.wait_ge(out_kept, g)
                o = bank[7][:, 0:T]
                pT = probsT[:, n % 2, :]
                if it.widths == CMP:
                    mm = pe.matmul(o, it.v[0:N_CMP, :], pT[0:N_CMP, P:3 * P], start=it.first, stop=it.last,
                                   skip_group_check=True)
                else:
                    pe.matmul(o, it.v[:, 0, :], pT[:, P:3 * P], start=it.first, stop=False, skip_group_check=True)
                    if it.widths == FULL:
                        pe.matmul(o[:, 0:P], it.v[:, 1, :], pT[:, 0:P], start=False, stop=False,
                                  skip_group_check=True)
                    mm = pe.matmul(o[:, P:T], it.v[:, 1, :], pT[:, 3 * P:4 * P], start=False, stop=it.last,
                                   skip_group_check=True)
                mm.then_inc(values_summed, 1)

            def attend(which):
                first, end = which[0], which[-1] + 1
                for n in range(first, end + 2):
                    if n < end:
                        scores(n)
                    if first <= n - 1 < end:
                        turn_probs(n - 1)
                    if first <= n - 2 < end:
                        weigh_values(n - 2)

            norm_sum()
            product("hgrn_qf", features, xn, ready=xn_made(0))
            product("hgrn_v", token_rows, xn)
            product("gate_q_k", features, xn)
            product("attn_v", token_rows, xn)
            product("idx_q", features, xn)
            g = PLAN["idx_tail"]
            group_free(g.g0)
            pair = bank[2 * (g.g0 % 2)], bank[2 * (g.g0 % 2) + 1]
            for j in range(4):
                arrived(g.b0, j)
                w = slab((4 * g.b0 + j) % RING, 80)
                for k in range(4):
                    kt = 4 * j + k
                    pe.matmul(pair[0][0:64, 0:T], w[:, k, 0:64], xnT[:, kt, :], start=(kt == 0), stop=(kt == KT - 1))
                    for h in range(TH):
                        mm = pe.matmul(pair[1][:, h * 16:h * 16 + 16], xnT[:, kt, h * P:h * P + P],
                                       w[:, k, 64:80], start=(kt == 0 and h == 0), stop=(kt == KT - 1),
                                       skip_group_check=True)
                mm.then_inc(chunks_used, 1)

            for hg in range(2):
                if hg:
                    pe.wait_ge(hg_root, 2)
                    pe.wait_ge(hg_done, 2)
                placed = HG_SCORES * hg
                for n in range(len(LEVELS)):
                    pe.wait_ge(hg_operands, HG_OPS * hg + n + 1)
                    if placed + n >= 2:
                        pe.wait_ge(hg_placed, placed + n - 1)
                    for t in range(8):
                        mm = pe.matmul(bank[4 + n % 2][:, t * CHUNK_T:t * CHUNK_T + CHUNK_T],
                                       hg_keys[:, t * P:t * P + P],
                                       hg_queries[:, t * CHUNK_T:t * CHUNK_T + CHUNK_T], start=True, stop=True)
                    mm.then_inc(hg_scores, 1)
                pe.wait_ge(hg_placed, placed + len(LEVELS))
                qs, ks = hg_tiles(hg)
                for t in range(8):
                    mm = pe.matmul(bank[4 + t // 4][:, (t % 4) * P:(t % 4) * P + P], ks[:, t * P:t * P + P],
                                   qs[:, t * P:t * P + P], start=True, stop=True)
                mm.then_inc(hg_scores, 1)
                pe.wait_ge(hg_operands, HG_OPS * (hg + 1))
                pe.wait_ge(hg_placed, placed + len(LEVELS) + 1)
                for h in range(4):
                    mm = pe.matmul(bank[4][:, h * P:h * P + P], hg_keys[:, h * T:h * T + P],
                                   hg_queries[:, h * P:h * P + P], start=True, stop=True)
                mm.then_inc(hg_scores, 1)
                pe.wait_ge(hg_placed, placed + HG_SCORES)
                for h in range(4):
                    o = bank[6 + h // 2][:, (h % 2) * T:(h % 2) * T + T]
                    v = hgrn_v[:, :, (4 * hg + h) * HD:(4 * hg + h + 1) * HD]
                    pe.matmul(o[:, 0:P], v[:, 0, :], hg_diag[:, 2 * h, :], start=(h % 2 == 0), stop=False,
                              skip_group_check=True)
                    pe.matmul(o[:, P:T], v[:, 1, :], hg_diag[:, 2 * h + 1, :], start=False, stop=False,
                              skip_group_check=True)
                    mm = pe.matmul(o[:, P:T], v[:, 0, :], hg_cross[:, h, :], start=False, stop=True,
                                   skip_group_check=True)
                    if h % 2:
                        mm.then_inc(hg_out, 1)
                for c in range(2):
                    pe.wait_ge(hg_square, 2 * hg + c + 1)
                    if c or hg:
                        pe.wait_ge(hg_root, 2 * hg + c)
                    pe.matmul(bank[5][:, :], ones[:, :], hg_osq, start=True, stop=True).then_inc(hg_sum, 1)

            pe.wait_ge(evac_a, PLAN["idx_tail"].g0 + 1)
            pe.wait_ge(evac_b, PLAN["idx_tail"].g0 + 1)
            pe.wait_ge(hg_done, 4)
            for n in range(IDX_HEADS):
                if n >= 2:
                    pe.wait_ge(idx_relu, n - 1)
                r = slice(64 * (n % 2), 64 * (n % 2) + 64)
                q = proj[:, 40 + n // 2, :]
                pe.matmul(bank[4 + n % 2][:, 0:P], q[r, 0:P], ikT[r, 0:P], start=True, stop=True)
                pe.matmul(bank[4 + n % 2][:, P:P + T], q[r, P:T], ikT[r, :], start=True, stop=True)\
                  .then_inc(idx_logits, 1)
            pe.wait_ge(idx_relu, IDX_HEADS)
            head_sum(MIX_PAIRS)
            pe.wait_ge(head_normed, 8)
            attend(DSA)
            pe.wait_ge(y_ready, Y_DSA)
            product("mix_out", features, yt)

            pe.wait_ge(rows_scaled, 1)
            turn_rows()
            norm_sum()
            product("cross_q", features, xn, ready=xn_made(1))
            pe.wait_ge(rows_kept, 16)
            product("cross_k", features, yt)
            product("cross_v", token_rows, yt)
            head_sum(CROSS_PAIRS)
            pe.wait_ge(head_normed, 12)
            pe.wait_ge(evac_a, PLAN["cross_v"].g0 + 1)
            pe.wait_ge(evac_b, PLAN["cross_v"].g0 + 1)
            attend(CROSS)
            g = PLAN["cross_out"]
            pe.wait_ge(y_ready, Y_CROSS)
            for j in range(4):
                group_free(g.g0 + j)
                arrived(g.b0, j)
                pair = bank[2 * ((g.g0 + j) % 2)], bank[2 * ((g.g0 + j) % 2) + 1]
                w = slab((4 * g.b0 + j) % RING)
                for k in range(4):
                    for f in range(4):
                        mm = pe.matmul(pair[f // 2][:, (f % 2) * T:(f % 2) * T + T], w[:, k, f * P:f * P + P],
                                       proj[:, 28 + k, :], start=(k == 0 and f % 2 == 0), stop=(k == 3),
                                       skip_group_check=True)
                mm.then_inc(chunks_used, 1)

            norm_sum()
            for half in range(2):
                product(f"up{half}", features, xn, ready=xn_made(2) if half == 0 else 0)
                g = PLAN[f"down{half}"]
                pe.wait_ge(hidden_ready, 8 * (half + 1))
                with pe.Fori(0, 2) as i:
                    for q in range(2):
                        group_free(g.g0 + q, i * 2)
                        for r in range(2):
                            mm = features(lambda kt: proj[:, kt, :], g.b0 + 2 * q + r, g.g0 + q,
                                          k0=16 * r, of=32, it=i, per_body=4)
            
            norm_sum()
            product("pool_in", features, xn, ready=xn_made(3))
            pe.wait_ge(rows_scaled, 2)
            turn_rows()
            pe.wait_ge(rows_kept, 24)
            product("mem_k0", features, yt)
            product("mem_v0", token_rows, yt)
            g = PLAN["pool_mix"]
            for j in range(4):
                group_free(g.g0 + j)
                arrived(g.b0, j)
                pe.wait_ge(pooled_ready, j + 1)
                pair = bank[2 * ((g.g0 + j) % 2)], bank[2 * ((g.g0 + j) % 2) + 1]
                w = slab((4 * g.b0 + j) % RING, 384, 3)
                for k in range(3):
                    for f in range(3):
                        mm = pe.matmul(pair[f // 2][:, (f % 2) * T:(f % 2) * T + T], w[:, k, f * P:f * P + P],
                                       proj[:, 32 + 3 * j + k, :], start=(k == 0 and f % 2 == 0), stop=(k == 2),
                                       skip_group_check=True)
                mm.then_inc(chunks_used, 1)
            pe.wait_ge(evac_a, PLAN["pool_mix"].g0)
            pe.wait_ge(evac_b, PLAN["pool_mix"].g0)
            attend(MEM0)
            pe.wait_ge(y_ready, Y_POOLED)
            product("out0", features, yt)

            norm_sum()
            product("cmp_kv", features, xn, ready=xn_made(4))
            product("sel_k", features, xn)
            product("sel_v", token_rows, xn)
            product("win_k", features, xn)
            product("win_v", token_rows, xn)
            pe.wait_ge(rope_pos, 1)
            pe.matmul(bank[5][0:ROT, 0:T], ones[0:1, 0:ROT], rstd[0:1, 0, 0:T], start=True, stop=True)
            pe.matmul(bank[6][0:ROT, 0:2], inv_row[0:1, :], ones[0:1, 0:2], start=True, stop=True)\
              .then_inc(rope_pos, 1)

            swaps = [0]

            def swap_halves(x, width):
                n = swaps[0]
                if n >= 2:
                    pe.wait_ge(rope_done, n - 1)
                pe.matmul(bank[5 + n % 2][0:ROT, 0:width], swap[:, :], x, start=True, stop=True)\
                  .then_inc(rope_swapped, 1)
                swaps[0] += 1

            pe.wait_ge(rope_tables, 1)
            pe.wait_ge(evac_a, PLAN["win_v"].g0)
            pe.wait_ge(evac_b, PLAN["win_v"].g0)
            for t in (8, 10, 16, 18):
                swap_halves(proj[0:ROT, t:t + 2, :], 2 * T)
            for c, name in enumerate(("cmp_hid_k", "cmp_hid_v")):
                g = PLAN[name]
                group_free(g.g0)
                pe.wait_ge(zpe_ready, c + 1)
                hid = bank[2 * (g.g0 % 2)]
                for j in range(4):
                    arrived(g.b0, j)
                    w = slab((4 * g.b0 + j) % RING, 256, 8)
                    for k in range(8):
                        for m in range(2):
                            mm = pe.matmul(hid[:, m * 64:m * 64 + 4 * N_CMP], w[:, k, m * P:m * P + P],
                                           zpe(c)[:, 8 * j + k, :], start=(j == 0 and k == 0 and m == 0),
                                           stop=(j == 3 and k == 7), skip_group_check=True)
                    mm.then_inc(chunks_used, 1)
            pe.wait_ge(evac_a, PLAN["nsa_q"].g0)
            pe.wait_ge(rope_done, 4)
            for m in range(2):
                pe.matmul(bank[7][:, 0:4 * N_CMP], cmp_w2[:, 0, m, :], hidT[:, 0, m, :], start=(m == 0), stop=(m == 1))
            for kv in range(4):
                for m in range(2):
                    mm = pe.matmul(bank[5][0:N_CMP, kv * P:kv * P + P],
                                   hidT[:, 1, m, kv * N_CMP:kv * N_CMP + N_CMP], cmp_w2[:, 1, m, :],
                                   start=(kv == 0 and m == 0), stop=(m == 1), skip_group_check=True)
            mm.then_inc(cmp_second, 1)
            pe.wait_ge(cmp_ready, 1)
            swap_halves(kcmpT[0:ROT, 0:4 * N_CMP], 4 * N_CMP)
            norm_sum()
            product("nsa_q", features, xn, ready=xn_made(5))
            g = PLAN["nsa_gate"]
            group_free(g.g0)
            pair = bank[2 * (g.g0 % 2)], bank[2 * (g.g0 % 2) + 1]
            for j in range(4):
                arrived(g.b0, j)
                w = slab((4 * g.b0 + j) % RING, 36)
                for k in range(4):
                    kt = 4 * j + k
                    for h in range(TH):
                        mm = pe.matmul(pair[h][:, 0:36], xnT[:, kt, h * P:h * P + P], w[:, k, :],
                                       start=(kt == 0), stop=(kt == KT - 1), skip_group_check=True)
                mm.then_inc(chunks_used, 1)
            product("nsa_zq", features, xn)
            product("nsa_qm", features, xn)
            product("nsa_zm", features, xn)
            for t in range(24, 36, 2):
                swap_halves(proj[0:ROT, t:t + 2, :], 2 * T)
            pe.wait_ge(rope_done, len(ROPE_TURNS))
            pe.wait_ge(rows_scaled, 3)
            turn_rows()
            pe.wait_ge(rows_kept, 32)
            product("mem_k1", features, yt)
            product("mem_v1", token_rows, yt)
            pe.wait_ge(evac_a, PLAN["out1"].g0)
            pe.wait_ge(evac_b, PLAN["out1"].g0)
            attend(NSA)
            attend(MEM1)
            pe.wait_ge(y_ready, Y_NSA)
            product("out1", features, yt)
            norm_sum()
            for n in range(8):
                pe.wait_ge(final_ready, 4 * (n // 2) + 4)
                if n >= 2:
                    pe.wait_ge(final_kept, n - 1)
                h, c = n % 2, n // 2
                for k in range(4):
                    mm = pe.transpose(bank[5 + n % 2][:, k * P:k * P + P], yT[:, 4 * c + k, h * P:h * P + P],
                                      ident[:, :])
                mm.then_inc(final_turned, 1)

        @block.scalar
        def _(act):
            count = [0]

            def then(ins):
                count[0] += 1
                ins.then_inc(act_order, 1)
                act.wait_ge(act_order, count[0])

            def keep_first(name, dst, per=1):
                g = PLAN[name]
                if g.g0:
                    act.wait_ge(evac_a, g.g0)
                peel = g.groups if g.groups < 4 else (2 if g.b0 == 0 else 0)
                for n in range(peel):
                    act.wait_ge(chunks_used, g.made(n))
                    act.activation(dst(n), bank[2 * ((g.g0 + n) % 2)][:, :], ACT.Copy).then_inc(evac_a, 1)
                if peel < g.groups:
                    with act.Fori(0, (g.groups - peel) // 2) as i:
                        for q in range(2):
                            n = g.g0 + peel + q
                            act.wait_ge(chunks_used, i * (2 * g.chunks) + g.made(peel + q))
                            act.wait_ge(evac_a, g.g0 + peel)
                            act.activation(dst(i * 2 + (peel + q)), bank[2 * (n % 2)][:, :], ACT.Copy)\
                               .then_inc(evac_a, 1)

            def tiles(t0):
                return lambda n: proj[:, bass.ds(n * 4 + t0, 2), :].rearrange("p a t -> p (a t)")

            def rows(v):
                return lambda n: v[:, 0, bass.ds(n * 512, 512)]

            normed = [0]

            def norm_squares_and_root():
                n = normed[0]
                for c in range(4):
                    act.activation(scratch[:, c * 1024:c * 1024 + 1024],
                                   hT[:, 4 * c:4 * c + 4, :].rearrange("p a t -> p (a t)"), ACT.Square)\
                       .then_inc(norm_squares, 1)
                act.wait_ge(norm_sums, n + 1)
                act.activation(rstd[:, 0, 0:T], bank[4][:, 0:T], ACT.Sqrt, scale=1.0 / D, bias=eps_col[:, 0:1])\
                   .then_inc(norm_root, 1)
                normed[0] += 1

            def row_squares(n):
                act.wait_ge(tokens_in, 16 * (n + 2))
                for h in range(TH):
                    last = act.activation(xflat[:, h * D:h * D + D], tokens[:, h, :], ACT.Square,
                                          accum_out=tok_rstd[:, h:h + 1])
                last.then_inc(rows_squared, 1)
                act.wait_ge(rows_squared, 2 * n + 1)
                act.activation(tok_rstd[:, 2:4], tok_rstd[:, 0:2], ACT.Sqrt, scale=1.0 / D, bias=eps_col[:, 0:1])\
                   .then_inc(rows_squared, 1)

            def head_norms(pairs):
                first, end = pairs[0], pairs[-1] + 1
                for n in range(first, end + 1):
                    if n < end:
                        if n >= 2:
                            act.wait_ge(head_sums, n - 1)
                        act.activation(head_sq[:, n % 2, :], pair_tile(norm_pairs[n][0]), ACT.Square)\
                           .then_inc(head_squares, 1)
                    if n > first:
                        m = n - 1
                        act.wait_ge(head_sums, m + 1)
                        if m >= 2:
                            act.wait_ge(head_normed, m - 1)
                        act.activation(rstd[:, m % 2, :], bank[4 + m % 2][:, :], ACT.Sqrt, scale=1.0 / HD,
                                       bias=eps_col[:, 0:1]).then_inc(head_root, 1)

            def exps(n):
                it = items[n]
                act.wait_ge(max_ready, n + 1)
                if n >= 2:
                    act.wait_ge(probs_turned, n - 1)
                for h in range(TH):
                    w = it.widths[h]
                    src = bank[4 + n % 2][:, h * T:h * T + w] if it.mask is None else masked_scores[:, n % 2, h, 0:w]
                    last = act.activation(probs[:, n % 2, h, 0:w], src, ACT.Exp, scale=ATT_SCALE,
                                          bias=stats[:, n % 2, 2 + h:3 + h], accum_out=stats[:, n % 2, 4 + h:5 + h])
                last.then_inc(exp_ready, 1)

            def keep_turned(n):
                it = items[n]
                act.wait_ge(probs_turned, n + 1)
                if n >= 2:
                    act.wait_ge(values_summed, n - 1)
                r = N_CMP if it.widths == CMP else P
                c = slice(P, 3 * P) if it.widths == CMP else (slice(P, 4 * P) if it.widths == CAUSAL else slice(0, 4 * P))
                act.activation(probsT[0:r, n % 2, c], bank[6][0:r, c], ACT.Copy).then_inc(turned_kept, 1)

            def attend(which):
                first, end = which[0], which[-1] + 1
                for n in range(first, end + 1):
                    if n < end:
                        exps(n)
                    if n > first:
                        keep_turned(n - 1)

            act.wait_ge(rows_kept, 8)
            norm_squares_and_root()
            keep_first("hgrn_qf", tiles(0))
            keep_first("hgrn_v", rows(hgrn_v))
            keep_first("gate_q_k", tiles(16))
            keep_first("attn_v", rows(attn_v))
            keep_first("idx_q", tiles(40))
            g = PLAN["idx_tail"].g0
            act.wait_ge(chunks_used, PLAN["idx_tail"].made())
            act.wait_ge(evac_a, g)
            act.activation(ikT[0:64, :], bank[2 * (g % 2)][0:64, 0:T], ACT.Copy)
            act.activation(ikT[64:128, :], bank[2 * (g % 2)][0:64, 0:T], ACT.Copy).then_inc(evac_a, 1)

            act.wait_ge(gains_ready, 1)
            act.wait_ge(hg_dve, 1)
            act.activation(lower[:, 0:8], lower[:, 8:16], ACT.Sigmoid).then_inc(hg_act, 1)
            act.wait_ge(evac_b, g)
            for hg in range(2):
                qs, fs = hg_tiles(hg)
                act.activation(fs, fs, ACT.Sigmoid).then_inc(hg_act, 1)
                if hg:
                    act.wait_ge(hg_done, 2)
                act.activation(hg_tmp, qs, ACT.Sigmoid).then_inc(hg_act, 1)
                act.activation(pair_tile(16 + 4 * hg, 4), pair_tile(16 + 4 * hg, 4), ACT.Silu).then_inc(hg_act, 1)
                act.wait_ge(hg_dve, 3 * hg + 2)
                act.activation(hg_logf, fs, ACT.Ln).then_inc(hg_act, 1)
                for n in range(HG_OPS):
                    act.wait_ge(hg_exp, 2 * (HG_OPS * hg + n) + 1)
                    act.activation(hg_decay, hg_decay, ACT.Exp).then_inc(hg_exp, 1)
                for c in range(2):
                    m = 2 * hg + c
                    act.wait_ge(hg_out, m + 1)
                    if m:
                        act.wait_ge(hg_sum, m)
                    act.activation(hg_osq, bank[6 + c][:, :], ACT.Square).then_inc(hg_square, 1)
                    act.wait_ge(hg_sum, m + 1)
                    if m:
                        act.wait_ge(hg_done, m)
                    act.activation(rstd[:, 0, :], bank[5][:, :], ACT.Sqrt, scale=1.0 / HD, bias=eps_col[:, 0:1])\
                       .then_inc(hg_root, 1)

            for n in range(IDX_HEADS):
                act.wait_ge(idx_logits, n + 1)
                if n >= 2:
                    act.wait_ge(idx_added, n - 1)
                act.activation(idx_relus[:, n % 2, :], bank[4 + n % 2][:, 0:3 * P], ACT.Relu).then_inc(idx_relu, 1)
            head_norms(MIX_PAIRS)
            attend(DSA)

            row_squares(0)
            act.wait_ge(rows_kept, 16)
            act.wait_ge(evac_b, PLAN["cross_q"].g0)
            norm_squares_and_root()
            keep_first("cross_q", tiles(16))
            keep_first("cross_k", tiles(20))
            keep_first("cross_v", rows(cross_v))
            act.wait_ge(evac_a, PLAN["cross_v"].g0)
            act.wait_ge(evac_b, PLAN["cross_v"].g0)
            head_norms(CROSS_PAIRS)
            attend(CROSS)

            act.wait_ge(evac_b, PLAN["up0"].g0)
            norm_squares_and_root()
            for half in range(2):
                g = PLAN[f"up{half}"]
                act.wait_ge(evac_a, g.g0)
                act.wait_ge(evac_b, g.g0)
                with act.Fori(0, 4) as i:
                    for q in range(2):
                        n = g.g0 + q
                        hid = tiles(0)(i * 2 + q)
                        act.wait_ge(chunks_used, i * (2 * g.chunks) + g.made(q))
                        act.wait_ge(evac_b, g.g0)
                        act.activation(hid, bank[2 * (n % 2)][:, :], ACT.Relu).then_inc(evac_a, 1)
                        act.activation(tiles(2)(i * 2 + q), bank[2 * (n % 2) + 1][:, :], ACT.Relu).then_inc(evac_b, 1)

            act.wait_ge(evac_b, PLAN["pool_in"].g0)
            norm_squares_and_root()
            keep_first("pool_in", tiles(0))
            act.wait_ge(evac_a, PLAN["mem_k0"].g0)
            act.wait_ge(evac_b, PLAN["mem_k0"].g0)
            for t in (12, 16, 20, 28):
                act.activation(pair_tile(t, 4), pair_tile(t, 4), ACT.Silu).then_inc(silu_ready, 1)
            row_squares(1)
            keep_first("mem_k0", tiles(48))
            keep_first("mem_v0", rows(mem_v0))
            attend(MEM0)

            act.wait_ge(evac_b, PLAN["cmp_kv"].g0)
            norm_squares_and_root()
            keep_first("cmp_kv", tiles(0))
            keep_first("sel_k", tiles(8))
            keep_first("sel_v", rows(sel_v))
            keep_first("win_k", tiles(16))
            keep_first("win_v", rows(win_v))
            act.wait_ge(rope_angle, 1)
            act.activation(rope_s[:, :], rope_s[:, :], ACT.Sin).then_inc(rope_sin, 1)
            act.activation(rope_c[:, :], rope_c[:, :], ACT.Sin, scale=-1.0, bias=eps_col[0:ROT, 1:2]).then_inc(rope_sin, 1)
            for c, name in enumerate(("cmp_hid_k", "cmp_hid_v")):
                g = PLAN[name].g0
                act.wait_ge(chunks_used, PLAN[name].made())
                for m in range(2):
                    last = act.activation(hidT[:, c, m, :], bank[2 * (g % 2)][:, m * 64:m * 64 + 4 * N_CMP], ACT.Silu)
                last.then_inc(evac_a, 1)
            act.wait_ge(rope_done, 5)
            norm_squares_and_root()
            keep_first("nsa_q", tiles(24))
            g = PLAN["nsa_gate"].g0
            act.wait_ge(chunks_used, PLAN["nsa_gate"].made())
            for h in range(TH):
                last = act.activation(nsa_gates[:, h, :], bank[2 * (g % 2) + h][:, 0:36], ACT.Sigmoid)
            last.then_inc(evac_a, 1)
            keep_first("nsa_zq", tiles(36))
            keep_first("nsa_qm", tiles(48))
            keep_first("nsa_zm", tiles(52))
            act.wait_ge(evac_a, PLAN["mem_k1"].g0)
            act.wait_ge(evac_b, PLAN["mem_k1"].g0)
            for t in (36, 40, 44, 52):
                act.activation(pair_tile(t, 4), pair_tile(t, 4), ACT.Silu).then_inc(silu_ready, 1)
            row_squares(2)
            keep_first("mem_k1", tiles(56))
            keep_first("mem_v1", rows(mem_v1))
            attend(NSA)
            attend(MEM1)
            act.wait_ge(evac_b, PLAN["out1"].g0 + 4)
            norm_squares_and_root()

        @block.vector
        def _(dve):
            count = [0]

            def then(ins):
                count[0] += 1
                ins.then_inc(dve_order, 1)
                dve.wait_ge(dve_order, count[0])

            def keep_second(name, dst):
                g = PLAN[name]
                if g.g0:
                    dve.wait_ge(evac_b, g.g0)
                peel = g.groups if g.groups < 4 else (2 if g.b0 == 0 else 0)
                for n in range(peel):
                    dve.wait_ge(chunks_used, g.made(n))
                    dve.tensor_copy(dst(n), bank[2 * ((g.g0 + n) % 2) + 1][:, :]).then_inc(evac_b, 1)
                if peel < g.groups:
                    with dve.Fori(0, (g.groups - peel) // 2) as i:
                        for q in range(2):
                            n = g.g0 + peel + q
                            dve.wait_ge(chunks_used, i * (2 * g.chunks) + g.made(peel + q))
                            dve.tensor_copy(dst(i * 2 + (peel + q)), bank[2 * (n % 2) + 1][:, :]).then_inc(evac_b, 1)

            def tiles(t0):
                return lambda n: proj[:, bass.ds(n * 4 + (t0 + 2), 2), :].rearrange("p a t -> p (a t)")

            def rows(v):
                return lambda n: v[:, 1, bass.ds(n * 512, 512)]

            def residual(name):
                g = PLAN[name]
                dve.wait_ge(evac_a, g.g0)
                with dve.Fori(0, 2) as i:
                    for q in range(2):
                        n = g.g0 + q
                        dve.wait_ge(chunks_used, i * (2 * g.chunks) + g.made(q))
                        for c, read_out in ((0, evac_a), (1, evac_b)):
                            h = hT[:, bass.ds(i * 8 + (4 * q + 2 * c), 2), :].rearrange("p a t -> p (a t)")
                            dve.tensor_tensor(h, bank[2 * (n % 2) + c][:, :], h, ALU.add).then_inc(read_out, 1)

            normed = [0]

            def norm(out, slot, cols, ready):
                dve.wait_ge(norm_root, normed[0] + 1)
                then(dve.reciprocal(rstd[:, 1, 0:T], rstd[:, 0, 0:T]))
                for kt in range(KT):
                    dve.scalar_tensor_tensor(out=out[:, kt, :], in0=hT[:, kt, :],
                                             scalar=gains[:, slot, cols.start + kt:cols.start + kt + 1],
                                             in1=rstd[:, 1, 0:T], op0=ALU.mult, op1=ALU.mult).then_inc(ready, 1)
                normed[0] += 1
                dve.wait_ge(ready, KT if ready is final_ready else KT * normed[0])

            def scale_rows(n):
                dve.wait_ge(rows_squared, 2 * n + 2)
                then(dve.reciprocal(tok_rstd[:, 4:6], tok_rstd[:, 2:4]))
                for h in range(TH):
                    last = dve.tensor_scalar(tokens[:, h, :], tokens[:, h, :], tok_rstd[:, 4 + h:5 + h], None, ALU.mult)
                last.then_inc(rows_scaled, 1)

            turned = [0]

            def keep_rows(out, cols=None):
                for n in range(KT // 2):
                    m = turned[0]
                    dve.wait_ge(rows_turned, m + 1)
                    if cols is None:
                        last = dve.tensor_copy(out[:, 2 * n:2 * n + 2, :].rearrange("p a t -> p (a t)"),
                                               bank[5 + m % 3][:, :])
                    else:
                        for c in range(2):
                            k = cols.start + 2 * n + c
                            last = dve.tensor_scalar(out[:, 2 * n + c, :], bank[5 + m % 3][:, c * T:c * T + T],
                                                     gains[:, 0, k:k + 1], None, ALU.mult)
                    last.then_inc(rows_kept, 1)
                    turned[0] += 1

            def head_norms(pairs):
                for n in pairs:
                    t, col = norm_pairs[n]
                    dve.wait_ge(head_root, n + 1)
                    then(dve.reciprocal(rstd[:, n % 2, :], rstd[:, n % 2, :]))
                    dve.scalar_tensor_tensor(out=pair_tile(t), in0=pair_tile(t), scalar=gains[:, 1, col:col + 1],
                                             in1=rstd[:, n % 2, :], op0=ALU.mult, op1=ALU.mult)\
                       .then_inc(head_normed, 1)

            def maxima(n):
                it = items[n]
                st = stats[:, n % 2, :]
                dve.wait_ge(scores_ready, n + 1)
                if n >= 2:
                    dve.wait_ge(exp_ready, n - 1)
                s = bank[4 + n % 2][:, :].rearrange("p (h s) -> p h s", h=TH)
                if it.mask is None:
                    last = dve.tensor_reduce(st[:, 0:2], s, AX, ALU.max)
                else:
                    for h in range(TH):
                        w = it.widths[h]
                        last = dve.tensor_tensor_reduce(masked_scores[:, n % 2, h, 0:w], s[:, h, 0:w],
                                                        it.mask[:, h, 0:w], 1.0, -3.4e38, ALU.add, ALU.max,
                                                        st[:, h:h + 1])
                then(last)
                dve.tensor_scalar(st[:, 2:4], st[:, 0:2], NEG / 8, -ATT_SCALE, ALU.max, ALU.mult)\
                   .then_inc(max_ready, 1)

            def normalise(n):
                it = items[n]
                st = stats[:, n % 2, :]
                dve.wait_ge(exp_ready, n + 1)
                sums = st[:, 4:6]
                if it.widths == CMP:
                    sums = st[:, 10:12]
                    then(dve.tensor_scalar(sums, st[:, 4:6], 1e-30, None, ALU.max))
                then(dve.reciprocal(st[:, 6:8], sums))
                if it.gate is not None:
                    then(dve.tensor_tensor(st[:, 6:8], st[:, 6:8], it.gate, ALU.mult))
                for h in range(TH):
                    w = it.widths[h]
                    p = probs[:, n % 2, h, 0:w]
                    last = dve.tensor_scalar(p, p, st[:, 6 + h:7 + h], None, ALU.mult)
                last.then_inc(probs_ready, 1)

            def keep_out(n):
                it = items[n]
                if not it.last:
                    return
                o = bank[7][:, 0:T]
                dve.wait_ge(values_summed, n + 1)
                if it.times is None:
                    last = dve.tensor_copy(it.out, o)
                else:
                    last = dve.tensor_tensor(it.out, o, it.times, ALU.mult)
                last.then_inc(out_kept, 1)

            def attend(which):
                first, end = which[0], which[-1] + 1
                for n in range(first, end + 2):
                    if n < end:
                        maxima(n)
                    if first <= n - 1 < end:
                        normalise(n - 1)
                    if first <= n - 2 < end:
                        keep_out(n - 2)
                outs = sum(items[n].last for n in which)
                dve.wait_ge(out_kept, outs_before[end])
                dve.sem_inc(y_ready, outs)

            dve.wait_ge(gains_turned, 1)
            dve.tensor_copy(gains[:, 0, :], bank[4][:, 0:P])
            dve.tensor_copy(gains[:, 1, 0:65], bank[4][:, P:P + 65])
            dve.tensor_copy(pe_cols[:, :, :].rearrange("p i l -> p (i l)"), bank[4][:, 2 * P:2 * P + 64])\
               .then_inc(gains_ready, 1)
            keep_rows(hT)
            dve.wait_ge(gains_ready, 1)
            norm(xnT, 0, G_MIX, xn_ready)
            keep_second("hgrn_qf", tiles(0))
            keep_second("hgrn_v", rows(hgrn_v))
            keep_second("gate_q_k", tiles(16))
            keep_second("attn_v", rows(attn_v))
            keep_second("idx_q", tiles(40))
            g = PLAN["idx_tail"].g0
            dve.wait_ge(chunks_used, PLAN["idx_tail"].made())
            dve.tensor_scalar(idx_w[:, :, :].rearrange("p h n -> p (h n)"), bank[2 * (g % 2) + 1][:, 0:32],
                              IDX_SCALE, None, ALU.mult).then_inc(evac_b, 1)

            lb0 = gains[:, 1, G_LB.start:G_LB.start + 8]
            lb1 = gains[:, 1, G_LB.start + 8:G_LB.start + 16]
            dve.tensor_tensor(lower[:, 8:16], lb0, lb1, ALU.subtract).then_inc(hg_dve, 1)
            dve.wait_ge(hg_act, 1)
            then(dve.tensor_scalar(lower[:, 8:16], lower[:, 0:8], -1.0, 1.0, ALU.mult, ALU.add))
            dve.wait_ge(consts_ready, 3)
            then(dve.memset(hg_diag, 0.0))
            for hg in range(2):
                qs, fs = hg_tiles(hg)
                dve.wait_ge(hg_act, 1 + 4 * hg + 1)
                for h in range(4):
                    f = fs[:, h * T:h * T + T]
                    c = 4 * hg + h
                    last = dve.tensor_scalar(f, f, lower[:, 8 + c:9 + c], lower[:, c:c + 1], ALU.mult, ALU.add)
                last.then_inc(hg_dve, 1)
                dve.wait_ge(hg_act, 1 + 4 * hg + 2)
                dve.scalar_tensor_tensor(out=qs, in0=qs, scalar=ATT_SCALE, in1=hg_tmp, op0=ALU.mult, op1=ALU.mult)\
                   .then_inc(hg_dve, 1)
                dve.wait_ge(hg_act, 1 + 4 * hg + 4)
                dve.tensor_scalar(fs, fs, -1.0, 1.0, ALU.mult, ALU.add).then_inc(hg_dve, 1)
                then(dve.tensor_tensor_scan(hg_cum, hg_reset, hg_logf, 0.0, ALU.mult, ALU.add))
                dve.wait_ge(hg_dve, 3 * hg + 4)

                def place(n):
                    w = LEVELS[n]
                    if HG_SCORES * hg + n:
                        dve.wait_ge(hg_placed, HG_SCORES * hg + n)
                    dve.wait_ge(hg_scores, HG_SCORES * hg + n + 1)
                    out = hg_diag.rearrange("p m (b two w) -> p m b two w", two=2, w=w)[:, :, :, 1, :]
                    mask = spread(level_mask[:, n:n + 1, :], 1, 8).rearrange("p m (b w) -> p m b w", w=w)
                    got = bank[4 + n % 2][:, :].rearrange("p (m b w) -> p m b w", m=8, w=w)
                    dve.copy_predicated(out, mask.bitcast(I32), got).then_inc(hg_placed, 1)

                for n, w in enumerate(LEVELS):
                    if HG_OPS * hg + n:
                        dve.wait_ge(hg_operands, HG_OPS * hg + n)
                    cum = hg_cum.rearrange("p (b two w) -> p b two w", two=2, w=w)
                    dec = hg_decay.rearrange("p (b two w) -> p b two w", two=2, w=w)
                    mid = spread(cum[:, :, 0, w - 1:w], 2, w)
                    if w < CHUNK_T:
                        dve.tensor_tensor(dec[:, :, 1, :], cum[:, :, 1, :], mid, ALU.subtract)
                    else:
                        dve.tensor_copy(dec[:, :, 1, :], cum[:, :, 1, :])
                    dve.tensor_tensor(dec[:, :, 0, :], mid, cum[:, :, 0, :], ALU.subtract).then_inc(hg_exp, 1)
                    dve.wait_ge(hg_exp, 2 * (HG_OPS * hg + n) + 2)
                    if HG_SCORES * hg + n:
                        dve.wait_ge(hg_scores, HG_SCORES * hg + n)
                    dve.tensor_tensor(hg_keys, fs, hg_decay, ALU.mult)
                    q4 = qs.rearrange("p (b two w) -> p b two w", two=2, w=w)
                    dve.tensor_tensor(hg_queries.rearrange("p (b w) -> p b w", w=w), q4[:, :, 1, :], dec[:, :, 1, :],
                                      ALU.mult).then_inc(hg_operands, 1)
                    if n:
                        place(n - 1)
                place(len(LEVELS) - 1)
                n = len(LEVELS)
                dve.wait_ge(hg_placed, HG_SCORES * hg + n)
                dve.wait_ge(hg_scores, HG_SCORES * hg + n + 1)
                for c in range(2):
                    last = dve.copy_predicated(hg_diag[:, 4 * c:4 * c + 4, :],
                                               spread(ident[:, :].rearrange("p (m t) -> p m t", m=1), 1, 4).bitcast(I32),
                                               bank[4 + c][:, :].rearrange("p (m t) -> p m t", m=4))
                last.then_inc(hg_placed, 1)
                dve.wait_ge(hg_operands, HG_OPS * hg + len(LEVELS))
                cum = hg_cum.rearrange("p (h c t) -> p h c t", h=4, c=4)
                dec = hg_decay.rearrange("p (h c t) -> p h c t", h=4, c=4)
                total = lambda c: spread(cum[:, :, c, CHUNK_T - 1:CHUNK_T], 2, CHUNK_T)
                dve.tensor_copy(dec[:, :, 2, :], cum[:, :, 2, :])
                dve.tensor_tensor(dec[:, :, 3, :], cum[:, :, 3, :], total(2), ALU.add)
                dve.tensor_tensor(dec[:, :, 1, :], total(1), cum[:, :, 1, :], ALU.subtract)
                then(dve.tensor_tensor(dec[:, :, 0, :], total(0), cum[:, :, 0, :], ALU.subtract))
                dve.tensor_tensor(dec[:, :, 0, :], dec[:, :, 0, :], total(1), ALU.add).then_inc(hg_exp, 1)
                dve.wait_ge(hg_exp, 2 * (HG_OPS * (hg + 1)))
                halves = lambda x: x.rearrange("p (h c t) -> p h c t", h=4, c=2)
                dve.tensor_tensor(halves(hg_keys)[:, :, 0, :], halves(fs)[:, :, 0, :], halves(hg_decay)[:, :, 0, :],
                                  ALU.mult)
                dve.tensor_tensor(hg_queries.rearrange("p (h t) -> p h t", h=4), halves(qs)[:, :, 1, :],
                                  halves(hg_decay)[:, :, 1, :], ALU.mult).then_inc(hg_operands, 1)
                dve.wait_ge(hg_scores, HG_SCORES * (hg + 1))
                dve.tensor_copy(hg_cross.rearrange("p m t -> p (m t)"), bank[4][:, :]).then_inc(hg_placed, 1)
                for c in range(2):
                    m = 2 * hg + c
                    if m:
                        dve.wait_ge(hg_done, m)
                    dve.wait_ge(hg_root, m + 1)
                    then(dve.reciprocal(rstd[:, 1, :], rstd[:, 0, :]))
                    then(dve.scalar_tensor_tensor(out=hg_tmp[:, 0:512], in0=bank[6 + c][:, :],
                                                  scalar=gains[:, 1, G_ONORM:G_ONORM + 1], in1=rstd[:, 1, :],
                                                  op0=ALU.mult, op1=ALU.mult))
                    t = 4 * hg + 2 * c
                    dve.tensor_tensor(yT[:, t:t + 2, :].rearrange("p a t -> p (a t)"), hg_tmp[:, 0:512],
                                      pair_tile(16 + t), ALU.mult).then_inc(hg_done, 1)
            dve.wait_ge(hg_done, 4)
            dve.sem_inc(y_ready, 8)

            both = [(0, slice(0, P), P), (1, slice(P, P + T), T)]
            for n in range(IDX_HEADS):
                dve.wait_ge(idx_relu, n + 1)
                if n:
                    dve.wait_ge(idx_added, n)
                for h, c, w in both:
                    acc, r, wt = idx_score[:, h, 0:w], idx_relus[:, n % 2, c], idx_w[:, h, n:n + 1]
                    if n == 0:
                        last = dve.tensor_scalar(acc, r, wt, None, ALU.mult)
                    else:
                        last = dve.scalar_tensor_tensor(out=acc, in0=r, scalar=wt, in1=acc, op0=ALU.mult, op1=ALU.add)
                last.then_inc(idx_added, 1)
            dve.wait_ge(idx_added, IDX_HEADS)
            for h, c, w in both:
                acc, bias = idx_score[:, h, 0:w], sel_bias[:, h, 0:w]
                then(dve.tensor_tensor(acc, acc, causal[:, h, 0:w], ALU.add))
                for r in range(TOPK // 8):
                    then(dve.max(best[:, h, :], acc))
                    then(dve.match_replace(acc, best[:, h, :], acc, TAKEN))
                then(dve.tensor_scalar(bias, acc, TAKEN / 2, NEG, ALU.is_gt, ALU.mult))
                then(dve.tensor_tensor(bias, bias, causal[:, h, 0:w], ALU.min))
            head_norms(MIX_PAIRS)
            attend(DSA)
            residual("mix_out")

            scale_rows(0)
            keep_rows(yT, G_MEM)
            norm(xnT, 0, G_CROSS, xn_ready)
            keep_second("cross_q", tiles(16))
            keep_second("cross_k", tiles(20))
            keep_second("cross_v", rows(cross_v))
            head_norms(CROSS_PAIRS)
            attend(CROSS)
            residual("cross_out")

            norm(xnT, 0, G_MLP, xn_ready)
            for half in range(2):
                g = PLAN[f"up{half}"]
                with dve.Fori(0, 4) as i:
                    for q in range(2):
                        n = g.g0 + q
                        hid = proj[:, bass.ds(i * 8 + 4 * q, 4), :].rearrange("p a t -> p (a t)")
                        dve.wait_ge(evac_b, i * 2 + (n + 1))
                        dve.tensor_tensor(hid, hid, hid, ALU.mult).then_inc(hidden_ready, 1)
                residual(f"down{half}")

            norm(xnT, 0, G_2A, xn_ready)
            count_t = pair_tile(56, 1)
            then(dve.memset(pair_tile(57, 1), 1.0))
            then(dve.tensor_tensor_scan(count_t, pair_tile(57, 1), pair_tile(57, 1), 0.0, ALU.mult, ALU.add))
            for n, win in enumerate(POOL_WINDOWS):
                then(dve.tensor_scalar(pair_tile(44 + n, 1), count_t, float(win), None, ALU.min))
                then(dve.reciprocal(pair_tile(44 + n, 1), pair_tile(44 + n, 1)))
            keep_second("pool_in", tiles(0))
            scale_rows(1)
            keep_rows(yT, G_M2A)
            keep_second("mem_k0", tiles(48))
            keep_second("mem_v0", rows(mem_v0))
            dve.wait_ge(evac_a, PLAN["mem_k0"].g0)
            ping = proj[:, 56:59, :], proj[:, 59:62, :]
            for n, win in enumerate(POOL_WINDOWS):
                if n:
                    dve.wait_ge(pooled_ready, n)
                u = proj[:, 3 * n:3 * n + 3, :]
                src = u
                for s in range(n + 1):
                    d = 1 << s
                    dst = ping[s % 2]
                    dve.tensor_copy(dst[:, :, 0:d], src[:, :, 0:d])
                    then(dve.tensor_tensor(dst[:, :, d:T], src[:, :, d:T], src[:, :, 0:T - d], ALU.add))
                    src = dst
                rc = spread(proj[:, 44 + n:45 + n, :], 1, 3)
                then(dve.tensor_tensor(src, src, rc, ALU.mult))
                dve.tensor_tensor(proj[:, 32 + 3 * n:35 + 3 * n, :], src, u, ALU.subtract).then_inc(pooled_ready, 1)
            dve.wait_ge(silu_ready, 4)
            dve.wait_ge(evac_a, PLAN["pool_mix"].g0)
            for j in range(4):
                g = PLAN["pool_mix"].g0 + j
                dve.wait_ge(chunks_used, PLAN["pool_mix"].made(j))
                for f in range(3):
                    t = 3 * j + f
                    last = dve.scalar_tensor_tensor(out=yT[:, t, :], in0=bank[2 * (g % 2) + f // 2][:, (f % 2) * T:(f % 2) * T + T],
                                                    scalar=gains[:, 1, G_POOL.start + t:G_POOL.start + t + 1],
                                                    in1=proj[:, 12 + t, :], op0=ALU.mult, op1=ALU.mult)
                    if f == 1:
                        last.then_inc(evac_a, 1)
                last.then_inc(evac_b, 1)
            dve.wait_ge(evac_b, PLAN["pool_mix"].g0 + 4)
            dve.sem_inc(y_ready, 12)
            attend(MEM0)
            residual("out0")

            norm(xnT, 1, G_KV, xn_ready)
            keep_second("cmp_kv", tiles(0))
            keep_second("sel_k", tiles(8))
            keep_second("sel_v", rows(sel_v))
            keep_second("win_k", tiles(16))
            keep_second("win_v", rows(win_v))
            dve.wait_ge(misc_in, 32)
            dve.tensor_copy(rstd[0:1, 0, 0:T], pos_i[:, :]).then_inc(rope_pos, 1)
            dve.wait_ge(rope_pos, 2)
            col = stats[0:ROT, 0, 8:9]
            then(dve.tensor_copy(col, bank[6][0:ROT, 0:1]))
            ang, turns = rope_s[:, :], rope_c[:, :]
            then(dve.tensor_scalar(ang, bank[5][0:ROT, 0:T], col, None, ALU.mult))
            then(dve.tensor_scalar(turns, ang, 0.15915494309189535, 12582912.0, ALU.mult, ALU.add))
            then(dve.tensor_scalar(turns, turns, 12582912.0, None, ALU.subtract))
            for part in TWO_PI_PARTS:
                then(dve.scalar_tensor_tensor(out=ang, in0=turns, scalar=-part, in1=ang, op0=ALU.mult, op1=ALU.add))
            then(dve.tensor_scalar(ang, ang, 3.1415925, -3.1415925, ALU.min, ALU.max))
            then(dve.tensor_scalar(turns, ang, -1.0, None, ALU.mult))
            dve.tensor_tensor(turns, turns, ang, ALU.max).then_inc(rope_angle, 1)
            dve.wait_ge(rope_sin, 2)
            dve.sem_inc(rope_tables, 1)

            def rotate(n):
                x, tiles_, t_from = ROPE_TURNS[n]
                if t_from is None:
                    c = spread(rope_c[:, :].rearrange("p (m t) -> p m t", m=1), 1, 2)
                    s = spread(rope_s[:, :].rearrange("p (m t) -> p m t", m=1), 1, 2)
                    view = lambda y: y[0:ROT, 0:2 * T].rearrange("p (m t) -> p m t", m=2)
                else:
                    c, s = (spread(y[:, t_from:T:CMP_STRIDE].rearrange("p (m t) -> p m t", m=1), 1, 4)
                            for y in (rope_c, rope_s))
                    view = lambda y: y[0:ROT, 0:4 * N_CMP].rearrange("p (m t) -> p m t", m=4)
                b = bank[5 + n % 2]
                a_, b_ = view(rstd[:, 0, :]), view(rstd[:, 1, :])
                if n:
                    dve.wait_ge(rope_done, n)
                dve.wait_ge(rope_swapped, n + 1)
                dve.tensor_tensor(a_, x, c, ALU.mult)
                then(dve.tensor_tensor(b_, view(b), s, ALU.mult))
                dve.tensor_tensor(x, a_, b_, ALU.add).then_inc(rope_done, 1)

            dve.wait_ge(evac_a, PLAN["cmp_hid_k"].g0)
            for n in range(4):
                rotate(n)
            for c in range(2):
                for kv in range(4):
                    z = proj[:, 4 * c + kv, :].rearrange("p (m r) -> p r m", r=CMP_STRIDE)
                    for half in range(2):
                        l = slice(CMP_STRIDE * half, CMP_STRIDE * half + CMP_STRIDE)
                        last = dve.tensor_tensor(zpe(c)[:, l, kv * N_CMP:kv * N_CMP + N_CMP],
                                                 z[:, :, half:half + N_CMP],
                                                 spread(pe_cols[:, c, l].rearrange("p (l n) -> p l n", n=1), 2, N_CMP),
                                                 ALU.add)
                last.then_inc(zpe_ready, 1)
            dve.wait_ge(evac_b, PLAN["cmp_hid_k"].g0)
            for c, name in enumerate(("cmp_hid_k", "cmp_hid_v")):
                dve.wait_ge(chunks_used, PLAN[name].made())
                dve.sem_inc(evac_b, 1)
            dve.wait_ge(cmp_second, 1)
            dve.tensor_copy(vcmp[0:N_CMP, :, :].rearrange("p m d -> p (m d)"), bank[5][0:N_CMP, :])
            dve.tensor_copy(kcmpT[:, 0:4 * N_CMP], bank[7][:, 0:4 * N_CMP]).then_inc(cmp_ready, 1)
            dve.wait_ge(cmp_ready, 1)
            rotate(4)
            norm(xnT, 0, G_2B, xn_ready)
            keep_second("nsa_q", tiles(24))
            g = PLAN["nsa_gate"].g0
            dve.wait_ge(evac_b, g)
            dve.wait_ge(evac_a, g + 1)
            dve.sem_inc(evac_b, 1)
            keep_second("nsa_zq", tiles(36))
            keep_second("nsa_qm", tiles(48))
            keep_second("nsa_zm", tiles(52))
            for n in range(5, len(ROPE_TURNS)):
                rotate(n)
            scale_rows(2)
            keep_rows(yT, G_M2B)
            keep_second("mem_k1", tiles(56))
            keep_second("mem_v1", rows(mem_v1))
            dve.wait_ge(silu_ready, 8)
            attend(NSA)
            attend(MEM1)
            residual("out1")

            norm(yT, 1, G_FINAL, final_ready)
            for n in range(8):
                h, c = n % 2, n // 2
                dve.wait_ge(final_turned, n + 1)
                dve.tensor_copy(tokens[:, h, c * 512:c * 512 + 512], bank[5 + n % 2][:, :]).then_inc(final_kept, 1)


_INS = ['x', 'mem', 'norm_mix', 'w_in', 'hgrn_lb_logits', 'hgrn_onorm', 'attn_qnorm', 'attn_knorm', 'w_out',
        'norm_cross', 'mem_norm', 'wq_x', 'wk_x', 'wv_x', 'wo_x', 'xq_norm', 'xk_norm', 'norm_mlp', 'w_up',
        'w_down', 'mem_2', 'positions_2', 'norm_g_2', 'mem_norm_g_2', 'w_mem_kv_2', 'w_out_2', 'a_w_in_2',
        'a_w_pool_2', 'a_pool_scale_2', 'b_w_in_2', 'kv_norm_g_2', 'w_kv_2', 'cmp_pe_2', 'cmp_w1_2', 'cmp_w2_2',
        'final_g_2']


def kernel(**inputs):
    import numpy as np
    import concourse.bacc as bacc
    from concourse.bass_utils import run_bass_kernel_spmd

    nc = bacc.Bacc("TRN2", target_bir_lowering=False, num_devices=1, dynamic_dma_scratch_size=1024)
    arrays, args = {}, {}
    for name in _INS:
        arr = np.ascontiguousarray(inputs[name])
        arrays[f"in_{name}"] = arr
        args[name] = nc.dram_tensor(f"in_{name}", arr.shape, mybir.dt.from_np(arr.dtype), kind="ExternalInput").ap()
    args["out"] = nc.dram_tensor("out", (1, T, D), F32, kind="ExternalOutput").ap()
    build_program(nc, args)
    r = run_bass_kernel_spmd(nc, [arrays], core_ids=[0])
    return r.results[0]["out"]
```

```python
from contextlib import ExitStack

import concourse.bass as bass
from concourse import mybir

F32 = mybir.dt.float32
I32 = mybir.dt.int32
F32R = mybir.dt.float32r
ALU = mybir.AluOpType
ACT = mybir.ActivationFunctionType
AX = mybir.AxisListType.X

P = 128
D = 2048
KT = D // P
T = 256
TH = T // P
HD = 128
FF_PART = 2048
EPS = 1e-6
ATT_SCALE = HD ** -0.5
RING = 4
CHUNK = 2048
UNITS = 4
NEG = -1e30
TAKEN = -3e38
TOPK = 64
IDX_HEADS = 16
IDX_SCALE = IDX_HEADS ** -0.5 * 64 ** -0.5
CMP_LEN, CMP_STRIDE = 32, 16
N_CMP = (T - CMP_LEN) // CMP_STRIDE + 1
ROPE_THETA = 500000.0
ROT = HD // 4
POOL_WINDOWS = (2, 4, 8, 16)
CHUNK_T = 64
LEVELS = (1, 2, 4, 8, 16, 32, 64)
TWO_PI_PARTS = (6.28125, 0.0019354820251464844, -1.7484556025237907e-07)


def spread(ap, dim, count):
    shape = list(ap.shape)
    shape[dim] = count
    return ap.broadcast_to(shape)


class Gemm:

    def __init__(self, b0, blocks, g0, groups, rows, width):
        self.b0, self.blocks, self.g0, self.groups, self.rows, self.width = b0, blocks, g0, groups, rows, width
        self.units = 8 * blocks // groups

    def made(self, n=0):
        return 8 * self.b0 + self.units * (n + 1)

    def unit(self, u):
        half = (self.rows + 1) // 2
        return (0, half) if u % 2 == 0 else (half, self.rows - half)


def plan_stream():
    order = [("hgrn_qf", 4, 4), ("hgrn_v", 2, 2), ("gate_q_k", 6, 6), ("idx_q", 2, 2), ("idx_tail", 1, 1, 4, 80),
             ("attn_v", 2, 2), ("cross_k", 1, 1), ("cross_v", 1, 1),
             ("mem_k0", 1, 1), ("mem_v0", 1, 1), ("mem_k1", 1, 1), ("mem_v1", 1, 1), ("mix_out", 4, 4),
             ("cross_q", 1, 1), ("cross_out", 1, 4),
             *((f"{side}{part}", 4, 4) for part in range(4) for side in ("up", "down")),
             ("pool_in", 8, 8), ("pool_mix", 1, 4, 3, 384), ("out0", 4, 4),
             ("cmp_kv", 2, 2), ("sel_k", 1, 1), ("sel_v", 1, 1), ("win_k", 1, 1), ("win_v", 1, 1),
             ("cmp_hid_k", 1, 1, 8, 256), ("cmp_hid_v", 1, 1, 8, 256),
             ("nsa_q", 3, 3), ("nsa_gate", 1, 1, 4, 36), ("nsa_zq", 3, 3), ("nsa_qm", 1, 1), ("nsa_zm", 1, 1),
             ("out1", 4, 4)]
    plan, b, g = {}, 0, 0
    for name, blocks, groups, *shape in order:
        plan[name] = Gemm(b, blocks, g, groups, *(shape or (4, 512)))
        b += blocks
        g += groups
    return plan


def build_program(nc, a):
    PLAN = plan_stream()
    ctx = ExitStack()
    with ctx:
        def sb(name, shape, dt=F32):
            return ctx.enter_context(nc.sbuf_tensor(name, shape, dt))

        def sem(name):
            return ctx.enter_context(nc.semaphore(name))

        proj_at = (nc.sbuf_base + 31) // 32 * 32
        proj = sb("proj", [P, 64, T])
        hidden = nc.alloc_sbuf_tensor_at("hidden", [P, 2, KT, T], F32R, offset=proj_at)
        hT = sb("hT", [P, KT, T])
        x_high = sb("x_high", [P, KT, T], F32R)
        x_low = sb("x_low", [P, KT, T], F32R)
        ring = sb("ring", [P, RING, CHUNK])
        w_high = sb("w_high", [P, UNITS, CHUNK // 2], F32R)
        w_low = sb("w_low", [P, UNITS, CHUNK // 2], F32R)
        scratch = sb("scratch", [P, 6144])
        heads_scratch = sb("heads_scratch", [P, 3072])
        ident = sb("ident", [P, P])
        ones = sb("ones", [P, P])
        gains = sb("gains", [P, 2, P])
        pe_cols = sb("pe_cols", [P, 2, CMP_LEN])
        lower = sb("lower", [P, 16])
        causal = sb("causal", [P, TH, T])
        cmp_mask = sb("cmp_mask", [P, TH, 16])
        rstd = sb("rstd", [P, 2, 2 * T])
        ikT = sb("ikT", [P, T])
        idx_w = sb("idx_w", [P, TH, 16])
        small = sb("small", [P, 64])
        stats = sb("stats", [P, 2, 16])
        best = sb("best", [P, TH, 8])
        nsa_gates = sb("nsa_gates", [P, TH, 36])
        swap = sb("swap", [ROT, ROT])
        inv_row = sb("inv_row", [1, ROT])
        eps_col = sb("eps_col", [P, 4])
        tok_rstd = sb("tok_rstd", [P, 8])
        kcmpT = sb("kcmpT", [P, 64])
        bank = [ctx.enter_context(nc.psum_tensor(f"bank{i}", [P, 512], F32)) for i in range(8)]

        landed = [sem(f"landed{i}") for i in range(RING)]
        units_used = sem("units_used")
        high_ready = sem("high_ready")
        low_ready = sem("low_ready")
        evacuated = sem("evacuated")
        gains_in = sem("gains_in")
        tokens_in = sem("tokens_in")
        misc_in = sem("misc_in")
        out_stored = sem("out_stored")
        consts_ready = sem("consts_ready")
        pool_order = sem("pool_order")
        dve_order = sem("dve_order")
        act_order = sem("act_order")
        gains_turned = sem("gains_turned")
        gains_ready = sem("gains_ready")
        rows_scaled = sem("rows_scaled")
        rows_squared = sem("rows_squared")
        rows_turned = sem("rows_turned")
        rows_kept = sem("rows_kept")
        norm_squares = sem("norm_squares")
        norm_sums = sem("norm_sums")
        norm_root = sem("norm_root")
        x_ready = sem("x_ready")
        out_ready = sem("out_ready")
        idx_turned = sem("idx_turned")
        idx_keys = sem("idx_keys")
        head_squares = sem("head_squares")
        head_sums = sem("head_sums")
        head_root = sem("head_root")
        head_normed = sem("head_normed")
        scores_ready = sem("scores_ready")
        max_ready = sem("max_ready")
        exp_ready = sem("exp_ready")
        probs_ready = sem("probs_ready")
        probs_turned = sem("probs_turned")
        turned_kept = sem("turned_kept")
        values_summed = sem("values_summed")
        out_kept = sem("out_kept")
        hg_act = sem("hg_act")
        hg_dve = sem("hg_dve")
        hg_exp = sem("hg_exp")
        hg_pe = sem("hg_pe")
        hg_operands = sem("hg_operands")
        hg_scores = sem("hg_scores")
        hg_placed = sem("hg_placed")
        hg_out = sem("hg_out")
        hg_square = sem("hg_square")
        hg_sum = sem("hg_sum")
        hg_root = sem("hg_root")
        hg_done = sem("hg_done")
        idx_logits = sem("idx_logits")
        idx_relu = sem("idx_relu")
        idx_added = sem("idx_added")
        mask_ready = sem("mask_ready")
        silu_ready = sem("silu_ready")
        hidden_ready = sem("hidden_ready")
        hidden_squared = sem("hidden_squared")
        rope_pos = sem("rope_pos")
        rope_angle = sem("rope_angle")
        rope_sin = sem("rope_sin")
        rope_tables = sem("rope_tables")
        rope_swapped = sem("rope_swapped")
        rope_done = sem("rope_done")
        hid_act = sem("hid_act")
        cmp_second = sem("cmp_second")
        cmp_ready = sem("cmp_ready")
        final_turned = sem("final_turned")
        final_kept = sem("final_kept")

        G_MIX, G_CROSS, G_MEM, G_MLP, G_2A, G_2B, G_M2A, G_M2B = (slice(16 * i, 16 * i + 16) for i in range(8))
        G_KV, G_FINAL = slice(0, 16), slice(16, 32)
        G_POOL, G_LB = slice(32, 44), slice(44, 60)
        G_ONORM, G_QN, G_KN, G_XQ, G_XK = 60, 61, 62, 63, 64

        hgrn_v = proj[:, 48:56, :].rearrange("p a t -> p (a t)").rearrange("p (h n) -> p h n", h=TH)
        attn_v = proj[:, 0:8, :].rearrange("p a t -> p (a t)").rearrange("p (h n) -> p h n", h=TH)

        def values_at(tile):
            return proj[:, tile:tile + 4, :].rearrange("p a t -> p (a t)").rearrange("p (h n) -> p h n", h=TH)

        cross_v, mem_v0, sel_v, win_v, mem_v1 = (values_at(t) for t in (12, 52, 12, 20, 60))
        tokens = scratch[:, 0:TH * D].rearrange("p (h n) -> p h n", h=TH)
        gain_rows = scratch[:, 5120:5504].rearrange("p (s c) -> p s c", s=3)
        masked_scores = heads_scratch[:, 0:1024].rearrange("p (b h s) -> p b h s", b=2, h=TH)
        probs = heads_scratch[:, 1024:2048].rearrange("p (b h s) -> p b h s", b=2, h=TH)
        probsT = heads_scratch[:, 2048:3072].rearrange("p (b n) -> p b n", b=2)
        sel_bias = scratch[:, 4096:4608].rearrange("p (h s) -> p h s", h=TH)
        idx_score = scratch[:, 4608:5120].rearrange("p (h s) -> p h s", h=TH)
        idx_relus = scratch[:, 0:768].rearrange("p (b n) -> p b n", b=2)
        idx_rows = scratch[:, 768:768 + 160].rearrange("p (h n) -> p h n", h=TH)
        head_sq = scratch[:, 5120:6144].rearrange("p (b n) -> p b n", b=2)

        vcmp = scratch[0:16, 4096:4608].rearrange("p (m d) -> p m d", m=4)
        rope_c, rope_s = (scratch[0:ROT, c:c + T] for c in (4848, 5104))
        pos_i = scratch[0:1, 5376:5632].bitcast(I32)
        cmp_w2 = scratch[:, 5632:6144].rearrange("p (i m d) -> p i m d", i=2, m=2)

        hg_logf, hg_cum, hg_decay, hg_keys, hg_queries, hg_reset, hg_tmp, hg_osq = (
            scratch[:, 512 * n:512 * n + 512] for n in range(8))
        level_mask = scratch[:, 4096:4096 + len(LEVELS) * CHUNK_T].rearrange("p (n t) -> p n t", t=CHUNK_T)
        hg_diag = heads_scratch[:, 0:2048].rearrange("p (m t) -> p m t", t=P)
        hg_cross = heads_scratch[:, 2048:3072].rearrange("p (m t) -> p m t", t=P)
        hidT = scratch[:, 4608:4608 + 16 * N_CMP].rearrange("p (c m n) -> p c m n", c=2, m=2)

        def zpe(x, c):
            n = CMP_LEN * 4 * N_CMP
            return x[:, 8 * c:8 * c + 8, :].rearrange("p a t -> p (a t)")[:, 0:n].rearrange("p (l n) -> p l n", l=CMP_LEN)

        ROPE_TURNS = ([(proj[0:ROT, t:t + 2, :], 2, None) for t in (8, 10, 16, 18)]
                      + [(kcmpT[0:ROT, 0:4 * N_CMP].rearrange("p (m t) -> p m t", m=4), 4, CMP_LEN - 1)]
                      + [(proj[0:ROT, t:t + 2, :], 2, None) for t in range(24, 36, 2)])

        block = ctx.enter_context(nc.Block())

        norm_pairs = ([(24 + 2 * n, G_QN) for n in range(4)] + [(32 + 2 * n, G_KN) for n in range(4)]
                      + [(16 + 2 * n, G_XQ) for n in range(2)] + [(8 + 2 * n, G_XK) for n in range(2)])
        MIX_PAIRS, CROSS_PAIRS = range(0, 8), range(8, 12)

        class Item:
            def __init__(self, q, k, v, widths, out, mask=None, gate=None, first=True, last=True, times=None):
                self.q, self.k, self.v, self.widths, self.out = q, k, v, widths, out
                self.mask, self.gate, self.first, self.last, self.times = mask, gate, first, last, times

        CAUSAL, FULL, CMP = (P, T), (T, T), (N_CMP, N_CMP)
        items = []
        for h in range(8):
            items.append(Item(proj[:, 24 + h, :], proj[:, 32 + h, :], attn_v[:, :, h * HD:h * HD + HD],
                              CAUSAL, proj[:, 24 + h, :], mask=sel_bias))
        DSA = range(0, 8)
        for h in range(4):
            items.append(Item(proj[:, 16 + h, :], proj[:, 8 + h, :], cross_v[:, :, h * HD:h * HD + HD],
                              FULL, proj[:, 28 + h, :]))
        CROSS = range(8, 12)
        for h in range(4):
            items.append(Item(proj[:, 24 + h, :], proj[:, 48 + h, :], mem_v0[:, :, h * HD:h * HD + HD],
                              FULL, proj[:, 28 + h, :], times=proj[:, 28 + h, :]))
        MEM0 = range(12, 16)
        for h in range(12):
            kv = h // 3
            for branch in range(3):
                q = proj[:, 24 + h, :]
                gate = nsa_gates[:, :, 3 * h + branch]
                if branch == 0:
                    it = Item(q, kcmpT[:, kv * N_CMP:kv * N_CMP + N_CMP], vcmp[:, kv, :], CMP, None,
                              mask=cmp_mask, gate=gate, last=False)
                elif branch == 1:
                    it = Item(q, proj[:, 8 + kv, :], sel_v[:, :, kv * HD:kv * HD + HD], CAUSAL, None,
                              mask=causal, gate=gate, first=False, last=False)
                else:
                    it = Item(q, proj[:, 16 + kv, :], win_v[:, :, kv * HD:kv * HD + HD], CAUSAL, proj[:, 36 + h, :],
                              mask=causal, gate=gate, first=False, times=proj[:, 36 + h, :])
                items.append(it)
        NSA = range(16, 52)
        for h in range(4):
            items.append(Item(proj[:, 48 + h, :], proj[:, 56 + h, :], mem_v1[:, :, h * HD:h * HD + HD],
                              FULL, proj[:, 52 + h, :], times=proj[:, 52 + h, :]))
        MEM1 = range(52, 56)
        outs_before = [sum(it.last for it in items[:n]) for n in range(len(items) + 1)]

        operands, x_made = [("mix", 4), ("cross_mem", 4), ("mem0", 4), ("mem1", 4), ("mix_y", 4), ("cross", 4),
                            ("cross_y", 1), ("mlp", 4), ("pool", 4), ("pooled", 4), ("pool_y", 4), ("kv", 4),
                            ("blocks", 2), ("nsa", 4), ("nsa_y", 4)], {}
        total = 0
        for name, n in operands:
            x_made[name] = total
            total += n

        def hg_tiles(hg):
            return pair_tile(2 * hg), pair_tile(8 + 2 * hg)

        def pair_tile(n, step=2):
            return proj[:, n:n + step, :].rearrange("p a t -> p (a t)")

        STEPS = len(LEVELS) + 2

        def exps_before(hg, s):
            return 2 * (len(LEVELS) + 1) * hg + 2 * min(s, len(LEVELS))

        @block.sync
        def _(sp):
            x_rows = a["x"].rearrange("a (h p) n -> p (a h) n", p=P)
            mem_rows = a["mem"].rearrange("a (h p) n -> p (a h) n", p=P)
            mem2_rows = a["mem_2"].rearrange("a (h p) n -> p (a h) n", p=P)
            sp.dma_start(tokens, x_rows).then_inc(tokens_in, 16)

            row = 0
            def gain(name, rows, view, slot):
                nonlocal row
                sp.dma_start(gain_rows[row:row + rows, slot, :], view).then_inc(gains_in, 16)
                row += rows

            for name, n in (("norm_mix", 16), ("norm_cross", 16), ("mem_norm", 16), ("norm_mlp", 16),
                            ("norm_g_2", 32), ("mem_norm_g_2", 32)):
                gain(name, n, a[name].rearrange("l (r c) -> (l r) c", c=P), 0)
            row = 0
            gain("kv_norm_g_2", 16, a["kv_norm_g_2"].rearrange("(r c) -> r c", c=P), 1)
            gain("final_g_2", 16, a["final_g_2"].rearrange("(r c) -> r c", c=P), 1)
            gain("a_pool_scale_2", 12, a["a_pool_scale_2"].rearrange("l (r c) -> (l r) c", c=P), 1)
            gain("hgrn_lb_logits", 16, a["hgrn_lb_logits"].rearrange("l (r c) -> (l r) c", c=P), 1)
            for name in ("hgrn_onorm", "attn_qnorm", "attn_knorm", "xq_norm", "xk_norm"):
                gain(name, 1, a[name], 1)
            row = 0
            gain("cmp_pe_2", 64, a["cmp_pe_2"].rearrange("i l d -> (i l) d"), 2)
            def stream(name, source):
                g = PLAN[name]

                def block_of(n, b, more):
                    for j in range(4):
                        need = 8 * b + 2 * j - 2 * RING + 2
                        if need > 0:
                            sp.wait_ge(low_ready, need + more)
                        dst = ring[:, j, 0:g.rows * g.width].rearrange("p (k n) -> p k n", k=g.rows)
                        sp.dma_start(dst, source(n, j)).then_inc(landed[j], 16)

                peel = g.blocks if g.blocks < 3 else int(g.b0 == 0)
                for n in range(peel):
                    block_of(n, g.b0 + n, 0)
                if peel < g.blocks:
                    with sp.Fori(0, g.blocks - peel) as i:
                        block_of(i + peel, g.b0 + peel, i * 8)

            def columns(w, col0):
                w3 = w.rearrange("(k p) n -> p k n", p=P)

                return lambda n, j: w3[:, 4 * j:4 * j + 4, bass.ds(n * 512 + col0, 512)]

            w_in = a["w_in"].rearrange("l k n -> (l k) n")
            stream("hgrn_qf", columns(w_in, 0))
            stream("hgrn_v", columns(w_in, 2048))
            stream("gate_q_k", columns(w_in, 3072))
            stream("idx_q", columns(w_in, 7168))
            w_in3 = w_in.rearrange("(k p) n -> p k n", p=P)
            stream("idx_tail", lambda n, j: w_in3[:, 4 * j:4 * j + 4, 8192:8272])
            stream("attn_v", columns(w_in, 6144))
            sp.wait_ge(mask_ready, 1)
            sp.dma_start(tokens, mem_rows).then_inc(tokens_in, 16)
            w_mem = a["w_mem_kv_2"].rearrange("l k n -> (l k) n")
            stream("cross_k", columns(a["wk_x"].rearrange("l k n -> (l k) n"), 0))
            stream("cross_v", columns(a["wv_x"].rearrange("l k n -> (l k) n"), 0))
            sp.wait_ge(rows_turned, 16)
            sp.dma_start(tokens, mem2_rows).then_inc(tokens_in, 16)
            stream("mem_k0", columns(w_mem[0:D, :], 0))
            stream("mem_v0", columns(w_mem[0:D, :], 512))
            stream("mem_k1", columns(w_mem[D:2 * D, :], 0))
            stream("mem_v1", columns(w_mem[D:2 * D, :], 512))
            stream("mix_out", columns(a["w_out"].rearrange("l k n -> (l k) n"), 0))
            stream("cross_q", columns(a["wq_x"].rearrange("l k n -> (l k) n"), 0))
            wo3 = a["wo_x"].rearrange("l (k p) n -> p (l k) n", p=P)
            stream("cross_out", lambda n, j: wo3[:, :, 512 * j:512 * j + 512])
            w_up = a["w_up"].rearrange("l k n -> (l k) n")
            w_down = a["w_down"].rearrange("l k n -> (l k) n")
            for part in range(4):
                stream(f"up{part}", columns(w_up, part * FF_PART))
                stream(f"down{part}", columns(w_down[part * FF_PART:(part + 1) * FF_PART, :], 0))
            sp.wait_ge(norm_sums, 3)
            sp.dma_start(pos_i[:, :], a["positions_2"]).then_inc(misc_in, 16)
            sp.dma_start(cmp_w2[:, :, :, :], a["cmp_w2_2"].rearrange("i (k p) d -> p i k d", p=P)).then_inc(misc_in, 16)
            stream("pool_in", columns(a["a_w_in_2"].rearrange("l k n -> (l k) n"), 0))
            w_pool = a["a_w_pool_2"].rearrange("l g (k p) n -> p (l g) k n", p=P)
            stream("pool_mix", lambda n, j: w_pool[:, j, :, :])
            w_out2 = a["w_out_2"].rearrange("l k n -> (l k) n")
            stream("out0", columns(w_out2[0:D, :], 0))
            w_kv = a["w_kv_2"]
            stream("cmp_kv", columns(w_kv, 0))
            stream("sel_k", columns(w_kv, 1024))
            stream("sel_v", columns(w_kv, 1536))
            stream("win_k", columns(w_kv, 2048))
            stream("win_v", columns(w_kv, 2560))
            w1 = a["cmp_w1_2"].rearrange("i (l p) n -> p i l n", p=P)
            stream("cmp_hid_k", lambda n, j: w1[:, 0, 8 * j:8 * j + 8, :])
            stream("cmp_hid_v", lambda n, j: w1[:, 1, 8 * j:8 * j + 8, :])
            w_b = a["b_w_in_2"].rearrange("l k n -> (l k) n")
            w_b3 = w_b.rearrange("(k p) n -> p k n", p=P)
            stream("nsa_q", columns(w_b, 0))
            stream("nsa_gate", lambda n, j: w_b3[:, 4 * j:4 * j + 4, 1536:1572])
            stream("nsa_zq", columns(w_b, 1572))
            stream("nsa_qm", columns(w_b, 3108))
            stream("nsa_zm", columns(w_b, 3620))
            stream("out1", columns(w_out2[D:2 * D, :], 0))
            sp.wait_ge(final_kept, 8)
            sp.dma_start(a["out"].rearrange("a (h p) n -> p (a h) n", p=P), tokens).then_inc(out_stored, 16)
            sp.wait_ge(out_stored, 16)

        @block.gpsimd
        def _(pool):
            count = [0]

            def then(ins):
                count[0] += 1
                ins.then_inc(pool_order, 1)
                pool.wait_ge(pool_order, count[0])

            def select(out, pattern, base, per_row, op=ALU.is_ge, fill=0.0):
                then(pool.affine_select(out=out, in_=out, compare_op=op, fill=fill, base=base,
                                        pattern=pattern, channel_multiplier=per_row))

            then(pool.memset(ident[:, :], 0.0))
            select(ident[:, :], [[-1, P]], 0, 1, ALU.not_equal, 1.0)
            pool.memset(ones[:, :], 1.0)
            pool.memset(eps_col[:, 0:1], EPS)
            pool.memset(eps_col[:, 1:2], 1.5707963267948966)
            pool.memset(eps_col[:, 2:3], 0.0).then_inc(consts_ready, 1)
            then(pool.memset(causal[:, :, :], 0.0))
            select(causal[:, :, :], [[P, TH], [-1, T]], 0, 1, fill=NEG)
            then(pool.memset(cmp_mask[:, :, :], 0.0))
            select(cmp_mask[:, :, :], [[P, TH], [-CMP_STRIDE, 16]], 1 - CMP_LEN, 1, fill=NEG)
            then(pool.memset(swap[:, :], 0.0))
            select(swap[:, :], [[-1, ROT]], -ROT // 2, 1, ALU.not_equal, -1.0)
            select(swap[:, :], [[-1, ROT]], ROT // 2, 1, ALU.not_equal, 1.0)
            for j in range(ROT):
                last = pool.memset(inv_row[:, j:j + 1], float(ROPE_THETA ** (-(j % (ROT // 2)) * 2.0 / ROT)))
            last.then_inc(consts_ready, 1)
            pool.wait_ge(norm_sums, 1)
            then(pool.memset(level_mask[:, :, :], 1.0))
            for n, w in enumerate(LEVELS):
                v = level_mask[:, n, :].rearrange("p (b w) -> p b w", w=w)
                select(v, [[-2 * w, CHUNK_T // w], [0, w]], 0, 1)
                select(v, [[2 * w, CHUNK_T // w], [0, w]], w - 1, -1)
            then(pool.memset(hg_reset, 1.0))
            v = hg_reset.rearrange("p (c t) -> p c t", t=CHUNK_T)
            pool.memset(v[:, :, 0], 0.0).then_inc(consts_ready, 1)

            def low_parts(name):
                g = PLAN[name]

                def block_of(b, more):
                    for u in range(8):
                        r0, rows = g.unit(u)
                        n = rows * g.width
                        pool.wait_ge(high_ready, 8 * b + u + 1 + more)
                        pool.tensor_tensor(w_low[:, u % UNITS, 0:n], ring[:, u // 2, r0 * g.width:r0 * g.width + n],
                                           w_high[:, u % UNITS, 0:n], ALU.subtract).then_inc(low_ready, 1)

                if g.blocks < 3:
                    for n in range(g.blocks):
                        block_of(g.b0 + n, 0)
                else:
                    with pool.Fori(0, g.blocks) as i:
                        block_of(g.b0, i * 8)

            for name in PLAN:
                low_parts(name)

        @block.tensor
        def _(pe):
            def group_free(g, more=0):
                if g >= 2:
                    pe.wait_ge(evacuated, g - 1 + more)

            def parts(u, g):
                rows = g.unit(u)[1]
                return (w[:, u % UNITS, 0:rows * g.width].rearrange("p (k n) -> p k n", k=rows)
                        for w in (w_high, w_low))

            def accumulate(out, w, x, start, stop, tokens_first=False):
                (wh, wl), (xh, xl) = w, x
                for n, (a_, b_) in enumerate(((wh, xh), (wh, xl), (wl, xh))):
                    lhs, rhs = (b_, a_) if tokens_first else (a_, b_)
                    mm = pe.matmul(out, lhs, rhs, start=start and n == 0, stop=stop and n == 2,
                                   skip_group_check=True)
                return mm

            def features_unit(g, b, u, pair, x, first, of, more=0):
                pe.wait_ge(low_ready, 8 * b + u + 1 + more)
                wh, wl = parts(u, g)
                r0, rows = g.unit(u)
                for k in range(rows):
                    kt = first + r0 + k
                    for f in range(g.width // P):
                        cols = slice(f * P, f * P + P)
                        mm = accumulate(pair[f // 2][:, (f % 2) * T:(f % 2) * T + T],
                                        (wh[:, k, cols], wl[:, k, cols]), x(kt),
                                        start=(kt == 0 and f % 2 == 0), stop=(kt == of - 1))
                mm.then_inc(units_used, 1)

            def tokens_unit(g, b, u, pair, x, first, of, more=0):
                pe.wait_ge(low_ready, 8 * b + u + 1 + more)
                wh, wl = parts(u, g)
                r0, rows = g.unit(u)
                for k in range(rows):
                    kt = first + r0 + k
                    xh, xl = x(kt)
                    for h in range(TH):
                        t = slice(h * P, h * P + P)
                        mm = accumulate(pair[h][:, 0:g.width], (wh[:, k, :], wl[:, k, :]), (xh[:, t], xl[:, t]),
                                        start=(kt == 0), stop=(kt == of - 1), tokens_first=True)
                mm.then_inc(units_used, 1)

            def pair_of(g):
                return bank[2 * (g % 2)], bank[2 * (g % 2) + 1]

            def product(name, unit, x, made=None):
                g = PLAN[name]

                def block_of(n, more, more_groups, wait):
                    group_free(g.g0 + n, more_groups)
                    for u in range(8):
                        if wait and u % 2 == 0:
                            pe.wait_ge(x_ready, made + u // 2 + 1)
                        unit(g, g.b0 + n, u, pair_of(g.g0 + n), x, 4 * (u // 2), KT, more)

                peel = g.blocks if g.blocks < 4 else (2 if g.b0 == 0 else 0)
                for n in range(peel):
                    block_of(n, 0, 0, made is not None and n == 0)
                if peel < g.blocks:
                    if peel == 0 and made is not None:
                        pe.wait_ge(x_ready, made + 4)
                    with pe.Fori(0, (g.blocks - peel) // 2) as i:
                        for q in range(2):
                            block_of(peel + q, i * 16, i * 2, False)

            operand = lambda kt: (x_high[:, kt, :], x_low[:, kt, :])
            hidden_tile = lambda kt: (hidden[:, 0, kt, :], hidden[:, 1, kt, :])

            pe.wait_ge(consts_ready, 1)
            pe.wait_ge(gains_in, 16 * 16)
            pe.transpose(bank[4][:, 0:P], gain_rows[:, 0, :], ident[:, :])
            pe.transpose(bank[4][:, P:P + 65], gain_rows[0:65, 1, :], ident[0:65, 0:65])
            pe.transpose(bank[4][:, 2 * P:2 * P + 64], gain_rows[0:64, 2, :], ident[0:64, 0:64])\
              .then_inc(gains_turned, 1)

            turned = [0]

            def turn_rows():
                for n in range(KT // 2):
                    m = turned[0]
                    if m >= 3:
                        pe.wait_ge(rows_kept, m - 2)
                    for c in range(2):
                        for h in range(TH):
                            mm = pe.transpose(bank[5 + m % 3][:, c * T + h * P:c * T + h * P + P],
                                              tokens[:, h, (2 * n + c) * P:(2 * n + c) * P + P], ident[:, :])
                    mm.then_inc(rows_turned, 1)
                    turned[0] += 1

            pe.wait_ge(tokens_in, 16)
            turn_rows()

            normed = [0]

            def norm_sum():
                n = normed[0]
                for c in range(4):
                    pe.wait_ge(norm_squares, 4 * n + c + 1)
                    for k in range(4):
                        kt = 4 * c + k
                        mm = pe.matmul(bank[4][:, 0:T], ones[:, :], scratch[:, kt * T:kt * T + T],
                                       start=(kt == 0), stop=(kt == KT - 1))
                mm.then_inc(norm_sums, 1)
                normed[0] += 1

            def head_sum(pairs):
                for n in pairs:
                    pe.wait_ge(head_squares, n + 1)
                    if n >= 2:
                        pe.wait_ge(head_root, n - 1)
                    pe.matmul(bank[4 + n % 2][:, :], ones[:, :], head_sq[:, n % 2, :], start=True, stop=True)\
                      .then_inc(head_sums, 1)

            def scores(n):
                it = items[n]
                if n >= 2:
                    pe.wait_ge(exp_ready, n - 1)
                for h in range(TH):
                    w = it.widths[h]
                    mm = pe.matmul(bank[4 + n % 2][:, h * T:h * T + w], it.q[:, h * P:h * P + P],
                                   it.k[:, 0:w], start=True, stop=True)
                mm.then_inc(scores_ready, 1)

            def turned_col(s, h):
                return P + h * P if s == 0 else (0 if h == 0 else 3 * P)

            def turn_probs(n):
                it = items[n]
                pe.wait_ge(probs_ready, n + 1)
                if n >= 1:
                    pe.wait_ge(turned_kept, n)
                for h in range(TH):
                    for s in range(TH):
                        w = min(P, it.widths[h] - s * P)
                        if w > 0:
                            c = turned_col(s, h)
                            mm = pe.transpose(bank[6][0:w, c:c + P], probs[:, n % 2, h, s * P:s * P + w],
                                              ident[:, :])
                mm.then_inc(probs_turned, 1)

            def weigh_values(n):
                it = items[n]
                g = outs_before[n]
                pe.wait_ge(turned_kept, n + 1)
                if it.first and g:
                    pe.wait_ge(out_kept, g)
                o = bank[7][:, 0:T]
                pT = probsT[:, n % 2, :]
                if it.widths == CMP:
                    mm = pe.matmul(o, it.v[0:N_CMP, :], pT[0:N_CMP, P:3 * P], start=it.first, stop=it.last,
                                   skip_group_check=True)
                else:
                    pe.matmul(o, it.v[:, 0, :], pT[:, P:3 * P], start=it.first, stop=False, skip_group_check=True)
                    if it.widths == FULL:
                        pe.matmul(o[:, 0:P], it.v[:, 1, :], pT[:, 0:P], start=False, stop=False,
                                  skip_group_check=True)
                    mm = pe.matmul(o[:, P:T], it.v[:, 1, :], pT[:, 3 * P:4 * P], start=False, stop=it.last,
                                   skip_group_check=True)
                mm.then_inc(values_summed, 1)

            def attend(which):
                first, end = which[0], which[-1] + 1
                for n in range(first, end + 2):
                    if n < end:
                        scores(n)
                    if first <= n - 1 < end:
                        turn_probs(n - 1)
                    if first <= n - 2 < end:
                        weigh_values(n - 2)

            norm_sum()
            product("hgrn_qf", features_unit, operand, made=x_made["mix"])
            product("hgrn_v", tokens_unit, operand)

            def hgrn_step(s, more):
                pe.wait_ge(hg_operands, s + 1 + more)
                pe.wait_ge(hg_placed, max(s, 1) + more)
                b = bank[4 + s % 2]
                if s < len(LEVELS):
                    for t in range(4):
                        mm = pe.matmul(b[:, t * CHUNK_T:t * CHUNK_T + CHUNK_T], hg_keys[:, t * P:t * P + P],
                                       hg_queries[:, t * CHUNK_T:t * CHUNK_T + CHUNK_T], start=True, stop=True)
                elif s == len(LEVELS):
                    for t in range(4):
                        mm = pe.matmul(b[:, t * P:t * P + P], hg_keys[:, t * P:t * P + P],
                                       hg_queries[:, t * P:t * P + P], start=True, stop=True)
                else:
                    for h in range(2):
                        mm = pe.matmul(b[:, h * P:h * P + P], hg_keys[:, h * T:h * T + P],
                                       hg_queries[:, h * P:h * P + P], start=True, stop=True)
                mm.then_inc(hg_scores, 1)

            g = PLAN["gate_q_k"]
            with pe.Fori(0, 4) as i:
                for q in range(2):
                    group_free(g.g0 + q, i * 2)
                    for u in range(8):
                        features_unit(g, g.b0 + q, u, pair_of(g.g0 + q), operand, 4 * (u // 2), KT, i * 16)
                        if u % 2:
                            hgrn_step(4 * q + u // 2, i * STEPS)
                hgrn_step(8, i * STEPS)

            g = PLAN["idx_tail"]
            group_free(g.g0)
            for u in range(8):
                tokens_unit(g, g.b0, u, pair_of(g.g0), operand, 4 * (u // 2), KT)
            pe.wait_ge(hg_placed, 4 * STEPS + 1)
            for m in range(4):
                if m >= 2:
                    pe.wait_ge(hg_done, m - 1)
                for h in range(2):
                    o = bank[6 + m % 2][:, h * T:h * T + T]
                    n = 2 * m + h
                    v = hgrn_v[:, :, n * HD:n * HD + HD]
                    pe.matmul(o[:, 0:P], v[:, 0, :], hg_diag[:, 2 * n, :], start=(h == 0), stop=False,
                              skip_group_check=True)
                    pe.matmul(o[:, P:T], v[:, 1, :], hg_diag[:, 2 * n + 1, :], start=False, stop=False,
                              skip_group_check=True)
                    mm = pe.matmul(o[:, P:T], v[:, 0, :], hg_cross[:, n, :], start=False, stop=True,
                                   skip_group_check=True)
                mm.then_inc(hg_out, 1)
                pe.wait_ge(hg_square, m + 1)
                if m:
                    pe.wait_ge(hg_root, m)
                pe.matmul(bank[5][:, :], ones[:, :], hg_osq, start=True, stop=True).then_inc(hg_sum, 1)

            pe.wait_ge(idx_keys, 1)
            for h in range(TH):
                mm = pe.transpose(bank[4][0:64, h * P:h * P + P], idx_rows[:, h, 0:64], ident[:, :])
            mm.then_inc(idx_turned, 1)
            pe.wait_ge(idx_keys, 2)
            pe.wait_ge(hg_root, 4)
            for n in range(IDX_HEADS):
                if n >= 2:
                    pe.wait_ge(idx_relu, n - 1)
                r = slice(64 * (n % 2), 64 * (n % 2) + 64)
                q = proj[:, 40 + n // 2, :]
                pe.matmul(bank[4 + n % 2][:, 0:P], q[r, 0:P], ikT[r, 0:P], start=True, stop=True)
                pe.matmul(bank[4 + n % 2][:, P:P + T], q[r, P:T], ikT[r, :], start=True, stop=True)\
                  .then_inc(idx_logits, 1)
            product("attn_v", tokens_unit, operand)
            pe.wait_ge(idx_relu, IDX_HEADS)
            head_sum(MIX_PAIRS)
            pe.wait_ge(head_normed, 8)
            attend(DSA)
            for n, (name, k, v) in enumerate((("cross_mem", "cross_k", "cross_v"), ("mem0", "mem_k0", "mem_v0"),
                                              ("mem1", "mem_k1", "mem_v1"))):
                pe.wait_ge(rows_scaled, min(n, 1) + 1)
                turn_rows()
                product(k, features_unit, operand, made=x_made[name])
                product(v, tokens_unit, operand)
            product("mix_out", features_unit, operand, made=x_made["mix_y"])

            norm_sum()
            product("cross_q", features_unit, operand, made=x_made["cross"])
            head_sum(CROSS_PAIRS)
            pe.wait_ge(head_normed, 12)
            attend(CROSS)
            g = PLAN["cross_out"]
            pe.wait_ge(x_ready, x_made["cross_y"] + 1)
            for u in range(8):
                if u % 2 == 0:
                    group_free(g.g0 + u // 2)
                features_unit(g, g.b0, u, pair_of(g.g0 + u // 2), operand, 0, 4)

            norm_sum()
            for part in range(4):
                product(f"up{part}", features_unit, operand, made=x_made["mlp"] if part == 0 else None)
                pe.wait_ge(hidden_ready, 4 * (part + 1) + 1)
                product(f"down{part}", features_unit, hidden_tile)

            norm_sum()
            product("pool_in", features_unit, operand, made=x_made["pool"])
            g = PLAN["pool_mix"]
            for u in range(8):
                j = u // 2
                if u % 2 == 0:
                    group_free(g.g0 + j)
                    pe.wait_ge(x_ready, x_made["pooled"] + j + 1)
                features_unit(g, g.b0, u, pair_of(g.g0 + j),
                              lambda kt: (x_high[:, 3 * j + kt, :], x_low[:, 3 * j + kt, :]), 0, 3)
            attend(MEM0)
            product("out0", features_unit, operand, made=x_made["pool_y"])

            norm_sum()
            product("cmp_kv", features_unit, operand, made=x_made["kv"])
            product("sel_k", features_unit, operand)
            product("sel_v", tokens_unit, operand)
            product("win_k", features_unit, operand)
            product("win_v", tokens_unit, operand)
            pe.wait_ge(rope_pos, 1)
            pe.matmul(bank[5][0:ROT, 0:T], ones[0:1, 0:ROT], rstd[0:1, 0, 0:T], start=True, stop=True)
            pe.matmul(bank[6][0:ROT, 0:2], inv_row[0:1, :], ones[0:1, 0:2], start=True, stop=True)\
              .then_inc(rope_pos, 1)

            swaps = [0]

            def swap_halves(x, width):
                n = swaps[0]
                if n >= 2:
                    pe.wait_ge(rope_done, n - 1)
                pe.matmul(bank[5 + n % 2][0:ROT, 0:width], swap[:, :], x, start=True, stop=True)\
                  .then_inc(rope_swapped, 1)
                swaps[0] += 1

            pe.wait_ge(rope_tables, 1)
            pe.wait_ge(evacuated, PLAN["win_v"].g0)
            for t in (8, 10, 16, 18):
                swap_halves(proj[0:ROT, t:t + 2, :], 2 * T)
            for c, name in enumerate(("cmp_hid_k", "cmp_hid_v")):
                g = PLAN[name]
                group_free(g.g0)
                pe.wait_ge(x_ready, x_made["blocks"] + c + 1)
                hid = bank[2 * (g.g0 % 2)]
                for u in range(8):
                    pe.wait_ge(low_ready, 8 * g.b0 + u + 1)
                    wh, wl = parts(u, g)
                    for k in range(4):
                        l = 4 * u + k
                        for m in range(2):
                            cols = slice(m * P, m * P + P)
                            mm = accumulate(hid[:, m * 64:m * 64 + 4 * N_CMP], (wh[:, k, cols], wl[:, k, cols]),
                                            (zpe(x_high, c)[:, l, :], zpe(x_low, c)[:, l, :]),
                                            start=(l == 0 and m == 0), stop=(l == CMP_LEN - 1))
                    mm.then_inc(units_used, 1)
            pe.wait_ge(evacuated, PLAN["nsa_q"].g0)
            pe.wait_ge(rope_done, 4)
            for m in range(2):
                pe.matmul(bank[7][:, 0:4 * N_CMP], cmp_w2[:, 0, m, :], hidT[:, 0, m, :], start=(m == 0), stop=(m == 1))
            for kv in range(4):
                for m in range(2):
                    mm = pe.matmul(bank[5][0:N_CMP, kv * P:kv * P + P],
                                   hidT[:, 1, m, kv * N_CMP:kv * N_CMP + N_CMP], cmp_w2[:, 1, m, :],
                                   start=(kv == 0 and m == 0), stop=(m == 1), skip_group_check=True)
            mm.then_inc(cmp_second, 1)
            pe.wait_ge(cmp_ready, 1)
            swap_halves(kcmpT[0:ROT, 0:4 * N_CMP], 4 * N_CMP)
            norm_sum()
            product("nsa_q", features_unit, operand, made=x_made["nsa"])
            g = PLAN["nsa_gate"]
            group_free(g.g0)
            for u in range(8):
                tokens_unit(g, g.b0, u, pair_of(g.g0), operand, 4 * (u // 2), KT)
            product("nsa_zq", features_unit, operand)
            product("nsa_qm", features_unit, operand)
            product("nsa_zm", features_unit, operand)
            pe.wait_ge(evacuated, PLAN["nsa_gate"].g0)
            for t in range(24, 36, 2):
                swap_halves(proj[0:ROT, t:t + 2, :], 2 * T)
            pe.wait_ge(rope_done, len(ROPE_TURNS))
            pe.wait_ge(evacuated, PLAN["out1"].g0)
            attend(NSA)
            attend(MEM1)
            product("out1", features_unit, operand, made=x_made["nsa_y"])
            norm_sum()
            for n in range(8):
                pe.wait_ge(out_ready, n // 2 + 1)
                if n >= 2:
                    pe.wait_ge(final_kept, n - 1)
                h, c = n % 2, n // 2
                for k in range(4):
                    mm = pe.transpose(bank[5 + n % 2][:, k * P:k * P + P], proj[:, 4 * c + k, h * P:h * P + P],
                                      ident[:, :])
                mm.then_inc(final_turned, 1)

        @block.scalar
        def _(act):
            count = [0]

            def then(ins):
                count[0] += 1
                ins.then_inc(act_order, 1)
                act.wait_ge(act_order, count[0])

            made = [0]
            gemm_of = {b: g for g in PLAN.values() for b in range(g.b0, g.b0 + g.blocks)}
            last_unit = 8 * len(gemm_of)

            def high_unit(g, b, u, more=0):
                r0, rows = g.unit(u)
                n = rows * g.width
                if u % 2 == 0:
                    act.wait_ge(landed[u // 2], 16 * (b + 1) + 2 * more)
                if 8 * b + u >= UNITS:
                    act.wait_ge(units_used, 8 * b + u + 1 - UNITS + more)
                act.activation(w_high[:, u % UNITS, 0:n], ring[:, u // 2, r0 * g.width:r0 * g.width + n], ACT.Copy)\
                   .then_inc(high_ready, 1)

            def high(count):
                for k in range(made[0], min(made[0] + count, last_unit)):
                    high_unit(gemm_of[k // 8], k // 8, k % 8)
                made[0] += count

            def high_parts(name):
                g = PLAN[name]
                turns = g.blocks - 1
                if turns >= 3:
                    with act.Fori(0, turns) as i:
                        for u in range(4, 12):
                            high_unit(g, g.b0 + u // 8, u % 8, i * 8)
                    made[0] += 8 * turns
                else:
                    high(8 * turns)
                high(8)

            normed = [0]

            def norm_squares_and_root():
                n = normed[0]
                for c in range(4):
                    act.activation(scratch[:, c * 1024:c * 1024 + 1024],
                                   hT[:, 4 * c:4 * c + 4, :].rearrange("p a t -> p (a t)"), ACT.Square)\
                       .then_inc(norm_squares, 1)
                act.wait_ge(norm_sums, n + 1)
                act.activation(rstd[:, 0, 0:T], bank[4][:, 0:T], ACT.Sqrt, scale=1.0 / D, bias=eps_col[:, 0:1])\
                   .then_inc(norm_root, 1)
                normed[0] += 1

            def row_squares(n):
                act.wait_ge(tokens_in, 16 * (n + 2))
                then(act.activation(heads_scratch[:, 0:D], tokens[:, 0, :], ACT.Square, accum_out=tok_rstd[:, 0:1]))
                act.activation(heads_scratch[:, 0:D], tokens[:, 1, :], ACT.Square,
                               accum_out=tok_rstd[:, 1:2]).then_inc(rows_squared, 1)
                act.wait_ge(rows_squared, 2 * n + 1)
                act.activation(tok_rstd[:, 2:4], tok_rstd[:, 0:2], ACT.Sqrt, scale=1.0 / D, bias=eps_col[:, 0:1])\
                   .then_inc(rows_squared, 1)

            def head_norms(pairs):
                first, end = pairs[0], pairs[-1] + 1
                for n in range(first, end + 1):
                    if n < end:
                        if n >= 2:
                            act.wait_ge(head_sums, n - 1)
                        act.activation(head_sq[:, n % 2, :], pair_tile(norm_pairs[n][0]), ACT.Square)\
                           .then_inc(head_squares, 1)
                    if n > first:
                        m = n - 1
                        act.wait_ge(head_sums, m + 1)
                        if m >= 2:
                            act.wait_ge(head_normed, m - 1)
                        act.activation(rstd[:, m % 2, :], bank[4 + m % 2][:, :], ACT.Sqrt, scale=1.0 / HD,
                                       bias=eps_col[:, 0:1]).then_inc(head_root, 1)

            def exps(n):
                it = items[n]
                act.wait_ge(max_ready, n + 1)
                if n >= 2:
                    act.wait_ge(probs_turned, n - 1)
                for h in range(TH):
                    w = it.widths[h]
                    src = bank[4 + n % 2][:, h * T:h * T + w] if it.mask is None else masked_scores[:, n % 2, h, 0:w]
                    last = act.activation(probs[:, n % 2, h, 0:w], src, ACT.Exp, scale=ATT_SCALE,
                                          bias=stats[:, n % 2, 2 + h:3 + h], accum_out=stats[:, n % 2, 4 + h:5 + h])
                last.then_inc(exp_ready, 1)

            def keep_turned(n):
                it = items[n]
                act.wait_ge(probs_turned, n + 1)
                if n >= 2:
                    act.wait_ge(values_summed, n - 1)
                r = N_CMP if it.widths == CMP else P
                c = slice(P, 3 * P) if it.widths == CMP else (slice(P, 4 * P) if it.widths == CAUSAL else slice(0, 4 * P))
                act.activation(probsT[0:r, n % 2, c], bank[6][0:r, c], ACT.Copy).then_inc(turned_kept, 1)

            def attend(which):
                first, end = which[0], which[-1] + 1
                for n in range(first, end + 1):
                    if n < end:
                        exps(n)
                    if n > first:
                        keep_turned(n - 1)

            high(UNITS)
            act.wait_ge(rows_kept, 8)
            norm_squares_and_root()
            act.wait_ge(hg_dve, 1)
            act.activation(lower[:, 0:8], lower[:, 8:16], ACT.Sigmoid).then_inc(hg_act, 1)
            high_parts("hgrn_qf")
            high_parts("hgrn_v")
            act.wait_ge(evacuated, PLAN["hgrn_v"].g0)
            for hg in range(4):
                qs, fs = hg_tiles(hg)
                act.activation(fs, fs, ACT.Sigmoid).then_inc(hg_act, 1)
                act.wait_ge(hg_dve, 3 * hg + 1)
                act.activation(hg_tmp, qs, ACT.Sigmoid).then_inc(hg_act, 1)
                act.wait_ge(hg_dve, 3 * hg + 2)
                act.activation(hg_logf, fs, ACT.Ln).then_inc(hg_act, 1)
                for s in range(STEPS):
                    if s != len(LEVELS):
                        act.wait_ge(hg_exp, exps_before(hg, s) + 1)
                        act.activation(hg_decay, hg_decay, ACT.Exp).then_inc(hg_exp, 1)
                    if s < 8:
                        high(2)
            high_parts("idx_tail")
            act.wait_ge(evacuated, PLAN["gate_q_k"].g0 + 2)
            for t in (16, 20):
                act.activation(pair_tile(t, 4), pair_tile(t, 4), ACT.Silu).then_inc(hg_act, 1)
            for m in range(4):
                act.wait_ge(hg_out, m + 1)
                if m:
                    act.wait_ge(hg_sum, m)
                act.activation(hg_osq, bank[6 + m % 2][:, :], ACT.Square).then_inc(hg_square, 1)
                act.wait_ge(hg_sum, m + 1)
                if m:
                    act.wait_ge(hg_done, m)
                act.activation(rstd[:, 0, :], bank[5][:, :], ACT.Sqrt, scale=1.0 / HD, bias=eps_col[:, 0:1])\
                   .then_inc(hg_root, 1)

            for n in range(IDX_HEADS):
                act.wait_ge(idx_logits, n + 1)
                if n >= 2:
                    act.wait_ge(idx_added, n - 1)
                act.activation(idx_relus[:, n % 2, :], bank[4 + n % 2][:, 0:3 * P], ACT.Relu).then_inc(idx_relu, 1)
            high_parts("attn_v")
            head_norms(MIX_PAIRS)
            attend(DSA)
            act.wait_ge(out_kept, outs_before[8])
            row_squares(0)
            high_parts("cross_k")
            row_squares(1)
            for name in ("cross_v", "mem_k0", "mem_v0", "mem_k1", "mem_v1", "mix_out"):
                high_parts(name)

            act.wait_ge(evacuated, PLAN["cross_q"].g0)
            norm_squares_and_root()
            high_parts("cross_q")
            act.wait_ge(evacuated, PLAN["cross_out"].g0)
            head_norms(CROSS_PAIRS)
            attend(CROSS)
            high_parts("cross_out")

            act.wait_ge(evacuated, PLAN["up0"].g0)
            norm_squares_and_root()
            for part in range(4):
                high_parts(f"up{part}")
                high_parts(f"down{part}")

            act.wait_ge(evacuated, PLAN["pool_in"].g0)
            norm_squares_and_root()
            high_parts("pool_in")
            act.wait_ge(evacuated, PLAN["pool_mix"].g0)
            for t in (12, 16, 20, 28):
                act.activation(pair_tile(t, 4), pair_tile(t, 4), ACT.Silu).then_inc(silu_ready, 1)
            high_parts("pool_mix")
            attend(MEM0)
            high_parts("out0")

            act.wait_ge(evacuated, PLAN["cmp_kv"].g0)
            norm_squares_and_root()
            for name in ("cmp_kv", "sel_k", "sel_v", "win_k", "win_v"):
                high_parts(name)
            act.wait_ge(rope_angle, 1)
            act.activation(rope_s[:, :], rope_s[:, :], ACT.Sin).then_inc(rope_sin, 1)
            act.activation(rope_c[:, :], rope_c[:, :], ACT.Sin, scale=-1.0, bias=eps_col[0:ROT, 1:2]).then_inc(rope_sin, 1)
            for c, name in enumerate(("cmp_hid_k", "cmp_hid_v")):
                high_parts(name)
                g = PLAN[name].g0
                act.wait_ge(units_used, PLAN[name].made())
                for m in range(2):
                    last = act.activation(hidT[:, c, m, :], bank[2 * (g % 2)][:, m * 64:m * 64 + 4 * N_CMP], ACT.Silu)
                last.then_inc(hid_act, 1)
            act.wait_ge(rope_done, 5)
            norm_squares_and_root()
            for name in ("nsa_q", "nsa_gate", "nsa_zq", "nsa_qm", "nsa_zm"):
                high_parts(name)
            act.wait_ge(evacuated, PLAN["out1"].g0)
            for t in (36, 40, 44, 52):
                act.activation(pair_tile(t, 4), pair_tile(t, 4), ACT.Silu).then_inc(silu_ready, 1)
            gates = nsa_gates[:, :, :].rearrange("p h n -> p (h n)")
            act.activation(gates, gates, ACT.Sigmoid).then_inc(silu_ready, 1)
            attend(NSA)
            attend(MEM1)
            high_parts("out1")
            act.wait_ge(evacuated, PLAN["out1"].g0 + 4)
            norm_squares_and_root()

        @block.vector
        def _(dve):
            count = [0]

            def then(ins):
                count[0] += 1
                ins.then_inc(dve_order, 1)
                dve.wait_ge(dve_order, count[0])

            def read_out(g, q, i, dst):
                n = g.g0 + q
                dve.wait_ge(units_used, i * (2 * g.units) + g.made(q))
                for c in range(2):
                    last = dve.tensor_copy(dst(i * 2 + q, c), bank[2 * (n % 2) + c][:, :])
                last.then_inc(evacuated, 1)

            def keep(name, dst):
                g = PLAN[name]
                if g.groups < 4:
                    for n in range(g.groups):
                        read_out(g, n, 0, dst)
                else:
                    with dve.Fori(0, g.groups // 2) as i:
                        for q in range(2):
                            read_out(g, q, i, dst)

            def tiles(t0):
                return lambda n, c: proj[:, bass.ds(n * 4 + (t0 + 2 * c), 2), :].rearrange("p a t -> p (a t)")

            def rows(v):
                return lambda n, c: v[:, c, bass.ds(n * 512, 512)]

            def residual(name):
                g = PLAN[name]
                dve.wait_ge(evacuated, g.g0)
                with dve.Fori(0, 2) as i:
                    for q in range(2):
                        n = g.g0 + q
                        dve.wait_ge(units_used, i * (2 * g.units) + g.made(q))
                        for c in range(2):
                            h = hT[:, bass.ds(i * 8 + (4 * q + 2 * c), 2), :].rearrange("p a t -> p (a t)")
                            last = dve.tensor_tensor(h, bank[2 * (n % 2) + c][:, :], h, ALU.add)
                        last.then_inc(evacuated, 1)

            def flat(x, t, n):
                return x[:, t:t + n, :].rearrange("p a t -> p (a t)")

            def split(src, high, low):
                then(dve.tensor_copy(high, src))
                return dve.tensor_tensor(low, src, high, ALU.subtract)

            def split_tiles(name, sources, n=4):
                for c, t in enumerate(sources):
                    split(pair_tile(t, n), flat(x_high, n * c, n), flat(x_low, n * c, n)).then_inc(x_ready, 1)

            normed = [0]

            def normed_tile(out, kt, slot, cols):
                return dve.scalar_tensor_tensor(out=out, in0=hT[:, kt, :],
                                                scalar=gains[:, slot, cols.start + kt:cols.start + kt + 1],
                                                in1=rstd[:, 1, 0:T], op0=ALU.mult, op1=ALU.mult)

            def norm(name, slot, cols):
                dve.wait_ge(norm_root, normed[0] + 1)
                then(dve.reciprocal(rstd[:, 1, 0:T], rstd[:, 0, 0:T]))
                for c in range(4):
                    tmp = heads_scratch[:, (c % 2) * 1024:(c % 2) * 1024 + 1024]
                    if c >= 2:
                        dve.wait_ge(x_ready, x_made[name] + c - 1)
                    for k in range(4):
                        last = normed_tile(tmp[:, k * T:k * T + T], 4 * c + k, slot, cols)
                    then(last)
                    split(tmp, flat(x_high, 4 * c, 4), flat(x_low, 4 * c, 4)).then_inc(x_ready, 1)
                normed[0] += 1
                dve.wait_ge(x_ready, x_made[name] + 4)

            def scale_rows(n):
                dve.wait_ge(rows_squared, 2 * n + 2)
                then(dve.reciprocal(tok_rstd[:, 4:6], tok_rstd[:, 2:4]))
                for h in range(TH):
                    last = dve.tensor_scalar(tokens[:, h, :], tokens[:, h, :], tok_rstd[:, 4 + h:5 + h], None, ALU.mult)
                last.then_inc(rows_scaled, 1)

            turned = [0]

            def keep_rows():
                for n in range(KT // 2):
                    m = turned[0]
                    dve.wait_ge(rows_turned, m + 1)
                    dve.tensor_copy(flat(hT, 2 * n, 2), bank[5 + m % 3][:, :]).then_inc(rows_kept, 1)
                    turned[0] += 1

            def operand_rows(name, cols):
                for n in range(KT // 2):
                    m = turned[0]
                    dve.wait_ge(rows_turned, m + 1)
                    srcs = [(2 * n + c, bank[5 + m % 3][:, c * T:c * T + T],
                             gains[:, 0, cols.start + 2 * n + c:cols.start + 2 * n + c + 1]) for c in range(2)]
                    for t, src, gain in srcs:
                        last = dve.tensor_scalar(x_high[:, t, :], src, gain, None, ALU.mult)
                    then(last)
                    for t, src, gain in srcs:
                        last = dve.scalar_tensor_tensor(out=x_low[:, t, :], in0=src, scalar=gain, in1=x_high[:, t, :],
                                                        op0=ALU.mult, op1=ALU.subtract)
                    last.then_inc(rows_kept, 1)
                    turned[0] += 1
                    if n % 2:
                        dve.wait_ge(rows_kept, turned[0])
                        dve.sem_inc(x_ready, 1)

            def head_norms(pairs):
                for n in pairs:
                    t, col = norm_pairs[n]
                    dve.wait_ge(head_root, n + 1)
                    then(dve.reciprocal(rstd[:, n % 2, :], rstd[:, n % 2, :]))
                    dve.scalar_tensor_tensor(out=pair_tile(t), in0=pair_tile(t), scalar=gains[:, 1, col:col + 1],
                                             in1=rstd[:, n % 2, :], op0=ALU.mult, op1=ALU.mult)\
                       .then_inc(head_normed, 1)

            def maxima(n):
                it = items[n]
                st = stats[:, n % 2, :]
                dve.wait_ge(scores_ready, n + 1)
                if n >= 2:
                    dve.wait_ge(exp_ready, n - 1)
                s = bank[4 + n % 2][:, :].rearrange("p (h s) -> p h s", h=TH)
                if it.mask is None:
                    last = dve.tensor_reduce(st[:, 0:2], s, AX, ALU.max)
                else:
                    for h in range(TH):
                        w = it.widths[h]
                        last = dve.tensor_tensor_reduce(masked_scores[:, n % 2, h, 0:w], s[:, h, 0:w],
                                                        it.mask[:, h, 0:w], 1.0, -3.4e38, ALU.add, ALU.max,
                                                        st[:, h:h + 1])
                then(last)
                dve.tensor_scalar(st[:, 2:4], st[:, 0:2], NEG / 8, -ATT_SCALE, ALU.max, ALU.mult)\
                   .then_inc(max_ready, 1)

            def normalise(n):
                it = items[n]
                st = stats[:, n % 2, :]
                dve.wait_ge(exp_ready, n + 1)
                sums = st[:, 4:6]
                if it.widths == CMP:
                    sums = st[:, 10:12]
                    then(dve.tensor_scalar(sums, st[:, 4:6], 1e-30, None, ALU.max))
                then(dve.reciprocal(st[:, 6:8], sums))
                if it.gate is not None:
                    then(dve.tensor_tensor(st[:, 6:8], st[:, 6:8], it.gate, ALU.mult))
                for h in range(TH):
                    w = it.widths[h]
                    p = probs[:, n % 2, h, 0:w]
                    last = dve.tensor_scalar(p, p, st[:, 6 + h:7 + h], None, ALU.mult)
                last.then_inc(probs_ready, 1)

            def keep_out(n):
                it = items[n]
                if not it.last:
                    return
                o = bank[7][:, 0:T]
                dve.wait_ge(values_summed, n + 1)
                if it.times is None:
                    last = dve.tensor_copy(it.out, o)
                else:
                    last = dve.tensor_tensor(it.out, o, it.times, ALU.mult)
                last.then_inc(out_kept, 1)

            def attend(which):
                first, end = which[0], which[-1] + 1
                for n in range(first, end + 2):
                    if n < end:
                        maxima(n)
                    if first <= n - 1 < end:
                        normalise(n - 1)
                    if first <= n - 2 < end:
                        keep_out(n - 2)
                dve.wait_ge(out_kept, outs_before[end])

            dve.wait_ge(gains_turned, 1)
            dve.tensor_copy(gains[:, 0, :], bank[4][:, 0:P])
            dve.tensor_copy(gains[:, 1, 0:65], bank[4][:, P:P + 65])
            dve.tensor_copy(pe_cols[:, :, :].rearrange("p i l -> p (i l)"), bank[4][:, 2 * P:2 * P + 64])\
               .then_inc(gains_ready, 1)
            keep_rows()
            dve.wait_ge(gains_ready, 1)
            lb0 = gains[:, 1, G_LB.start:G_LB.start + 8]
            lb1 = gains[:, 1, G_LB.start + 8:G_LB.start + 16]
            dve.tensor_tensor(lower[:, 8:16], lb0, lb1, ALU.subtract).then_inc(hg_dve, 1)
            norm("mix", 0, G_MIX)
            dve.wait_ge(hg_act, 1)
            dve.wait_ge(consts_ready, 3)
            then(dve.tensor_scalar(lower[:, 8:16], lower[:, 0:8], -1.0, 1.0, ALU.mult, ALU.add))
            dve.memset(hg_diag, 0.0).then_inc(hg_placed, 1)
            keep("hgrn_qf", tiles(0))
            keep("hgrn_v", rows(hgrn_v))
            dve.wait_ge(evacuated, PLAN["hgrn_v"].g0 + 2)

            def place(hg, s):
                dve.wait_ge(hg_placed, STEPS * hg + s + 1)
                dve.wait_ge(hg_scores, STEPS * hg + s + 1)
                diag = hg_diag[:, 4 * hg:4 * hg + 4, :]
                if s < len(LEVELS):
                    w = LEVELS[s]
                    out = diag.rearrange("p m (b two w) -> p m b two w", two=2, w=w)[:, :, :, 1, :]
                    mask = spread(level_mask[:, s:s + 1, :], 1, 4).rearrange("p m (b w) -> p m b w", w=w)
                    got = bank[4 + s % 2][:, 0:4 * CHUNK_T].rearrange("p (m b w) -> p m b w", m=4, w=w)
                    last = dve.copy_predicated(out, mask.bitcast(I32), got)
                elif s == len(LEVELS):
                    last = dve.copy_predicated(diag, spread(ident[:, :].rearrange("p (m t) -> p m t", m=1), 1, 4)
                                               .bitcast(I32), bank[5][:, :].rearrange("p (m t) -> p m t", m=4))
                else:
                    last = dve.tensor_copy(hg_cross[:, 2 * hg:2 * hg + 2, :].rearrange("p m t -> p (m t)"),
                                           bank[4][:, 0:T])
                last.then_inc(hg_placed, 1)

            for hg in range(4):
                qs, fs = hg_tiles(hg)
                dve.wait_ge(hg_act, 1 + 3 * hg + 1)
                for h in range(2):
                    f = fs[:, h * T:h * T + T]
                    c = 2 * hg + h
                    last = dve.tensor_scalar(f, f, lower[:, 8 + c:9 + c], lower[:, c:c + 1], ALU.mult, ALU.add)
                last.then_inc(hg_dve, 1)
                dve.wait_ge(hg_act, 1 + 3 * hg + 2)
                dve.scalar_tensor_tensor(out=qs, in0=qs, scalar=ATT_SCALE, in1=hg_tmp, op0=ALU.mult, op1=ALU.mult)\
                   .then_inc(hg_dve, 1)
                dve.wait_ge(hg_act, 1 + 3 * hg + 3)
                dve.tensor_scalar(fs, fs, -1.0, 1.0, ALU.mult, ALU.add).then_inc(hg_dve, 1)
                then(dve.tensor_tensor_scan(hg_cum, hg_reset, hg_logf, 0.0, ALU.mult, ALU.add))
                dve.wait_ge(hg_dve, 3 * hg + 4)

                for s in range(STEPS):
                    step = STEPS * hg + s
                    if step:
                        dve.wait_ge(hg_operands, step)
                    if s < len(LEVELS):
                        w = LEVELS[s]
                        cum = hg_cum.rearrange("p (b two w) -> p b two w", two=2, w=w)
                        dec = hg_decay.rearrange("p (b two w) -> p b two w", two=2, w=w)
                        mid = spread(cum[:, :, 0, w - 1:w], 2, w)
                        if w < CHUNK_T:
                            dve.tensor_tensor(dec[:, :, 1, :], cum[:, :, 1, :], mid, ALU.subtract)
                        else:
                            dve.tensor_copy(dec[:, :, 1, :], cum[:, :, 1, :])
                        dve.tensor_tensor(dec[:, :, 0, :], mid, cum[:, :, 0, :], ALU.subtract).then_inc(hg_exp, 1)
                    elif s > len(LEVELS):
                        cum = hg_cum.rearrange("p (h c t) -> p h c t", h=2, c=4)
                        dec = hg_decay.rearrange("p (h c t) -> p h c t", h=2, c=4)
                        total = lambda c: spread(cum[:, :, c, CHUNK_T - 1:CHUNK_T], 2, CHUNK_T)
                        dve.tensor_copy(dec[:, :, 2, :], cum[:, :, 2, :])
                        dve.tensor_tensor(dec[:, :, 3, :], cum[:, :, 3, :], total(2), ALU.add)
                        dve.tensor_tensor(dec[:, :, 1, :], total(1), cum[:, :, 1, :], ALU.subtract)
                        then(dve.tensor_tensor(dec[:, :, 0, :], total(0), cum[:, :, 0, :], ALU.subtract))
                        dve.tensor_tensor(dec[:, :, 0, :], dec[:, :, 0, :], total(1), ALU.add).then_inc(hg_exp, 1)
                    if s != len(LEVELS):
                        dve.wait_ge(hg_exp, exps_before(hg, s) + 2)
                    if step:
                        dve.wait_ge(hg_scores, step)
                    if s < len(LEVELS):
                        dve.tensor_tensor(hg_keys, fs, hg_decay, ALU.mult)
                        q4 = qs.rearrange("p (b two w) -> p b two w", two=2, w=w)
                        last = dve.tensor_tensor(hg_queries[:, 0:T].rearrange("p (b w) -> p b w", w=w), q4[:, :, 1, :],
                                                 dec[:, :, 1, :], ALU.mult)
                    elif s == len(LEVELS):
                        dve.tensor_copy(hg_keys, fs)
                        last = dve.tensor_copy(hg_queries, qs)
                    else:
                        halves = lambda x: x.rearrange("p (h c t) -> p h c t", h=2, c=2)
                        dve.tensor_tensor(halves(hg_keys)[:, :, 0, :], halves(fs)[:, :, 0, :],
                                          halves(hg_decay)[:, :, 0, :], ALU.mult)
                        last = dve.tensor_tensor(hg_queries[:, 0:T].rearrange("p (h t) -> p h t", h=2),
                                                 halves(qs)[:, :, 1, :], halves(hg_decay)[:, :, 1, :], ALU.mult)
                    last.then_inc(hg_operands, 1)
                    if s:
                        place(hg, s - 1)
                    if s in (4, 8):
                        read_out(PLAN["gate_q_k"], 2 * hg + (s == 8), 0, tiles(16))
                place(hg, STEPS - 1)
            g = PLAN["idx_tail"]
            dve.wait_ge(units_used, g.made())
            dve.wait_ge(hg_placed, 4 * STEPS + 1)
            pair = bank[2 * (g.g0 % 2)], bank[2 * (g.g0 % 2) + 1]
            for h in range(TH):
                last = dve.tensor_copy(idx_rows[:, h, 0:64], pair[h][:, 0:64])
            last.then_inc(idx_keys, 1)
            for h in range(TH):
                last = dve.tensor_scalar(idx_w[:, h, :], pair[h][:, 64:80], IDX_SCALE, None, ALU.mult)
            last.then_inc(evacuated, 1)
            dve.wait_ge(hg_act, 15)
            for m in range(4):
                if m:
                    dve.wait_ge(hg_done, m)
                dve.wait_ge(hg_root, m + 1)
                then(dve.reciprocal(rstd[:, 1, :], rstd[:, 0, :]))
                then(dve.scalar_tensor_tensor(out=hg_tmp, in0=bank[6 + m % 2][:, :],
                                              scalar=gains[:, 1, G_ONORM:G_ONORM + 1], in1=rstd[:, 1, :],
                                              op0=ALU.mult, op1=ALU.mult))
                dve.tensor_tensor(pair_tile(16 + 2 * m), hg_tmp, pair_tile(16 + 2 * m), ALU.mult).then_inc(hg_done, 1)
            dve.wait_ge(idx_turned, 1)
            dve.tensor_copy(ikT[0:64, :], bank[4][0:64, 0:T])
            dve.tensor_copy(ikT[64:128, :], bank[4][0:64, 0:T]).then_inc(idx_keys, 1)

            both = [(0, slice(0, P), P), (1, slice(P, P + T), T)]
            for n in range(IDX_HEADS):
                dve.wait_ge(idx_relu, n + 1)
                if n:
                    dve.wait_ge(idx_added, n)
                for h, c, w in both:
                    acc, r, wt = idx_score[:, h, 0:w], idx_relus[:, n % 2, c], idx_w[:, h, n:n + 1]
                    if n == 0:
                        last = dve.tensor_scalar(acc, r, wt, None, ALU.mult)
                    else:
                        last = dve.scalar_tensor_tensor(out=acc, in0=r, scalar=wt, in1=acc, op0=ALU.mult, op1=ALU.add)
                last.then_inc(idx_added, 1)
            dve.wait_ge(idx_added, IDX_HEADS)
            for h, c, w in both:
                acc, bias = idx_score[:, h, 0:w], sel_bias[:, h, 0:w]
                then(dve.tensor_tensor(acc, acc, causal[:, h, 0:w], ALU.add))
                for r in range(TOPK // 8):
                    then(dve.max(best[:, h, :], acc))
                    then(dve.match_replace(acc, best[:, h, :], acc, TAKEN))
                then(dve.tensor_scalar(bias, acc, TAKEN / 2, NEG, ALU.is_gt, ALU.mult))
                then(dve.tensor_tensor(bias, bias, causal[:, h, 0:w], ALU.min))
            dve.sem_inc(mask_ready, 1)
            keep("attn_v", rows(attn_v))
            head_norms(MIX_PAIRS)
            attend(DSA)
            scale_rows(0)
            operand_rows("cross_mem", G_MEM)
            keep("cross_k", tiles(8))
            scale_rows(1)
            keep("cross_v", rows(cross_v))
            operand_rows("mem0", G_M2A)
            keep("mem_k0", tiles(48))
            keep("mem_v0", rows(mem_v0))
            operand_rows("mem1", G_M2B)
            keep("mem_k1", tiles(56))
            keep("mem_v1", rows(mem_v1))
            split_tiles("mix_y", (16, 20, 24, 28))
            residual("mix_out")

            norm("cross", 0, G_CROSS)
            keep("cross_q", tiles(16))
            dve.wait_ge(evacuated, PLAN["cross_out"].g0)
            head_norms(CROSS_PAIRS)
            attend(CROSS)
            split_tiles("cross_y", (28,))
            residual("cross_out")

            norm("mlp", 0, G_MLP)
            squares = heads_scratch[:, 0:1024]
            dve.sem_inc(hidden_ready, 1)
            for part in range(4):
                g = PLAN[f"up{part}"]
                with dve.Fori(0, 2) as i:
                    for q in range(2):
                        n = g.g0 + q
                        dve.wait_ge(hidden_ready, i * 2 + (4 * part + q + 1))
                        dve.wait_ge(units_used, i * (2 * g.units) + g.made(q))
                        for c in range(2):
                            last = dve.tensor_scalar(squares[:, c * 512:c * 512 + 512], bank[2 * (n % 2) + c][:, :],
                                                     0.0, None, ALU.max)
                        last.then_inc(evacuated, 1)
                        dve.wait_ge(evacuated, i * 2 + (n + 1))
                        dve.tensor_tensor(squares, squares, squares, ALU.mult).then_inc(hidden_squared, 1)
                        dve.wait_ge(hidden_squared, i * 4 + (8 * part + 2 * q + 1))
                        high, low = (hidden[:, c, bass.ds(i * 8 + 4 * q, 4), :].rearrange("p a t -> p (a t)")
                                     for c in range(2))
                        dve.tensor_copy(high, squares).then_inc(hidden_squared, 1)
                        dve.wait_ge(hidden_squared, i * 4 + (8 * part + 2 * q + 2))
                        dve.tensor_tensor(low, squares, high, ALU.subtract).then_inc(hidden_ready, 1)
                residual(f"down{part}")

            norm("pool", 0, G_2A)
            count_t = pair_tile(43, 1)
            then(dve.memset(pair_tile(42, 1), 1.0))
            then(dve.tensor_tensor_scan(count_t, pair_tile(42, 1), pair_tile(42, 1), 0.0, ALU.mult, ALU.add))
            for n, win in enumerate(POOL_WINDOWS):
                then(dve.tensor_scalar(pair_tile(44 + n, 1), count_t, float(win), None, ALU.min))
                then(dve.reciprocal(pair_tile(44 + n, 1), pair_tile(44 + n, 1)))
            keep("pool_in", tiles(0))
            dve.wait_ge(evacuated, PLAN["pool_mix"].g0)
            ping = proj[:, 32:35, :], proj[:, 35:38, :]
            for n, win in enumerate(POOL_WINDOWS):
                if n:
                    dve.wait_ge(x_ready, x_made["pooled"] + n)
                u = proj[:, 3 * n:3 * n + 3, :]
                src = u
                for s in range(n + 1):
                    d = 1 << s
                    dst = ping[s % 2]
                    dve.tensor_copy(dst[:, :, 0:d], src[:, :, 0:d])
                    then(dve.tensor_tensor(dst[:, :, d:T], src[:, :, d:T], src[:, :, 0:T - d], ALU.add))
                    src = dst
                rc = spread(proj[:, 44 + n:45 + n, :], 1, 3)
                then(dve.tensor_tensor(src, src, rc, ALU.mult))
                pooled = pair_tile(38, 3)
                then(dve.tensor_tensor(proj[:, 38:41, :], src, u, ALU.subtract))
                split(pooled, flat(x_high, 3 * n, 3), flat(x_low, 3 * n, 3)).then_inc(x_ready, 1)
            dve.wait_ge(silu_ready, 4)
            for j in range(4):
                g = PLAN["pool_mix"].g0 + j
                dve.wait_ge(units_used, PLAN["pool_mix"].made(j))
                for f in range(3):
                    t = 3 * j + f
                    last = dve.scalar_tensor_tensor(out=proj[:, 12 + t, :], in0=bank[2 * (g % 2) + f // 2][:, (f % 2) * T:(f % 2) * T + T],
                                                    scalar=gains[:, 1, G_POOL.start + t:G_POOL.start + t + 1],
                                                    in1=proj[:, 12 + t, :], op0=ALU.mult, op1=ALU.mult)
                last.then_inc(evacuated, 1)
            attend(MEM0)
            dve.wait_ge(evacuated, PLAN["out0"].g0)
            split_tiles("pool_y", (12, 16, 20, 28))
            residual("out0")

            norm("kv", 1, G_KV)
            keep("cmp_kv", tiles(0))
            keep("sel_k", tiles(8))
            keep("sel_v", rows(sel_v))
            keep("win_k", tiles(16))
            keep("win_v", rows(win_v))
            dve.wait_ge(misc_in, 32)
            dve.tensor_copy(rstd[0:1, 0, 0:T], pos_i[:, :]).then_inc(rope_pos, 1)
            dve.wait_ge(rope_pos, 2)
            col = stats[0:ROT, 0, 8:9]
            then(dve.tensor_copy(col, bank[6][0:ROT, 0:1]))
            ang, turns = rope_s[:, :], rope_c[:, :]
            then(dve.tensor_scalar(ang, bank[5][0:ROT, 0:T], col, None, ALU.mult))
            then(dve.tensor_scalar(turns, ang, 0.15915494309189535, 12582912.0, ALU.mult, ALU.add))
            then(dve.tensor_scalar(turns, turns, 12582912.0, None, ALU.subtract))
            for part in TWO_PI_PARTS:
                then(dve.scalar_tensor_tensor(out=ang, in0=turns, scalar=-part, in1=ang, op0=ALU.mult, op1=ALU.add))
            then(dve.tensor_scalar(ang, ang, 3.1415925, -3.1415925, ALU.min, ALU.max))
            then(dve.tensor_scalar(turns, ang, -1.0, None, ALU.mult))
            dve.tensor_tensor(turns, turns, ang, ALU.max).then_inc(rope_angle, 1)
            dve.wait_ge(rope_sin, 2)
            dve.sem_inc(rope_tables, 1)

            def rotate(n):
                x, tiles_, t_from = ROPE_TURNS[n]
                if t_from is None:
                    c = spread(rope_c[:, :].rearrange("p (m t) -> p m t", m=1), 1, 2)
                    s = spread(rope_s[:, :].rearrange("p (m t) -> p m t", m=1), 1, 2)
                    view = lambda y: y[0:ROT, 0:2 * T].rearrange("p (m t) -> p m t", m=2)
                else:
                    c, s = (spread(y[:, t_from:T:CMP_STRIDE].rearrange("p (m t) -> p m t", m=1), 1, 4)
                            for y in (rope_c, rope_s))
                    view = lambda y: y[0:ROT, 0:4 * N_CMP].rearrange("p (m t) -> p m t", m=4)
                b = bank[5 + n % 2]
                a_, b_ = view(rstd[:, 0, :]), view(rstd[:, 1, :])
                if n:
                    dve.wait_ge(rope_done, n)
                dve.wait_ge(rope_swapped, n + 1)
                dve.tensor_tensor(a_, x, c, ALU.mult)
                then(dve.tensor_tensor(b_, view(b), s, ALU.mult))
                dve.tensor_tensor(x, a_, b_, ALU.add).then_inc(rope_done, 1)

            dve.wait_ge(evacuated, PLAN["cmp_hid_k"].g0)
            for n in range(4):
                rotate(n)
            n_blocks = CMP_LEN * 4 * N_CMP
            blocks = heads_scratch[:, 0:n_blocks].rearrange("p (l n) -> p l n", l=CMP_LEN)
            for c in range(2):
                if c:
                    dve.wait_ge(x_ready, x_made["blocks"] + 1)
                for kv in range(4):
                    z = proj[:, 4 * c + kv, :].rearrange("p (m r) -> p r m", r=CMP_STRIDE)
                    for half in range(2):
                        l = slice(CMP_STRIDE * half, CMP_STRIDE * half + CMP_STRIDE)
                        last = dve.tensor_tensor(blocks[:, l, kv * N_CMP:kv * N_CMP + N_CMP],
                                                 z[:, :, half:half + N_CMP],
                                                 spread(pe_cols[:, c, l].rearrange("p (l n) -> p l n", n=1), 2, N_CMP),
                                                 ALU.add)
                then(last)
                split(blocks, zpe(x_high, c), zpe(x_low, c)).then_inc(x_ready, 1)
            for c, name in enumerate(("cmp_hid_k", "cmp_hid_v")):
                dve.wait_ge(hid_act, c + 1)
                dve.sem_inc(evacuated, 1)
            dve.wait_ge(cmp_second, 1)
            dve.tensor_copy(vcmp[0:N_CMP, :, :].rearrange("p m d -> p (m d)"), bank[5][0:N_CMP, :])
            dve.tensor_copy(kcmpT[:, 0:4 * N_CMP], bank[7][:, 0:4 * N_CMP]).then_inc(cmp_ready, 1)
            dve.wait_ge(cmp_ready, 1)
            rotate(4)
            norm("nsa", 0, G_2B)
            keep("nsa_q", tiles(24))
            g = PLAN["nsa_gate"]
            dve.wait_ge(units_used, g.made())
            for h in range(TH):
                last = dve.tensor_copy(nsa_gates[:, h, :], bank[2 * (g.g0 % 2) + h][:, 0:36])
            last.then_inc(evacuated, 1)
            keep("nsa_zq", tiles(36))
            keep("nsa_qm", tiles(48))
            keep("nsa_zm", tiles(52))
            for n in range(5, len(ROPE_TURNS)):
                rotate(n)
            dve.wait_ge(silu_ready, 9)
            attend(NSA)
            attend(MEM1)
            split_tiles("nsa_y", (36, 40, 44, 52))
            residual("out1")

            dve.wait_ge(norm_root, normed[0] + 1)
            then(dve.reciprocal(rstd[:, 1, 0:T], rstd[:, 0, 0:T]))
            for kt in range(KT):
                last = normed_tile(proj[:, kt, :], kt, 1, G_FINAL)
                if kt % 4 == 3:
                    last.then_inc(out_ready, 1)
            for n in range(8):
                h, c = n % 2, n // 2
                dve.wait_ge(final_turned, n + 1)
                dve.tensor_copy(tokens[:, h, c * 512:c * 512 + 512], bank[5 + n % 2][:, :]).then_inc(final_kept, 1)


_INS = ['x', 'mem', 'norm_mix', 'w_in', 'hgrn_lb_logits', 'hgrn_onorm', 'attn_qnorm', 'attn_knorm', 'w_out',
        'norm_cross', 'mem_norm', 'wq_x', 'wk_x', 'wv_x', 'wo_x', 'xq_norm', 'xk_norm', 'norm_mlp', 'w_up',
        'w_down', 'mem_2', 'positions_2', 'norm_g_2', 'mem_norm_g_2', 'w_mem_kv_2', 'w_out_2', 'a_w_in_2',
        'a_w_pool_2', 'a_pool_scale_2', 'b_w_in_2', 'kv_norm_g_2', 'w_kv_2', 'cmp_pe_2', 'cmp_w1_2', 'cmp_w2_2',
        'final_g_2']


def kernel(**inputs):
    import numpy as np
    import concourse.bacc as bacc
    from concourse.bass_utils import run_bass_kernel_spmd

    nc = bacc.Bacc("TRN2", target_bir_lowering=False, num_devices=1, dynamic_dma_scratch_size=1024)
    arrays, args = {}, {}
    for name in _INS:
        arr = np.ascontiguousarray(inputs[name])
        arrays[f"in_{name}"] = arr
        args[name] = nc.dram_tensor(f"in_{name}", arr.shape, mybir.dt.from_np(arr.dtype), kind="ExternalInput").ap()
    args["out"] = nc.dram_tensor("out", (1, T, D), F32, kind="ExternalOutput").ap()
    build_program(nc, args)
    r = run_bass_kernel_spmd(nc, [arrays], core_ids=[0])
    return r.results[0]["out"]
```

```python
from contextlib import ExitStack

import concourse.bass as bass
from concourse import mybir

F32 = mybir.dt.float32
I32 = mybir.dt.int32
F32R = mybir.dt.float32r
ALU = mybir.AluOpType
ACT = mybir.ActivationFunctionType
AX = mybir.AxisListType.X

P = 128
D = 2048
KT = D // P
T = 256
TH = T // P
HD = 128
FF_PART = 2048
EPS = 1e-6
ATT_SCALE = HD ** -0.5
RING = 4
CHUNK = 2048
UNITS = 4
NEG = -1e30
TAKEN = -3e38
TOPK = 64
IDX_HEADS = 16
IDX_SCALE = IDX_HEADS ** -0.5 * 64 ** -0.5
CMP_LEN, CMP_STRIDE = 32, 16
N_CMP = (T - CMP_LEN) // CMP_STRIDE + 1
ROPE_THETA = 500000.0
ROT = HD // 4
POOL_WINDOWS = (2, 4, 8, 16)
CHUNK_T = 64
LEVELS = (1, 2, 4, 8, 16, 32, 64)
TWO_PI_PARTS = (6.28125, 0.0019354820251464844, -1.7484556025237907e-07)


def spread(ap, dim, count):
    shape = list(ap.shape)
    shape[dim] = count
    return ap.broadcast_to(shape)


class Gemm:

    def __init__(self, b0, blocks, g0, groups, rows, width):
        self.b0, self.blocks, self.g0, self.groups, self.rows, self.width = b0, blocks, g0, groups, rows, width
        self.units = 8 * blocks // groups

    def made(self, n=0):
        return 8 * self.b0 + self.units * (n + 1)

    def unit(self, u):
        half = (self.rows + 1) // 2
        return (0, half) if u % 2 == 0 else (half, self.rows - half)


def plan_stream():
    order = [("hgrn_qf", 4, 4), ("hgrn_v", 2, 2), ("gate_q_k", 6, 6), ("idx_q", 2, 2), ("idx_tail", 1, 1, 4, 80),
             ("attn_v", 2, 2), ("cross_k", 1, 1), ("cross_v", 1, 1),
             ("mem_k0", 1, 1), ("mem_v0", 1, 1), ("mix_out", 4, 4),
             ("cross_q", 1, 1), ("mem_k1", 1, 1), ("mem_v1", 1, 1), ("cross_out", 1, 4),
             *((f"{side}{part}", 4, 4) for part in range(4) for side in ("up", "down")),
             ("pool_in", 6, 6), ("pool_qm", 1, 1), ("pool_zm", 1, 1), ("pool_mix", 1, 4, 3, 384), ("out0", 4, 4),
             ("cmp_kv", 2, 2), ("sel_k", 1, 1), ("sel_v", 1, 1), ("win_k", 1, 1), ("win_v", 1, 1),
             ("cmp_hid_k", 1, 1, 8, 256), ("cmp_hid_v", 1, 1, 8, 256),
             ("nsa_q", 3, 3), ("nsa_gate", 1, 1, 4, 36), ("nsa_zq", 3, 3), ("nsa_qm", 1, 1), ("nsa_zm", 1, 1),
             ("out1", 4, 4)]
    plan, b, g = {}, 0, 0
    for name, blocks, groups, *shape in order:
        plan[name] = Gemm(b, blocks, g, groups, *(shape or (4, 512)))
        b += blocks
        g += groups
    return plan


def build_program(nc, a):
    PLAN = plan_stream()
    ctx = ExitStack()
    with ctx:
        def sb(name, shape, dt=F32):
            return ctx.enter_context(nc.sbuf_tensor(name, shape, dt))

        def sem(name):
            return ctx.enter_context(nc.semaphore(name))

        proj_at = (nc.sbuf_base + 31) // 32 * 32
        proj = sb("proj", [P, 64, T])
        hidden = nc.alloc_sbuf_tensor_at("hidden", [P, 2, KT, T], F32R, offset=proj_at)
        hT = sb("hT", [P, KT, T])
        x_high = sb("x_high", [P, KT, T], F32R)
        x_low = sb("x_low", [P, KT, T], F32R)
        ring = sb("ring", [P, RING, CHUNK])
        w_high = sb("w_high", [P, UNITS, CHUNK // 2], F32R)
        w_low = sb("w_low", [P, UNITS, CHUNK // 2], F32R)
        scratch = sb("scratch", [P, 6144])
        heads_scratch = sb("heads_scratch", [P, 3072])
        ident = sb("ident", [P, P])
        ones = sb("ones", [P, P])
        gains = sb("gains", [P, 2, P])
        pe_cols = sb("pe_cols", [P, 2, CMP_LEN])
        lower = sb("lower", [P, 16])
        causal = sb("causal", [P, TH, T])
        cmp_mask = sb("cmp_mask", [P, TH, 16])
        rstd = sb("rstd", [P, 2, 2 * T])
        ikT = sb("ikT", [P, T])
        idx_w = sb("idx_w", [P, TH, 16])
        small = sb("small", [P, 64])
        stats = sb("stats", [P, 2, 16])
        best = sb("best", [P, TH, 8])
        nsa_gates = sb("nsa_gates", [P, TH, 36])
        swap = sb("swap", [ROT, ROT])
        inv_row = sb("inv_row", [1, ROT])
        eps_col = sb("eps_col", [P, 4])
        tok_rstd = sb("tok_rstd", [P, 8])
        kcmpT = sb("kcmpT", [P, 64])
        bank = [ctx.enter_context(nc.psum_tensor(f"bank{i}", [P, 512], F32)) for i in range(8)]

        landed = [sem(f"landed{i}") for i in range(RING)]
        units_used = sem("units_used")
        high_ready = sem("high_ready")
        low_ready = sem("low_ready")
        evacuated = sem("evacuated")
        gains_in = sem("gains_in")
        tokens_in = sem("tokens_in")
        misc_in = sem("misc_in")
        out_stored = sem("out_stored")
        consts_ready = sem("consts_ready")
        pool_order = sem("pool_order")
        dve_order = sem("dve_order")
        act_order = sem("act_order")
        gains_turned = sem("gains_turned")
        gains_ready = sem("gains_ready")
        rows_scaled = sem("rows_scaled")
        rows_squared = sem("rows_squared")
        rows_turned = sem("rows_turned")
        rows_kept = sem("rows_kept")
        norm_squares = sem("norm_squares")
        norm_sums = sem("norm_sums")
        norm_root = sem("norm_root")
        x_ready = sem("x_ready")
        out_ready = sem("out_ready")
        idx_turned = sem("idx_turned")
        idx_keys = sem("idx_keys")
        head_squares = sem("head_squares")
        head_sums = sem("head_sums")
        head_root = sem("head_root")
        head_normed = sem("head_normed")
        scores_ready = sem("scores_ready")
        max_ready = sem("max_ready")
        exp_ready = sem("exp_ready")
        probs_ready = sem("probs_ready")
        probs_turned = sem("probs_turned")
        turned_kept = sem("turned_kept")
        values_summed = sem("values_summed")
        out_kept = sem("out_kept")
        hg_act = sem("hg_act")
        hg_dve = sem("hg_dve")
        hg_exp = sem("hg_exp")
        hg_pe = sem("hg_pe")
        hg_operands = sem("hg_operands")
        hg_scores = sem("hg_scores")
        hg_placed = sem("hg_placed")
        hg_out = sem("hg_out")
        hg_square = sem("hg_square")
        hg_sum = sem("hg_sum")
        hg_root = sem("hg_root")
        hg_done = sem("hg_done")
        idx_logits = sem("idx_logits")
        idx_relu = sem("idx_relu")
        idx_added = sem("idx_added")
        silu_ready = sem("silu_ready")
        hidden_ready = sem("hidden_ready")
        hidden_squared = sem("hidden_squared")
        rope_pos = sem("rope_pos")
        rope_angle = sem("rope_angle")
        rope_sin = sem("rope_sin")
        rope_tables = sem("rope_tables")
        rope_swapped = sem("rope_swapped")
        rope_done = sem("rope_done")
        hid_act = sem("hid_act")
        hid_turned = sem("hid_turned")
        cmp_second = sem("cmp_second")
        cmp_ready = sem("cmp_ready")
        final_turned = sem("final_turned")
        final_kept = sem("final_kept")

        G_MIX, G_CROSS, G_MEM, G_MLP, G_2A, G_2B, G_M2A, G_M2B = (slice(16 * i, 16 * i + 16) for i in range(8))
        G_KV, G_FINAL = slice(0, 16), slice(16, 32)
        G_POOL, G_LB = slice(32, 44), slice(44, 60)
        G_ONORM, G_QN, G_KN, G_XQ, G_XK = 60, 61, 62, 63, 64

        hgrn_v = proj[:, 48:56, :].rearrange("p a t -> p (a t)").rearrange("p (h n) -> p h n", h=TH)
        attn_v = proj[:, 0:8, :].rearrange("p a t -> p (a t)").rearrange("p (h n) -> p h n", h=TH)

        def values_at(tile):
            return proj[:, tile:tile + 4, :].rearrange("p a t -> p (a t)").rearrange("p (h n) -> p h n", h=TH)

        cross_v, mem_v0, sel_v, win_v, mem_v1 = (values_at(t) for t in (12, 52, 12, 20, 60))
        tokens = scratch[:, 0:TH * D].rearrange("p (h n) -> p h n", h=TH)
        gain_rows = scratch[:, 5120:5504].rearrange("p (s c) -> p s c", s=3)
        masked_scores = heads_scratch[:, 0:1024].rearrange("p (b h s) -> p b h s", b=2, h=TH)
        probs = heads_scratch[:, 1024:2048].rearrange("p (b h s) -> p b h s", b=2, h=TH)
        probsT = heads_scratch[:, 2048:3072].rearrange("p (b n) -> p b n", b=2)
        sel_bias = scratch[:, 4096:4608].rearrange("p (h s) -> p h s", h=TH)
        idx_score = scratch[:, 4608:5120].rearrange("p (h s) -> p h s", h=TH)
        idx_relus = heads_scratch[:, 0:768].rearrange("p (b n) -> p b n", b=2)
        idx_rows = scratch[:, 4608:4608 + 160].rearrange("p (h n) -> p h n", h=TH)
        head_sq = scratch[:, 5120:6144].rearrange("p (b n) -> p b n", b=2)

        vcmp = scratch[0:16, 4096:4608].rearrange("p (m d) -> p m d", m=4)
        rope_c, rope_s = (scratch[0:ROT, c:c + T] for c in (4848, 5104))
        pos_i = scratch[0:1, 5376:5632].bitcast(I32)
        cmp_w2 = scratch[:, 5632:6144].rearrange("p (i m d) -> p i m d", i=2, m=2)

        hg_logf, hg_cum, hg_decay, hg_keys, hg_queries, hg_reset, hg_tmp, hg_osq = (
            scratch[:, 512 * n:512 * n + 512] for n in range(8))
        level_mask = scratch[:, 4096:4096 + len(LEVELS) * CHUNK_T].rearrange("p (n t) -> p n t", t=CHUNK_T)
        hg_diag = heads_scratch[:, 0:2048].rearrange("p (m t) -> p m t", t=P)
        hg_cross = heads_scratch[:, 2048:3072].rearrange("p (m t) -> p m t", t=P)
        hidT = scratch[:, 4608:4608 + 16 * N_CMP].rearrange("p (c m n) -> p c m n", c=2, m=2)

        hid_rows = heads_scratch[0:4 * N_CMP, 2048:2560].rearrange("p (c n) -> p c n", c=2)

        def zpe(x, c):
            n = CMP_LEN * 4 * N_CMP
            return x[:, 8 * c:8 * c + 8, :].rearrange("p a t -> p (a t)")[:, 0:n].rearrange("p (l n) -> p l n", l=CMP_LEN)

        ROPE_TURNS = ([(proj[0:ROT, t:t + 2, :], 2, None) for t in (8, 10, 16, 18)]
                      + [(kcmpT[0:ROT, 0:4 * N_CMP].rearrange("p (m t) -> p m t", m=4), 4, CMP_LEN - 1)]
                      + [(proj[0:ROT, t:t + 2, :], 2, None) for t in range(24, 36, 2)])

        block = ctx.enter_context(nc.Block())

        norm_pairs = ([(24 + 2 * n, G_QN) for n in range(4)] + [(32 + 2 * n, G_KN) for n in range(4)]
                      + [(16 + 2 * n, G_XQ) for n in range(2)] + [(8 + 2 * n, G_XK) for n in range(2)])
        MIX_PAIRS, CROSS_PAIRS = range(0, 8), range(8, 12)

        class Item:
            def __init__(self, q, k, v, widths, out, mask=None, gate=None, first=True, last=True):
                self.q, self.k, self.v, self.widths, self.out = q, k, v, widths, out
                self.mask, self.gate, self.first, self.last = mask, gate, first, last

        CAUSAL, FULL, CMP = (P, T), (T, T), (N_CMP, N_CMP)
        items = []
        for h in range(8):
            items.append(Item(proj[:, 24 + h, :], proj[:, 32 + h, :], attn_v[:, :, h * HD:h * HD + HD],
                              CAUSAL, proj[:, 24 + h, :], mask=sel_bias))
        DSA = range(0, 8)
        for h in range(4):
            items.append(Item(proj[:, 16 + h, :], proj[:, 8 + h, :], cross_v[:, :, h * HD:h * HD + HD],
                              FULL, proj[:, 28 + h, :]))
        CROSS = range(8, 12)
        for h in range(4):
            items.append(Item(proj[:, 24 + h, :], proj[:, 48 + h, :], mem_v0[:, :, h * HD:h * HD + HD],
                              FULL, proj[:, 24 + h, :]))
        MEM0 = range(12, 16)
        for h in range(12):
            kv = h // 3
            for branch in range(3):
                q = proj[:, 24 + h, :]
                gate = nsa_gates[:, :, 3 * h + branch]
                if branch == 0:
                    it = Item(q, kcmpT[:, kv * N_CMP:kv * N_CMP + N_CMP], vcmp[:, kv, :], CMP, None,
                              mask=cmp_mask, gate=gate, last=False)
                elif branch == 1:
                    it = Item(q, proj[:, 8 + kv, :], sel_v[:, :, kv * HD:kv * HD + HD], CAUSAL, None,
                              mask=causal, gate=gate, first=False, last=False)
                else:
                    it = Item(q, proj[:, 16 + kv, :], win_v[:, :, kv * HD:kv * HD + HD], CAUSAL, q,
                              mask=causal, gate=gate, first=False)
                items.append(it)
        NSA = range(16, 52)
        for h in range(4):
            items.append(Item(proj[:, 48 + h, :], proj[:, 56 + h, :], mem_v1[:, :, h * HD:h * HD + HD],
                              FULL, proj[:, 48 + h, :]))
        MEM1 = range(52, 56)
        outs_before = [sum(it.last for it in items[:n]) for n in range(len(items) + 1)]

        operands, x_made = [("mix", 4), ("cross_mem", 4), ("mem0", 4), ("mix_y", 4), ("cross", 4),
                            ("mem1", 4), ("cross_y", 1), ("mlp", 4), ("pool", 4), ("pooled", 4), ("pool_y", 4), ("kv", 4),
                            ("blocks", 2), ("nsa", 4), ("nsa_y", 4)], {}
        total = 0
        for name, n in operands:
            x_made[name] = total
            total += n

        def hg_tiles(hg):
            return pair_tile(2 * hg), pair_tile(8 + 2 * hg)

        def pair_tile(n, step=2):
            return proj[:, n:n + step, :].rearrange("p a t -> p (a t)")

        STEPS = len(LEVELS) + 2

        def units_of(*names):
            return [(name, k) for name in names for k in range(8 * PLAN[name].blocks)]

        def side_by_side(units, steps):
            return [units[len(units) * n // steps:len(units) * (n + 1) // steps] for n in range(steps)]

        LEAD = 4
        IDX_ROWS_STEP, ROWS_STEP = 9, 5
        ROPED = 6
        SILU_STEP = 46
        HGRN_OUT_STEPS, IDX_STEPS = 6, IDX_HEADS
        BESIDE_INDEX = units_of("attn_v")
        BESIDE_MIX_HEADS = units_of("cross_k", "cross_v")
        BESIDE_DSA = units_of("mem_k0", "mem_v0")
        BESIDE_CROSS = units_of("mem_k1", "mem_v1")
        CROSS_HEADS = 8
        TOKENS_FIRST = ("attn_v", "cross_v", "mem_v0", "mem_v1", "nsa_gate")
        NEW_OPERAND = {"cross_k": "cross_mem", "mem_k0": "mem0", "mem_k1": "mem1"}
        BESIDE_NSA = units_of("nsa_zq", "nsa_qm", "nsa_zm")

        def exps_before(hg, s):
            return 2 * (len(LEVELS) + 1) * hg + 2 * min(s, len(LEVELS))

        @block.sync
        def _(sp):
            x_rows = a["x"].rearrange("a (h p) n -> p (a h) n", p=P)
            mem_rows = a["mem"].rearrange("a (h p) n -> p (a h) n", p=P)
            mem2_rows = a["mem_2"].rearrange("a (h p) n -> p (a h) n", p=P)
            sp.dma_start(tokens, x_rows).then_inc(tokens_in, 16)

            row = 0
            def gain(name, rows, view, slot):
                nonlocal row
                sp.dma_start(gain_rows[row:row + rows, slot, :], view).then_inc(gains_in, 16)
                row += rows

            for name, n in (("norm_mix", 16), ("norm_cross", 16), ("mem_norm", 16), ("norm_mlp", 16),
                            ("norm_g_2", 32), ("mem_norm_g_2", 32)):
                gain(name, n, a[name].rearrange("l (r c) -> (l r) c", c=P), 0)
            row = 0
            gain("kv_norm_g_2", 16, a["kv_norm_g_2"].rearrange("(r c) -> r c", c=P), 1)
            gain("final_g_2", 16, a["final_g_2"].rearrange("(r c) -> r c", c=P), 1)
            gain("a_pool_scale_2", 12, a["a_pool_scale_2"].rearrange("l (r c) -> (l r) c", c=P), 1)
            gain("hgrn_lb_logits", 16, a["hgrn_lb_logits"].rearrange("l (r c) -> (l r) c", c=P), 1)
            for name in ("hgrn_onorm", "attn_qnorm", "attn_knorm", "xq_norm", "xk_norm"):
                gain(name, 1, a[name], 1)
            row = 0
            gain("cmp_pe_2", 64, a["cmp_pe_2"].rearrange("i l d -> (i l) d"), 2)
            def stream(name, source, between=None):
                g = PLAN[name]

                def block_of(n, b, more):
                    for j in range(4):
                        need = 8 * b + 2 * j - 2 * RING + 2
                        if need > 0:
                            sp.wait_ge(low_ready, need + more)
                        dst = ring[:, j, 0:g.rows * g.width].rearrange("p (k n) -> p k n", k=g.rows)
                        sp.dma_start(dst, source(n, j)).then_inc(landed[j], 16)

                peel = g.blocks if g.blocks < 3 else int(g.b0 == 0)
                for n in range(peel):
                    if n == 1 and between:
                        between()
                    block_of(n, g.b0 + n, 0)
                if peel < g.blocks:
                    with sp.Fori(0, g.blocks - peel) as i:
                        block_of(i + peel, g.b0 + peel, i * 8)

            def columns(w, col0):
                w3 = w.rearrange("(k p) n -> p k n", p=P)

                return lambda n, j: w3[:, 4 * j:4 * j + 4, bass.ds(n * 512 + col0, 512)]

            w_in = a["w_in"].rearrange("l k n -> (l k) n")
            stream("hgrn_qf", columns(w_in, 0))
            stream("hgrn_v", columns(w_in, 2048))
            stream("gate_q_k", columns(w_in, 3072))
            stream("idx_q", columns(w_in, 7168))
            w_in3 = w_in.rearrange("(k p) n -> p k n", p=P)
            stream("idx_tail", lambda n, j: w_in3[:, 4 * j:4 * j + 4, 8192:8272])

            def load_memory():
                sp.wait_ge(hg_done, 4)
                sp.dma_start(tokens, mem_rows).then_inc(tokens_in, 16)
            stream("attn_v", columns(w_in, 6144), load_memory)
            w_mem = a["w_mem_kv_2"].rearrange("l k n -> (l k) n")
            stream("cross_k", columns(a["wk_x"].rearrange("l k n -> (l k) n"), 0))
            stream("cross_v", columns(a["wv_x"].rearrange("l k n -> (l k) n"), 0))
            sp.wait_ge(rows_turned, 16)
            sp.dma_start(tokens, mem2_rows).then_inc(tokens_in, 16)
            stream("mem_k0", columns(w_mem[0:D, :], 0))
            stream("mem_v0", columns(w_mem[0:D, :], 512))
            stream("mix_out", columns(a["w_out"].rearrange("l k n -> (l k) n"), 0))
            stream("cross_q", columns(a["wq_x"].rearrange("l k n -> (l k) n"), 0))
            stream("mem_k1", columns(w_mem[D:2 * D, :], 0))
            stream("mem_v1", columns(w_mem[D:2 * D, :], 512))
            wo3 = a["wo_x"].rearrange("l (k p) n -> p (l k) n", p=P)
            stream("cross_out", lambda n, j: wo3[:, :, 512 * j:512 * j + 512])
            w_up = a["w_up"].rearrange("l k n -> (l k) n")
            w_down = a["w_down"].rearrange("l k n -> (l k) n")
            for part in range(4):
                stream(f"up{part}", columns(w_up, part * FF_PART))
                stream(f"down{part}", columns(w_down[part * FF_PART:(part + 1) * FF_PART, :], 0))
            sp.wait_ge(norm_sums, 3)
            sp.dma_start(pos_i[:, :], a["positions_2"]).then_inc(misc_in, 16)
            sp.dma_start(cmp_w2[:, :, :, :], a["cmp_w2_2"].rearrange("i (k p) d -> p i k d", p=P)).then_inc(misc_in, 16)
            w_a = a["a_w_in_2"].rearrange("l k n -> (l k) n")
            stream("pool_in", columns(w_a, 0))
            stream("pool_qm", columns(w_a, 3072))
            stream("pool_zm", columns(w_a, 3584))
            w_pool = a["a_w_pool_2"].rearrange("l g (k p) n -> p (l g) k n", p=P)
            stream("pool_mix", lambda n, j: w_pool[:, j, :, :])
            w_out2 = a["w_out_2"].rearrange("l k n -> (l k) n")
            stream("out0", columns(w_out2[0:D, :], 0))
            w_kv = a["w_kv_2"]
            stream("cmp_kv", columns(w_kv, 0))
            stream("sel_k", columns(w_kv, 1024))
            stream("sel_v", columns(w_kv, 1536))
            stream("win_k", columns(w_kv, 2048))
            stream("win_v", columns(w_kv, 2560))
            w1 = a["cmp_w1_2"].rearrange("i (l p) n -> p i l n", p=P)
            stream("cmp_hid_k", lambda n, j: w1[:, 0, 8 * j:8 * j + 8, :])
            stream("cmp_hid_v", lambda n, j: w1[:, 1, 8 * j:8 * j + 8, :])
            w_b = a["b_w_in_2"].rearrange("l k n -> (l k) n")
            w_b3 = w_b.rearrange("(k p) n -> p k n", p=P)
            stream("nsa_q", columns(w_b, 0))
            stream("nsa_gate", lambda n, j: w_b3[:, 4 * j:4 * j + 4, 1536:1572])
            stream("nsa_zq", columns(w_b, 1572))
            stream("nsa_qm", columns(w_b, 3108))
            stream("nsa_zm", columns(w_b, 3620))
            stream("out1", columns(w_out2[D:2 * D, :], 0))
            sp.wait_ge(final_kept, 8)
            sp.dma_start(a["out"].rearrange("a (h p) n -> p (a h) n", p=P), tokens).then_inc(out_stored, 16)
            sp.wait_ge(out_stored, 16)

        @block.gpsimd
        def _(pool):
            count = [0]

            def then(ins):
                count[0] += 1
                ins.then_inc(pool_order, 1)
                pool.wait_ge(pool_order, count[0])

            def select(out, pattern, base, per_row, op=ALU.is_ge, fill=0.0):
                then(pool.affine_select(out=out, in_=out, compare_op=op, fill=fill, base=base,
                                        pattern=pattern, channel_multiplier=per_row))

            then(pool.memset(ident[:, :], 0.0))
            select(ident[:, :], [[-1, P]], 0, 1, ALU.not_equal, 1.0)
            pool.memset(ones[:, :], 1.0)
            pool.memset(eps_col[:, 0:1], EPS)
            pool.memset(eps_col[:, 1:2], 1.5707963267948966)
            pool.memset(eps_col[:, 2:3], 0.0).then_inc(consts_ready, 1)
            then(pool.memset(causal[:, :, :], 0.0))
            select(causal[:, :, :], [[P, TH], [-1, T]], 0, 1, fill=NEG)
            then(pool.memset(cmp_mask[:, :, :], 0.0))
            select(cmp_mask[:, :, :], [[P, TH], [-CMP_STRIDE, 16]], 1 - CMP_LEN, 1, fill=NEG)
            then(pool.memset(swap[:, :], 0.0))
            select(swap[:, :], [[-1, ROT]], -ROT // 2, 1, ALU.not_equal, -1.0)
            select(swap[:, :], [[-1, ROT]], ROT // 2, 1, ALU.not_equal, 1.0)
            for j in range(ROT):
                last = pool.memset(inv_row[:, j:j + 1], float(ROPE_THETA ** (-(j % (ROT // 2)) * 2.0 / ROT)))
            last.then_inc(consts_ready, 1)
            pool.wait_ge(norm_sums, 1)
            then(pool.memset(level_mask[:, :, :], 1.0))
            for n, w in enumerate(LEVELS):
                v = level_mask[:, n, :].rearrange("p (b w) -> p b w", w=w)
                select(v, [[-2 * w, CHUNK_T // w], [0, w]], 0, 1)
                select(v, [[2 * w, CHUNK_T // w], [0, w]], w - 1, -1)
            then(pool.memset(hg_reset, 1.0))
            v = hg_reset.rearrange("p (c t) -> p c t", t=CHUNK_T)
            pool.memset(v[:, :, 0], 0.0).then_inc(consts_ready, 1)

            def low_parts(name):
                g = PLAN[name]

                def block_of(b, more):
                    for u in range(8):
                        r0, rows = g.unit(u)
                        n = rows * g.width
                        pool.wait_ge(high_ready, 8 * b + u + 1 + more)
                        pool.tensor_tensor(w_low[:, u % UNITS, 0:n], ring[:, u // 2, r0 * g.width:r0 * g.width + n],
                                           w_high[:, u % UNITS, 0:n], ALU.subtract).then_inc(low_ready, 1)

                if g.blocks < 3:
                    for n in range(g.blocks):
                        block_of(g.b0 + n, 0)
                else:
                    with pool.Fori(0, g.blocks) as i:
                        block_of(g.b0, i * 8)

            for name in PLAN:
                low_parts(name)

        @block.tensor
        def _(pe):
            def group_free(g, more=0):
                if g >= 2:
                    pe.wait_ge(evacuated, g - 1 + more)

            def parts(u, g):
                rows = g.unit(u)[1]
                return (w[:, u % UNITS, 0:rows * g.width].rearrange("p (k n) -> p k n", k=rows)
                        for w in (w_high, w_low))

            def accumulate(out, w, x, start, stop, tokens_first=False):
                (wh, wl), (xh, xl) = w, x
                for n, (a_, b_) in enumerate(((wh, xh), (wh, xl), (wl, xh))):
                    lhs, rhs = (b_, a_) if tokens_first else (a_, b_)
                    mm = pe.matmul(out, lhs, rhs, start=start and n == 0, stop=stop and n == 2,
                                   skip_group_check=True)
                return mm

            def features_unit(g, b, u, pair, x, first, of, more=0):
                pe.wait_ge(low_ready, 8 * b + u + 1 + more)
                wh, wl = parts(u, g)
                r0, rows = g.unit(u)
                for k in range(rows):
                    kt = first + r0 + k
                    for f in range(g.width // P):
                        cols = slice(f * P, f * P + P)
                        mm = accumulate(pair[f // 2][:, (f % 2) * T:(f % 2) * T + T],
                                        (wh[:, k, cols], wl[:, k, cols]), x(kt),
                                        start=(kt == 0 and f % 2 == 0), stop=(kt == of - 1))
                mm.then_inc(units_used, 1)

            def tokens_unit(g, b, u, pair, x, first, of, more=0):
                pe.wait_ge(low_ready, 8 * b + u + 1 + more)
                wh, wl = parts(u, g)
                r0, rows = g.unit(u)
                for k in range(rows):
                    kt = first + r0 + k
                    xh, xl = x(kt)
                    for h in range(TH):
                        t = slice(h * P, h * P + P)
                        mm = accumulate(pair[h][:, 0:g.width], (wh[:, k, :], wl[:, k, :]), (xh[:, t], xl[:, t]),
                                        start=(kt == 0), stop=(kt == of - 1), tokens_first=True)
                mm.then_inc(units_used, 1)

            def pair_of(g):
                return bank[2 * (g % 2)], bank[2 * (g % 2) + 1]

            def product(name, unit, x, made=None, ready=x_ready):
                g = PLAN[name]

                def block_of(n, more, more_groups, wait):
                    group_free(g.g0 + n, more_groups)
                    for u in range(8):
                        if wait and u % 2 == 0:
                            pe.wait_ge(ready, made + u // 2 + 1)
                        unit(g, g.b0 + n, u, pair_of(g.g0 + n), x, 4 * (u // 2), KT, more)

                peel = g.blocks if g.blocks < 4 else (0 if made is None else 2)
                for n in range(peel):
                    block_of(n, 0, 0, made is not None and n == 0)
                if peel < g.blocks:
                    with pe.Fori(0, (g.blocks - peel) // 2) as i:
                        for q in range(2):
                            block_of(peel + q, i * 16, i * 2, False)

            operand = lambda kt: (x_high[:, kt, :], x_low[:, kt, :])
            hidden_tile = lambda kt: (hidden[:, 0, kt, :], hidden[:, 1, kt, :])

            pe.wait_ge(consts_ready, 1)
            pe.wait_ge(gains_in, 16 * 16)
            pe.transpose(bank[4][:, 0:P], gain_rows[:, 0, :], ident[:, :])
            pe.transpose(bank[4][:, P:P + 65], gain_rows[0:65, 1, :], ident[0:65, 0:65])
            pe.transpose(bank[4][:, 2 * P:2 * P + 64], gain_rows[0:64, 2, :], ident[0:64, 0:64])\
              .then_inc(gains_turned, 1)

            turned = [0]

            def turn_rows():
                for n in range(KT // 2):
                    m = turned[0]
                    if m >= 3:
                        pe.wait_ge(rows_kept, m - 2)
                    for c in range(2):
                        for h in range(TH):
                            mm = pe.transpose(bank[5 + m % 3][:, c * T + h * P:c * T + h * P + P],
                                              tokens[:, h, (2 * n + c) * P:(2 * n + c) * P + P], ident[:, :])
                    mm.then_inc(rows_turned, 1)
                    turned[0] += 1

            pe.wait_ge(tokens_in, 16)
            turn_rows()

            normed = [0]

            def norm_sum(squares=scratch):
                n = normed[0]
                for c in range(4):
                    pe.wait_ge(norm_squares, 4 * n + c + 1)
                    for k in range(4):
                        kt = 4 * c + k
                        mm = pe.matmul(bank[4][:, 0:T], ones[:, :], squares[:, kt * T:kt * T + T],
                                       start=(kt == 0), stop=(kt == KT - 1))
                mm.then_inc(norm_sums, 1)
                normed[0] += 1

            def head_sum(pairs):
                for n in pairs:
                    pe.wait_ge(head_squares, n + 1)
                    if n >= 2:
                        pe.wait_ge(head_root, n - 1)
                    pe.matmul(bank[4 + n % 2][:, :], ones[:, :], head_sq[:, n % 2, :], start=True, stop=True)\
                      .then_inc(head_sums, 1)

            def scores(n):
                it = items[n]
                if n >= 2:
                    pe.wait_ge(exp_ready, n - 1)
                for h in range(TH):
                    w = it.widths[h]
                    mm = pe.matmul(bank[4 + n % 2][:, h * T:h * T + w], it.q[:, h * P:h * P + P],
                                   it.k[:, 0:w], start=True, stop=True)
                mm.then_inc(scores_ready, 1)

            def turned_col(s, h):
                return P + h * P if s == 0 else (0 if h == 0 else 3 * P)

            def turn_probs(n):
                it = items[n]
                pe.wait_ge(probs_ready, n + 1)
                if n >= 1:
                    pe.wait_ge(turned_kept, n)
                for h in range(TH):
                    for s in range(TH):
                        w = min(P, it.widths[h] - s * P)
                        if w > 0:
                            c = turned_col(s, h)
                            mm = pe.transpose(bank[6][0:w, c:c + P], probs[:, n % 2, h, s * P:s * P + w],
                                              ident[:, :])
                mm.then_inc(probs_turned, 1)

            def weigh_values(n):
                it = items[n]
                g = outs_before[n]
                pe.wait_ge(turned_kept, n + 1)
                if it.first and g:
                    pe.wait_ge(out_kept, g)
                o = bank[7][:, 0:T]
                pT = probsT[:, n % 2, :]
                if it.widths == CMP:
                    mm = pe.matmul(o, it.v[0:N_CMP, :], pT[0:N_CMP, P:3 * P], start=it.first, stop=it.last,
                                   skip_group_check=True)
                else:
                    pe.matmul(o, it.v[:, 0, :], pT[:, P:3 * P], start=it.first, stop=False, skip_group_check=True)
                    if it.widths == FULL:
                        pe.matmul(o[:, 0:P], it.v[:, 1, :], pT[:, 0:P], start=False, stop=False,
                                  skip_group_check=True)
                    mm = pe.matmul(o[:, P:T], it.v[:, 1, :], pT[:, 3 * P:4 * P], start=False, stop=it.last,
                                   skip_group_check=True)
                mm.then_inc(values_summed, 1)

            def one_unit(name, k):
                g, n, u = PLAN[name], k // 8, k % 8
                if u == 0:
                    group_free(g.g0 + n)
                if name in NEW_OPERAND and u % 2 == 0:
                    pe.wait_ge(x_ready, x_made[NEW_OPERAND[name]] + u // 2 + 1)
                unit = tokens_unit if name in TOKENS_FIRST else features_unit
                unit(g, g.b0 + n, u, pair_of(g.g0 + n), operand, 4 * (u // 2), KT)

            def attend_step(which, n):
                first, end = which[0], which[-1] + 1
                if n < end:
                    scores(n)
                if first <= n - 1 < end:
                    turn_probs(n - 1)
                if first <= n - 2 < end:
                    weigh_values(n - 2)

            def attend(which, units=()):
                for n, beside in enumerate(side_by_side(units, len(which) + 2)):
                    for name, k in beside:
                        one_unit(name, k)
                    if which[0] + n == MEM1[0]:
                        pe.wait_ge(evacuated, PLAN["nsa_qm"].g0 + 1)
                    attend_step(which, which[0] + n)

            norm_sum()
            product("hgrn_qf", features_unit, operand, made=x_made["mix"])
            product("hgrn_v", tokens_unit, operand)

            def hgrn_step(s, more):
                pe.wait_ge(hg_operands, s + 1 + more)
                pe.wait_ge(hg_placed, max(s, 1) + more)
                b = bank[4 + s % 2]
                if s < len(LEVELS):
                    for t in range(4):
                        mm = pe.matmul(b[:, t * CHUNK_T:t * CHUNK_T + CHUNK_T], hg_keys[:, t * P:t * P + P],
                                       hg_queries[:, t * CHUNK_T:t * CHUNK_T + CHUNK_T], start=True, stop=True)
                elif s == len(LEVELS):
                    for t in range(4):
                        mm = pe.matmul(b[:, t * P:t * P + P], hg_keys[:, t * P:t * P + P],
                                       hg_queries[:, t * P:t * P + P], start=True, stop=True)
                else:
                    for h in range(2):
                        mm = pe.matmul(b[:, h * P:h * P + P], hg_keys[:, h * T:h * T + P],
                                       hg_queries[:, h * P:h * P + P], start=True, stop=True)
                mm.then_inc(hg_scores, 1)

            g = PLAN["gate_q_k"]
            with pe.Fori(0, 4) as i:
                for q in range(2):
                    group_free(g.g0 + q, i * 2)
                    for u in range(8):
                        features_unit(g, g.b0 + q, u, pair_of(g.g0 + q), operand, 4 * (u // 2), KT, i * 16)
                        if u % 2:
                            hgrn_step(4 * q + u // 2, i * STEPS)
                hgrn_step(8, i * STEPS)

            g = PLAN["idx_tail"]
            group_free(g.g0)
            for u in range(8):
                tokens_unit(g, g.b0, u, pair_of(g.g0), operand, 4 * (u // 2), KT)

            def hgrn_out(m):
                if m >= 2:
                    pe.wait_ge(hg_done, m - 1)
                for h in range(2):
                    o = bank[6 + m % 2][:, h * T:h * T + T]
                    n = 2 * m + h
                    v = hgrn_v[:, :, n * HD:n * HD + HD]
                    pe.matmul(o[:, 0:P], v[:, 0, :], hg_diag[:, 2 * n, :], start=(h == 0), stop=False,
                              skip_group_check=True)
                    pe.matmul(o[:, P:T], v[:, 1, :], hg_diag[:, 2 * n + 1, :], start=False, stop=False,
                              skip_group_check=True)
                    mm = pe.matmul(o[:, P:T], v[:, 0, :], hg_cross[:, n, :], start=False, stop=True,
                                   skip_group_check=True)
                mm.then_inc(hg_out, 1)

            def hgrn_sum(m):
                pe.wait_ge(hg_square, m + 1)
                if m:
                    pe.wait_ge(hg_root, m)
                pe.matmul(bank[5][:, :], ones[:, :], hg_osq, start=True, stop=True).then_inc(hg_sum, 1)

            def index_logits(n):
                if n >= 2:
                    pe.wait_ge(idx_relu, n - 1)
                r = slice(64 * (n % 2), 64 * (n % 2) + 64)
                q = proj[:, 40 + n // 2, :]
                pe.matmul(bank[4 + n % 2][:, 0:P], q[r, 0:P], ikT[r, 0:P], start=True, stop=True)
                pe.matmul(bank[4 + n % 2][:, P:P + T], q[r, P:T], ikT[r, :], start=True, stop=True)\
                  .then_inc(idx_logits, 1)

            pe.wait_ge(hg_placed, 4 * STEPS + 1)
            for n, beside in enumerate(side_by_side(BESIDE_INDEX, HGRN_OUT_STEPS + IDX_STEPS)):
                for name, k in beside:
                    one_unit(name, k)
                if 1 <= n <= 4:
                    hgrn_sum(n - 1)
                if n < 4:
                    hgrn_out(n)
                if n == 5:
                    pe.wait_ge(idx_keys, 1)
                    for h in range(TH):
                        mm = pe.transpose(bank[4][0:64, h * P:h * P + P], idx_rows[:, h, 0:64], ident[:, :])
                    mm.then_inc(idx_turned, 1)
                if n == 6:
                    pe.wait_ge(idx_keys, 2)
                    pe.wait_ge(hg_root, 4)
                if n >= HGRN_OUT_STEPS:
                    index_logits(n - HGRN_OUT_STEPS)
            pe.wait_ge(idx_relu, IDX_HEADS)

            def heads(pairs, units):
                for k, beside in enumerate(side_by_side(units, len(pairs) + 1)):
                    for name, u in beside:
                        one_unit(name, u)
                    if k < len(pairs):
                        head_sum(pairs[k:k + 1])

            def turned_memory(units, scaled):
                pe.wait_ge(rows_scaled, scaled)
                turn_rows()
                for name, u in units[:LEAD]:
                    one_unit(name, u)
                pe.wait_ge(rows_kept, turned[0])

            turned_memory(BESIDE_MIX_HEADS, 1)
            heads(MIX_PAIRS, BESIDE_MIX_HEADS[LEAD:])
            pe.wait_ge(head_root, len(MIX_PAIRS))
            turned_memory(BESIDE_DSA, 2)
            pe.wait_ge(head_normed, 8)
            attend(DSA, BESIDE_DSA[LEAD:])
            product("mix_out", features_unit, operand, made=x_made["mix_y"])

            norm_sum(proj[:, 16:32, :].rearrange("p a t -> p (a t)"))
            product("cross_q", features_unit, operand, made=x_made["cross"])
            turned_memory(BESIDE_CROSS, 2)
            heads(CROSS_PAIRS, BESIDE_CROSS[LEAD:CROSS_HEADS])
            pe.wait_ge(head_normed, 12)
            attend(CROSS, BESIDE_CROSS[CROSS_HEADS:])
            g = PLAN["cross_out"]
            pe.wait_ge(x_ready, x_made["cross_y"] + 1)
            for u in range(8):
                if u % 2 == 0:
                    group_free(g.g0 + u // 2)
                features_unit(g, g.b0, u, pair_of(g.g0 + u // 2), operand, 0, 4)

            norm_sum()
            for part in range(4):
                product(f"up{part}", features_unit, operand, made=x_made["mlp"] if part == 0 else None)
                product(f"down{part}", features_unit, hidden_tile, made=4 * part + 1, ready=hidden_ready)

            norm_sum()
            product("pool_in", features_unit, operand, made=x_made["pool"])
            product("pool_qm", features_unit, operand)
            pe.wait_ge(evacuated, PLAN["pool_zm"].g0)
            attend(MEM0, units_of("pool_zm"))
            g = PLAN["pool_mix"]
            for u in range(8):
                j = u // 2
                if u % 2 == 0:
                    group_free(g.g0 + j)
                    pe.wait_ge(x_ready, x_made["pooled"] + j + 1)
                features_unit(g, g.b0, u, pair_of(g.g0 + j),
                              lambda kt: (x_high[:, 3 * j + kt, :], x_low[:, 3 * j + kt, :]), 0, 3)
            product("out0", features_unit, operand, made=x_made["pool_y"])

            norm_sum()
            product("cmp_kv", features_unit, operand, made=x_made["kv"])
            product("sel_k", features_unit, operand)
            product("sel_v", tokens_unit, operand)
            product("win_k", features_unit, operand)
            product("win_v", tokens_unit, operand)
            pe.wait_ge(rope_pos, 1)
            pe.matmul(bank[5][0:ROT, 0:T], ones[0:1, 0:ROT], rstd[0:1, 0, 0:T], start=True, stop=True)
            pe.matmul(bank[6][0:ROT, 0:2], inv_row[0:1, :], ones[0:1, 0:2], start=True, stop=True)\
              .then_inc(rope_pos, 1)

            swaps = [0]

            def swap_halves(x, width):
                n = swaps[0]
                if n >= 2:
                    pe.wait_ge(rope_done, n - 1)
                pe.matmul(bank[5 + n % 2][0:ROT, 0:width], swap[:, :], x, start=True, stop=True)\
                  .then_inc(rope_swapped, 1)
                swaps[0] += 1

            pe.wait_ge(rope_tables, 1)
            pe.wait_ge(evacuated, PLAN["win_v"].g0)
            for t in (8, 10, 16, 18):
                swap_halves(proj[0:ROT, t:t + 2, :], 2 * T)
            for c, name in enumerate(("cmp_hid_k", "cmp_hid_v")):
                g = PLAN[name]
                group_free(g.g0)
                pe.wait_ge(x_ready, x_made["blocks"] + c + 1)
                hid = bank[2 * (g.g0 % 2)][:, 0:g.width]
                for u in range(8):
                    pe.wait_ge(low_ready, 8 * g.b0 + u + 1)
                    wh, wl = parts(u, g)
                    for k in range(4):
                        l = 4 * u + k
                        cols = slice(4 * N_CMP * l, 4 * N_CMP * l + P)
                        xh, xl = (x[:, 8 * c:8 * c + 8, :].rearrange("p a t -> p (a t)")[:, cols] for x in (x_high, x_low))
                        mm = accumulate(hid, (wh[:, k, :], wl[:, k, :]), (xh, xl), start=(l == 0),
                                        stop=(l == CMP_LEN - 1), tokens_first=True)
                    mm.then_inc(units_used, 1)
            product("nsa_q", features_unit, operand, made=x_made["nsa"])
            pe.wait_ge(hid_act, 2)
            pe.wait_ge(rope_done, 4)
            for c in range(2):
                for m in range(2):
                    n = 64 * (2 * c + m)
                    mm = pe.transpose(bank[6][:, n:n + 4 * N_CMP], hid_rows[:, c, m * P:m * P + P],
                                      ident[0:4 * N_CMP, 0:4 * N_CMP])
            mm.then_inc(hid_turned, 1)
            pe.wait_ge(hid_act, 3)
            for m in range(2):
                pe.matmul(bank[7][:, 0:4 * N_CMP], cmp_w2[:, 0, m, :], hidT[:, 0, m, :], start=(m == 0), stop=(m == 1))
            for kv in range(4):
                for m in range(2):
                    mm = pe.matmul(bank[5][0:N_CMP, kv * P:kv * P + P],
                                   hidT[:, 1, m, kv * N_CMP:kv * N_CMP + N_CMP], cmp_w2[:, 1, m, :],
                                   start=(kv == 0 and m == 0), stop=(m == 1), skip_group_check=True)
            mm.then_inc(cmp_second, 1)
            for k in range(8):
                one_unit("nsa_gate", k)
            pe.wait_ge(cmp_ready, 1)
            swap_halves(kcmpT[0:ROT, 0:4 * N_CMP], 4 * N_CMP)
            pe.wait_ge(evacuated, PLAN["nsa_gate"].g0)
            for n, (name, k) in enumerate(BESIDE_NSA[:ROPED]):
                one_unit(name, k)
                swap_halves(proj[0:ROT, 24 + 2 * n:26 + 2 * n, :], 2 * T)
            pe.wait_ge(rope_done, len(ROPE_TURNS))
            attend(range(NSA[0], MEM1[-1] + 1), BESIDE_NSA[ROPED:])
            product("out1", features_unit, operand, made=x_made["nsa_y"])
            norm_sum()
            for n in range(8):
                pe.wait_ge(out_ready, n // 2 + 1)
                if n >= 2:
                    pe.wait_ge(final_kept, n - 1)
                h, c = n % 2, n // 2
                for k in range(4):
                    mm = pe.transpose(bank[5 + n % 2][:, k * P:k * P + P], proj[:, 4 * c + k, h * P:h * P + P],
                                      ident[:, :])
                mm.then_inc(final_turned, 1)

        @block.scalar
        def _(act):
            count = [0]

            def then(ins):
                count[0] += 1
                ins.then_inc(act_order, 1)
                act.wait_ge(act_order, count[0])

            made = [0]
            gemm_of = {b: g for g in PLAN.values() for b in range(g.b0, g.b0 + g.blocks)}
            last_unit = 8 * len(gemm_of)

            def high_unit(g, b, u, more=0):
                r0, rows = g.unit(u)
                n = rows * g.width
                if u % 2 == 0:
                    act.wait_ge(landed[u // 2], 16 * (b + 1) + 2 * more)
                if 8 * b + u >= UNITS:
                    act.wait_ge(units_used, 8 * b + u + 1 - UNITS + more)
                act.activation(w_high[:, u % UNITS, 0:n], ring[:, u // 2, r0 * g.width:r0 * g.width + n], ACT.Copy)\
                   .then_inc(high_ready, 1)

            def high(count):
                for k in range(made[0], min(made[0] + count, last_unit)):
                    high_unit(gemm_of[k // 8], k // 8, k % 8)
                made[0] += count

            def high_parts(name):
                g = PLAN[name]
                turns = g.blocks - 1
                if turns >= 3:
                    with act.Fori(0, turns) as i:
                        for u in range(4, 12):
                            high_unit(g, g.b0 + u // 8, u % 8, i * 8)
                    made[0] += 8 * turns
                else:
                    high(8 * turns)
                high(8)

            normed = [0]

            def inverse_root(out, mean_of, n):
                then(act.activation(out, mean_of, ACT.Ln, scale=1.0 / n, bias=eps_col[:, 0:1]))
                return act.activation(out, out, ACT.Exp, scale=-0.5)

            def norm_squares_and_root(name=None, squares=scratch):
                n = normed[0]
                for c in range(4):
                    if name:
                        act.wait_ge(evacuated, PLAN[name].g0 + c + 1)
                    act.activation(squares[:, c * 1024:c * 1024 + 1024],
                                   hT[:, 4 * c:4 * c + 4, :].rearrange("p a t -> p (a t)"), ACT.Square)\
                       .then_inc(norm_squares, 1)
                act.wait_ge(norm_sums, n + 1)
                inverse_root(rstd[:, 0, 0:T], bank[4][:, 0:T], D).then_inc(norm_root, 1)
                normed[0] += 1

            def row_squares(n):
                act.wait_ge(tokens_in, 16 * (n + 2))
                then(act.activation(pair_tile(48, 8), tokens[:, 0, :], ACT.Square, accum_out=tok_rstd[:, 0:1]))
                act.activation(pair_tile(48, 8), tokens[:, 1, :], ACT.Square,
                               accum_out=tok_rstd[:, 1:2]).then_inc(rows_squared, 1)
                act.wait_ge(rows_squared, 2 * n + 1)
                act.activation(tok_rstd[:, 2:4], tok_rstd[:, 0:2], ACT.Sqrt, scale=1.0 / D, bias=eps_col[:, 0:1])\
                   .then_inc(rows_squared, 1)

            def heads(pairs, units, also={}):
                first, end = pairs[0], pairs[-1] + 1
                for k, beside in enumerate(side_by_side(units, len(pairs) + 1)):
                    n, m = first + k, first + k - 1
                    high(len(beside))
                    if n < end:
                        if n >= 2:
                            act.wait_ge(head_sums, n - 1)
                        act.activation(head_sq[:, n % 2, :], pair_tile(norm_pairs[n][0]), ACT.Square)\
                           .then_inc(head_squares, 1)
                    if m >= first:
                        act.wait_ge(head_sums, m + 1)
                        if m >= 2:
                            act.wait_ge(head_normed, m - 1)
                        inverse_root(rstd[:, m % 2, :], bank[4 + m % 2][:, :], HD).then_inc(head_root, 1)
                    if k in also:
                        also[k]()

            def exps(n):
                it = items[n]
                act.wait_ge(max_ready, n + 1)
                if n >= 2:
                    act.wait_ge(probs_turned, n - 1)
                for h in range(TH):
                    w = it.widths[h]
                    src = bank[4 + n % 2][:, h * T:h * T + w] if it.mask is None else masked_scores[:, n % 2, h, 0:w]
                    last = act.activation(probs[:, n % 2, h, 0:w], src, ACT.Exp, scale=ATT_SCALE,
                                          bias=stats[:, n % 2, 2 + h:3 + h], accum_out=stats[:, n % 2, 4 + h:5 + h])
                last.then_inc(exp_ready, 1)

            def keep_turned(n):
                it = items[n]
                act.wait_ge(probs_turned, n + 1)
                if n >= 2:
                    act.wait_ge(values_summed, n - 1)
                r = N_CMP if it.widths == CMP else P
                c = slice(P, 3 * P) if it.widths == CMP else (slice(P, 4 * P) if it.widths == CAUSAL else slice(0, 4 * P))
                act.activation(probsT[0:r, n % 2, c], bank[6][0:r, c], ACT.Copy).then_inc(turned_kept, 1)

            def attend(which, units=()):
                first, end = which[0], which[-1] + 1
                for k, beside in enumerate(side_by_side(units, len(which) + 2)):
                    n = first + k
                    high(len(beside))
                    if n < end:
                        exps(n)
                    if first < n <= end:
                        keep_turned(n - 1)
                    if n == SILU_STEP:
                        act.wait_ge(evacuated, PLAN["nsa_qm"].g0)
                        for t in (36, 40, 44):
                            act.activation(pair_tile(t, 4), pair_tile(t, 4), ACT.Silu).then_inc(silu_ready, 1)

            high(UNITS)
            act.wait_ge(rows_kept, 8)
            norm_squares_and_root()
            act.wait_ge(hg_dve, 1)
            act.activation(lower[:, 0:8], lower[:, 8:16], ACT.Sigmoid).then_inc(hg_act, 1)
            high_parts("hgrn_qf")
            high_parts("hgrn_v")
            act.wait_ge(evacuated, PLAN["hgrn_v"].g0)
            for hg in range(4):
                qs, fs = hg_tiles(hg)
                act.activation(fs, fs, ACT.Sigmoid).then_inc(hg_act, 1)
                act.wait_ge(hg_dve, 3 * hg + 1)
                act.activation(hg_tmp, qs, ACT.Sigmoid).then_inc(hg_act, 1)
                act.wait_ge(hg_dve, 3 * hg + 2)
                act.activation(hg_logf, fs, ACT.Ln).then_inc(hg_act, 1)
                for s in range(STEPS):
                    if s != len(LEVELS):
                        act.wait_ge(hg_exp, exps_before(hg, s) + 1)
                        act.activation(hg_decay, hg_decay, ACT.Exp).then_inc(hg_exp, 1)
                    if s < 8:
                        high(2)
            high_parts("idx_tail")
            act.wait_ge(evacuated, PLAN["gate_q_k"].g0 + 2)
            for t in (16, 20):
                act.activation(pair_tile(t, 4), pair_tile(t, 4), ACT.Silu).then_inc(hg_act, 1)

            def hgrn_square(m):
                act.wait_ge(hg_out, m + 1)
                if m:
                    act.wait_ge(hg_sum, m)
                act.activation(hg_osq, bank[6 + m % 2][:, :], ACT.Square).then_inc(hg_square, 1)

            def hgrn_root(m):
                act.wait_ge(hg_sum, m + 1)
                if m:
                    act.wait_ge(hg_done, m)
                inverse_root(rstd[:, 0, :], bank[5][:, :], HD).then_inc(hg_root, 1)

            for n, beside in enumerate(side_by_side(BESIDE_INDEX, HGRN_OUT_STEPS + IDX_STEPS)):
                high(len(beside))
                if 1 <= n <= 4:
                    hgrn_root(n - 1)
                if n < 4:
                    hgrn_square(n)
                if n >= HGRN_OUT_STEPS:
                    m = n - HGRN_OUT_STEPS
                    if m == IDX_ROWS_STEP:
                        row_squares(0)
                    act.wait_ge(idx_logits, m + 1)
                    if m >= 2:
                        act.wait_ge(idx_added, m - 1)
                    act.activation(idx_relus[:, m % 2, :], bank[4 + m % 2][:, 0:3 * P], ACT.Relu).then_inc(idx_relu, 1)

            high(LEAD)
            heads(MIX_PAIRS, BESIDE_MIX_HEADS[LEAD:], {ROWS_STEP: lambda: row_squares(1)})
            high(LEAD)
            attend(DSA, BESIDE_DSA[LEAD:])
            high_parts("mix_out")

            norm_squares_and_root("mix_out", pair_tile(16, 16))
            high_parts("cross_q")
            high(LEAD)
            act.wait_ge(evacuated, PLAN["mem_k1"].g0)
            heads(CROSS_PAIRS, BESIDE_CROSS[LEAD:CROSS_HEADS])
            attend(CROSS, BESIDE_CROSS[CROSS_HEADS:])
            high_parts("cross_out")

            norm_squares_and_root("cross_out")
            for part in range(4):
                high_parts(f"up{part}")
                high_parts(f"down{part}")

            norm_squares_and_root("down3")
            high_parts("pool_in")
            act.wait_ge(evacuated, PLAN["pool_qm"].g0)
            for t in (12, 16, 20):
                act.activation(pair_tile(t, 4), pair_tile(t, 4), ACT.Silu).then_inc(silu_ready, 1)
            high_parts("pool_qm")
            attend(MEM0, units_of("pool_zm"))
            act.wait_ge(evacuated, PLAN["pool_mix"].g0)
            act.activation(pair_tile(28, 4), pair_tile(28, 4), ACT.Silu).then_inc(silu_ready, 1)
            high_parts("pool_mix")
            high_parts("out0")

            norm_squares_and_root("out0")
            for name in ("cmp_kv", "sel_k", "sel_v", "win_k", "win_v"):
                high_parts(name)
            act.wait_ge(rope_angle, 1)
            act.activation(rope_s[:, :], rope_s[:, :], ACT.Sin).then_inc(rope_sin, 1)
            act.activation(rope_c[:, :], rope_c[:, :], ACT.Sin, scale=-1.0, bias=eps_col[0:ROT, 1:2]).then_inc(rope_sin, 1)
            for c, name in enumerate(("cmp_hid_k", "cmp_hid_v")):
                high_parts(name)
                g = PLAN[name].g0
                act.wait_ge(units_used, PLAN[name].made())
                act.activation(hid_rows[:, c, :], bank[2 * (g % 2)][0:4 * N_CMP, 0:PLAN[name].width], ACT.Silu)\
                   .then_inc(hid_act, 1)
            high_parts("nsa_q")
            act.wait_ge(hid_turned, 1)
            act.activation(hidT.rearrange("p c m n -> p (c m) n"),
                           bank[6][:, 0:256].rearrange("p (a n) -> p a n", a=4)[:, :, 0:4 * N_CMP],
                           ACT.Copy).then_inc(hid_act, 1)
            high_parts("nsa_gate")
            high(ROPED)
            act.wait_ge(evacuated, PLAN["nsa_gate"].g0 + 1)
            gates = nsa_gates[:, :, :].rearrange("p h n -> p (h n)")
            act.activation(gates, gates, ACT.Sigmoid).then_inc(silu_ready, 1)
            attend(range(NSA[0], MEM1[-1] + 1), BESIDE_NSA[ROPED:])
            act.wait_ge(evacuated, PLAN["out1"].g0)
            act.activation(pair_tile(52, 4), pair_tile(52, 4), ACT.Silu).then_inc(silu_ready, 1)
            high_parts("out1")
            norm_squares_and_root("out1")

        @block.vector
        def _(dve):
            count = [0]

            def then(ins):
                count[0] += 1
                ins.then_inc(dve_order, 1)
                dve.wait_ge(dve_order, count[0])

            def read_out(g, q, i, dst):
                n = g.g0 + q
                dve.wait_ge(units_used, i * (2 * g.units) + g.made(q))
                for c in range(2):
                    last = dve.tensor_copy(dst(i * 2 + q, c), bank[2 * (n % 2) + c][:, :])
                last.then_inc(evacuated, 1)

            def keep(name, dst):
                g = PLAN[name]
                if g.groups < 4:
                    for n in range(g.groups):
                        read_out(g, n, 0, dst)
                else:
                    with dve.Fori(0, g.groups // 2) as i:
                        for q in range(2):
                            read_out(g, q, i, dst)

            def tiles(t0):
                return lambda n, c: proj[:, bass.ds(n * 4 + (t0 + 2 * c), 2), :].rearrange("p a t -> p (a t)")

            def rows(v):
                return lambda n, c: v[:, c, bass.ds(n * 512, 512)]

            def residual(name):
                g = PLAN[name]
                dve.wait_ge(evacuated, g.g0)
                with dve.Fori(0, 2) as i:
                    for q in range(2):
                        n = g.g0 + q
                        dve.wait_ge(units_used, i * (2 * g.units) + g.made(q))
                        for c in range(2):
                            h = hT[:, bass.ds(i * 8 + (4 * q + 2 * c), 2), :].rearrange("p a t -> p (a t)")
                            last = dve.tensor_tensor(h, bank[2 * (n % 2) + c][:, :], h, ALU.add)
                        last.then_inc(evacuated, 1)

            def flat(x, t, n):
                return x[:, t:t + n, :].rearrange("p a t -> p (a t)")

            def split(src, high, low):
                then(dve.tensor_copy(high, src))
                return dve.tensor_tensor(low, src, high, ALU.subtract)

            def split_gated(name, c0, runs):
                for c, (t, z, silus) in enumerate(runs):
                    dve.wait_ge(silu_ready, silus)
                    y = pair_tile(t, 4)
                    then(dve.tensor_tensor(y, y, pair_tile(z, 4), ALU.mult))
                    split(y, flat(x_high, 4 * (c0 + c), 4), flat(x_low, 4 * (c0 + c), 4)).then_inc(x_ready, 1)

            def split_tiles(name, sources, n=4):
                for c, t in enumerate(sources):
                    split(pair_tile(t, n), flat(x_high, n * c, n), flat(x_low, n * c, n)).then_inc(x_ready, 1)

            normed = [0]

            kept_rstd = pair_tile(40, 1)

            def normed_tile(out, kt, slot, cols, scale):
                return dve.scalar_tensor_tensor(out=out, in0=hT[:, kt, :],
                                                scalar=gains[:, slot, cols.start + kt:cols.start + kt + 1],
                                                in1=scale, op0=ALU.mult, op1=ALU.mult)

            def norm(name, slot, cols, again=False):
                if again:
                    scale = kept_rstd
                else:
                    scale = rstd[:, 0, 0:T]
                    dve.wait_ge(norm_root, normed[0] + 1)
                for c in range(4):
                    tmp = heads_scratch[:, (c % 2) * 1024:(c % 2) * 1024 + 1024]
                    if c >= 2:
                        dve.wait_ge(x_ready, x_made[name] + c - 1)
                    for k in range(4):
                        last = normed_tile(tmp[:, k * T:k * T + T], 4 * c + k, slot, cols, scale)
                    then(last)
                    split(tmp, flat(x_high, 4 * c, 4), flat(x_low, 4 * c, 4)).then_inc(x_ready, 1)
                normed[0] += not again
                dve.wait_ge(x_ready, x_made[name] + 4)

            def scale_rows(n):
                dve.wait_ge(rows_squared, 2 * n + 2)
                then(dve.reciprocal(tok_rstd[:, 4:6], tok_rstd[:, 2:4]))
                for h in range(TH):
                    last = dve.tensor_scalar(tokens[:, h, :], tokens[:, h, :], tok_rstd[:, 4 + h:5 + h], None, ALU.mult)
                last.then_inc(rows_scaled, 1)

            turned = [0]

            def keep_rows():
                for n in range(KT // 2):
                    m = turned[0]
                    dve.wait_ge(rows_turned, m + 1)
                    dve.tensor_copy(flat(hT, 2 * n, 2), bank[5 + m % 3][:, :]).then_inc(rows_kept, 1)
                    turned[0] += 1

            def operand_rows(name, cols):
                for n in range(KT // 2):
                    m = turned[0]
                    dve.wait_ge(rows_turned, m + 1)
                    srcs = [(2 * n + c, bank[5 + m % 3][:, c * T:c * T + T],
                             gains[:, 0, cols.start + 2 * n + c:cols.start + 2 * n + c + 1]) for c in range(2)]
                    for t, src, gain in srcs:
                        last = dve.tensor_scalar(x_high[:, t, :], src, gain, None, ALU.mult)
                    then(last)
                    for t, src, gain in srcs:
                        last = dve.scalar_tensor_tensor(out=x_low[:, t, :], in0=src, scalar=gain, in1=x_high[:, t, :],
                                                        op0=ALU.mult, op1=ALU.subtract)
                    last.then_inc(rows_kept, 1)
                    turned[0] += 1
                    if n % 2:
                        dve.wait_ge(rows_kept, turned[0])
                        dve.sem_inc(x_ready, 1)

            def read_out_ended(beside, places):
                for name, u in beside:
                    if u % 8 == 7:
                        read_out(PLAN[name], u // 8, 0, places[name])

            def heads(pairs, units, places, between=(), also={}):
                for k, beside in enumerate(side_by_side(units, len(pairs) + 1)):
                    read_out_ended(beside, places)
                    if k:
                        n = pairs[0] + k - 1
                        t, col = norm_pairs[n]
                        dve.wait_ge(head_root, n + 1)
                        dve.scalar_tensor_tensor(out=pair_tile(t), in0=pair_tile(t), scalar=gains[:, 1, col:col + 1],
                                                 in1=rstd[:, n % 2, :], op0=ALU.mult, op1=ALU.mult)\
                           .then_inc(head_normed, 1)
                    for work in between[len(between) * k // (len(pairs) + 1):len(between) * (k + 1) // (len(pairs) + 1)]:
                        work()
                    if k in also:
                        also[k]()

            def maxima(n):
                it = items[n]
                st = stats[:, n % 2, :]
                dve.wait_ge(scores_ready, n + 1)
                if n >= 2:
                    dve.wait_ge(exp_ready, n - 1)
                s = bank[4 + n % 2][:, :].rearrange("p (h s) -> p h s", h=TH)
                if it.mask is None:
                    last = dve.tensor_reduce(st[:, 0:2], s, AX, ALU.max)
                else:
                    for h in range(TH):
                        w = it.widths[h]
                        last = dve.tensor_tensor_reduce(masked_scores[:, n % 2, h, 0:w], s[:, h, 0:w],
                                                        it.mask[:, h, 0:w], 1.0, -3.4e38, ALU.add, ALU.max,
                                                        st[:, h:h + 1])
                then(last)
                dve.tensor_scalar(st[:, 2:4], st[:, 0:2], NEG / 8, -ATT_SCALE, ALU.max, ALU.mult)\
                   .then_inc(max_ready, 1)

            def normalise(n):
                it = items[n]
                st = stats[:, n % 2, :]
                dve.wait_ge(exp_ready, n + 1)
                sums = st[:, 4:6]
                if it.widths == CMP:
                    sums = st[:, 10:12]
                    then(dve.tensor_scalar(sums, st[:, 4:6], 1e-30, None, ALU.max))
                then(dve.reciprocal(st[:, 6:8], sums))
                if it.gate is not None:
                    then(dve.tensor_tensor(st[:, 6:8], st[:, 6:8], it.gate, ALU.mult))
                for h in range(TH):
                    w = it.widths[h]
                    p = probs[:, n % 2, h, 0:w]
                    last = dve.tensor_scalar(p, p, st[:, 6 + h:7 + h], None, ALU.mult)
                last.then_inc(probs_ready, 1)

            def keep_out(n):
                it = items[n]
                if not it.last:
                    return
                o = bank[7][:, 0:T]
                dve.wait_ge(values_summed, n + 1)
                dve.tensor_copy(it.out, o).then_inc(out_kept, 1)

            def attend(which, units=(), places=None):
                first, end = which[0], which[-1] + 1
                for k, beside in enumerate(side_by_side(units, len(which) + 2)):
                    n = first + k
                    read_out_ended(beside, places)
                    if first <= n - 1 < end:
                        normalise(n - 1)
                    if n < end:
                        maxima(n)
                    if first <= n - 2 < end:
                        keep_out(n - 2)
                dve.wait_ge(out_kept, outs_before[end])

            dve.wait_ge(gains_turned, 1)
            dve.tensor_copy(gains[:, 0, :], bank[4][:, 0:P])
            dve.tensor_copy(gains[:, 1, 0:65], bank[4][:, P:P + 65])
            dve.tensor_copy(pe_cols[:, :, :].rearrange("p i l -> p (i l)"), bank[4][:, 2 * P:2 * P + 64])\
               .then_inc(gains_ready, 1)
            keep_rows()
            dve.wait_ge(gains_ready, 1)
            lb0 = gains[:, 1, G_LB.start:G_LB.start + 8]
            lb1 = gains[:, 1, G_LB.start + 8:G_LB.start + 16]
            dve.tensor_tensor(lower[:, 8:16], lb0, lb1, ALU.subtract).then_inc(hg_dve, 1)
            norm("mix", 0, G_MIX)
            dve.wait_ge(hg_act, 1)
            dve.wait_ge(consts_ready, 3)
            then(dve.tensor_scalar(lower[:, 8:16], lower[:, 0:8], -1.0, 1.0, ALU.mult, ALU.add))
            dve.memset(hg_diag, 0.0).then_inc(hg_placed, 1)
            keep("hgrn_qf", tiles(0))
            keep("hgrn_v", rows(hgrn_v))
            dve.wait_ge(evacuated, PLAN["hgrn_v"].g0 + 2)

            def place(hg, s):
                dve.wait_ge(hg_placed, STEPS * hg + s + 1)
                dve.wait_ge(hg_scores, STEPS * hg + s + 1)
                diag = hg_diag[:, 4 * hg:4 * hg + 4, :]
                if s < len(LEVELS):
                    w = LEVELS[s]
                    out = diag.rearrange("p m (b two w) -> p m b two w", two=2, w=w)[:, :, :, 1, :]
                    mask = spread(level_mask[:, s:s + 1, :], 1, 4).rearrange("p m (b w) -> p m b w", w=w)
                    got = bank[4 + s % 2][:, 0:4 * CHUNK_T].rearrange("p (m b w) -> p m b w", m=4, w=w)
                    last = dve.copy_predicated(out, mask.bitcast(I32), got)
                elif s == len(LEVELS):
                    last = dve.copy_predicated(diag, spread(ident[:, :].rearrange("p (m t) -> p m t", m=1), 1, 4)
                                               .bitcast(I32), bank[5][:, :].rearrange("p (m t) -> p m t", m=4))
                else:
                    last = dve.tensor_copy(hg_cross[:, 2 * hg:2 * hg + 2, :].rearrange("p m t -> p (m t)"),
                                           bank[4][:, 0:T])
                last.then_inc(hg_placed, 1)

            for hg in range(4):
                qs, fs = hg_tiles(hg)
                dve.wait_ge(hg_act, 1 + 3 * hg + 1)
                for h in range(2):
                    f = fs[:, h * T:h * T + T]
                    c = 2 * hg + h
                    last = dve.tensor_scalar(f, f, lower[:, 8 + c:9 + c], lower[:, c:c + 1], ALU.mult, ALU.add)
                last.then_inc(hg_dve, 1)
                dve.wait_ge(hg_act, 1 + 3 * hg + 2)
                dve.scalar_tensor_tensor(out=qs, in0=qs, scalar=ATT_SCALE, in1=hg_tmp, op0=ALU.mult, op1=ALU.mult)\
                   .then_inc(hg_dve, 1)
                dve.wait_ge(hg_act, 1 + 3 * hg + 3)
                dve.tensor_scalar(fs, fs, -1.0, 1.0, ALU.mult, ALU.add).then_inc(hg_dve, 1)
                then(dve.tensor_tensor_scan(hg_cum, hg_reset, hg_logf, 0.0, ALU.mult, ALU.add))
                dve.wait_ge(hg_dve, 3 * hg + 4)

                for s in range(STEPS):
                    step = STEPS * hg + s
                    if step:
                        dve.wait_ge(hg_operands, step)
                    if s < len(LEVELS):
                        w = LEVELS[s]
                        cum = hg_cum.rearrange("p (b two w) -> p b two w", two=2, w=w)
                        dec = hg_decay.rearrange("p (b two w) -> p b two w", two=2, w=w)
                        mid = spread(cum[:, :, 0, w - 1:w], 2, w)
                        if w < CHUNK_T:
                            dve.tensor_tensor(dec[:, :, 1, :], cum[:, :, 1, :], mid, ALU.subtract)
                        else:
                            dve.tensor_copy(dec[:, :, 1, :], cum[:, :, 1, :])
                        dve.tensor_tensor(dec[:, :, 0, :], mid, cum[:, :, 0, :], ALU.subtract).then_inc(hg_exp, 1)
                    elif s > len(LEVELS):
                        cum = hg_cum.rearrange("p (h c t) -> p h c t", h=2, c=4)
                        dec = hg_decay.rearrange("p (h c t) -> p h c t", h=2, c=4)
                        total = lambda c: spread(cum[:, :, c, CHUNK_T - 1:CHUNK_T], 2, CHUNK_T)
                        dve.tensor_copy(dec[:, :, 2, :], cum[:, :, 2, :])
                        dve.tensor_tensor(dec[:, :, 3, :], cum[:, :, 3, :], total(2), ALU.add)
                        dve.tensor_tensor(dec[:, :, 1, :], total(1), cum[:, :, 1, :], ALU.subtract)
                        then(dve.tensor_tensor(dec[:, :, 0, :], total(0), cum[:, :, 0, :], ALU.subtract))
                        dve.tensor_tensor(dec[:, :, 0, :], dec[:, :, 0, :], total(1), ALU.add).then_inc(hg_exp, 1)
                    if s != len(LEVELS):
                        dve.wait_ge(hg_exp, exps_before(hg, s) + 2)
                    if step:
                        dve.wait_ge(hg_scores, step)
                    if s < len(LEVELS):
                        dve.tensor_tensor(hg_keys, fs, hg_decay, ALU.mult)
                        q4 = qs.rearrange("p (b two w) -> p b two w", two=2, w=w)
                        last = dve.tensor_tensor(hg_queries[:, 0:T].rearrange("p (b w) -> p b w", w=w), q4[:, :, 1, :],
                                                 dec[:, :, 1, :], ALU.mult)
                    elif s == len(LEVELS):
                        dve.tensor_copy(hg_keys, fs)
                        last = dve.tensor_copy(hg_queries, qs)
                    else:
                        halves = lambda x: x.rearrange("p (h c t) -> p h c t", h=2, c=2)
                        dve.tensor_tensor(halves(hg_keys)[:, :, 0, :], halves(fs)[:, :, 0, :],
                                          halves(hg_decay)[:, :, 0, :], ALU.mult)
                        last = dve.tensor_tensor(hg_queries[:, 0:T].rearrange("p (h t) -> p h t", h=2),
                                                 halves(qs)[:, :, 1, :], halves(hg_decay)[:, :, 1, :], ALU.mult)
                    last.then_inc(hg_operands, 1)
                    if s:
                        place(hg, s - 1)
                    if s in (4, 8):
                        read_out(PLAN["gate_q_k"], 2 * hg + (s == 8), 0, tiles(16))
                place(hg, STEPS - 1)
            g = PLAN["idx_tail"]
            dve.wait_ge(units_used, g.made())
            dve.wait_ge(hg_placed, 4 * STEPS + 1)
            pair = bank[2 * (g.g0 % 2)], bank[2 * (g.g0 % 2) + 1]
            for h in range(TH):
                last = dve.tensor_copy(idx_rows[:, h, 0:64], pair[h][:, 0:64])
            last.then_inc(idx_keys, 1)
            for h in range(TH):
                last = dve.tensor_scalar(idx_w[:, h, :], pair[h][:, 64:80], IDX_SCALE, None, ALU.mult)
            last.then_inc(evacuated, 1)
            dve.wait_ge(hg_act, 15)

            def hgrn_output(m):
                if m:
                    dve.wait_ge(hg_done, m)
                dve.wait_ge(hg_root, m + 1)
                then(dve.scalar_tensor_tensor(out=hg_tmp, in0=bank[6 + m % 2][:, :],
                                              scalar=gains[:, 1, G_ONORM:G_ONORM + 1], in1=rstd[:, 0, :],
                                              op0=ALU.mult, op1=ALU.mult))
                dve.tensor_tensor(pair_tile(16 + 2 * m), hg_tmp, pair_tile(16 + 2 * m), ALU.mult).then_inc(hg_done, 1)

            both = [(0, slice(0, P), P), (1, slice(P, P + T), T)]

            def add_index_head(n):
                dve.wait_ge(idx_relu, n + 1)
                if n:
                    dve.wait_ge(idx_added, n)
                for h, c, w in both:
                    acc, r, wt = idx_score[:, h, 0:w], idx_relus[:, n % 2, c], idx_w[:, h, n:n + 1]
                    if n == 0:
                        last = dve.tensor_scalar(acc, r, wt, None, ALU.mult)
                    else:
                        last = dve.scalar_tensor_tensor(out=acc, in0=r, scalar=wt, in1=acc, op0=ALU.mult, op1=ALU.add)
                last.then_inc(idx_added, 1)

            for n, beside in enumerate(side_by_side(BESIDE_INDEX, HGRN_OUT_STEPS + IDX_STEPS)):
                read_out_ended(beside, {"attn_v": rows(attn_v)})
                if 1 <= n <= 4:
                    hgrn_output(n - 1)
                if n == 5:
                    dve.wait_ge(idx_turned, 1)
                    dve.tensor_copy(ikT[0:64, :], bank[4][0:64, 0:T])
                    dve.tensor_copy(ikT[64:128, :], bank[4][0:64, 0:T]).then_inc(idx_keys, 1)
                if n >= HGRN_OUT_STEPS:
                    add_index_head(n - HGRN_OUT_STEPS)
                if n == HGRN_OUT_STEPS + IDX_ROWS_STEP + 2:
                    scale_rows(0)
            dve.wait_ge(idx_added, IDX_HEADS)

            def mask_works(h, w):
                acc, bias = idx_score[:, h, 0:w], sel_bias[:, h, 0:w]

                def start():
                    then(dve.tensor_tensor(acc, acc, causal[:, h, 0:w], ALU.add))

                def eight_best():
                    then(dve.max(best[:, h, :], acc))
                    then(dve.match_replace(acc, best[:, h, :], acc, TAKEN))

                def end():
                    then(dve.tensor_scalar(bias, acc, TAKEN / 2, NEG, ALU.is_gt, ALU.mult))
                    then(dve.tensor_tensor(bias, bias, causal[:, h, 0:w], ALU.min))
                return [start] + [eight_best] * (TOPK // 8) + [end]

            operand_rows("cross_mem", G_MEM)
            heads(MIX_PAIRS, BESIDE_MIX_HEADS[LEAD:], {"cross_k": tiles(8), "cross_v": rows(cross_v)},
                  [work for h, _, w in both for work in mask_works(h, w)], {ROWS_STEP + 1: lambda: scale_rows(1)})
            operand_rows("mem0", G_M2A)
            attend(DSA, BESIDE_DSA[LEAD:], {"mem_k0": tiles(48), "mem_v0": rows(mem_v0)})
            split_tiles("mix_y", (16, 20, 24, 28))
            residual("mix_out")

            norm("cross", 0, G_CROSS)
            keep("cross_q", tiles(16))
            operand_rows("mem1", G_M2B)
            places = {"mem_k1": tiles(56), "mem_v1": rows(mem_v1)}
            heads(CROSS_PAIRS, BESIDE_CROSS[LEAD:CROSS_HEADS], places)
            attend(CROSS, BESIDE_CROSS[CROSS_HEADS:], places)
            split_tiles("cross_y", (28,))
            residual("cross_out")

            norm("mlp", 0, G_MLP)
            squares = heads_scratch[:, 0:1024]
            dve.sem_inc(hidden_ready, 1)
            for part in range(4):
                g = PLAN[f"up{part}"]
                with dve.Fori(0, 2) as i:
                    for q in range(2):
                        n = g.g0 + q
                        dve.wait_ge(hidden_ready, i * 2 + (4 * part + q + 1))
                        dve.wait_ge(units_used, i * (2 * g.units) + g.made(q))
                        for c in range(2):
                            last = dve.tensor_scalar(squares[:, c * 512:c * 512 + 512], bank[2 * (n % 2) + c][:, :],
                                                     0.0, None, ALU.max)
                        last.then_inc(evacuated, 1)
                        dve.wait_ge(evacuated, i * 2 + (n + 1))
                        dve.tensor_tensor(squares, squares, squares, ALU.mult).then_inc(hidden_squared, 1)
                        dve.wait_ge(hidden_squared, i * 4 + (8 * part + 2 * q + 1))
                        high, low = (hidden[:, c, bass.ds(i * 8 + 4 * q, 4), :].rearrange("p a t -> p (a t)")
                                     for c in range(2))
                        dve.tensor_copy(high, squares).then_inc(hidden_squared, 1)
                        dve.wait_ge(hidden_squared, i * 4 + (8 * part + 2 * q + 2))
                        dve.tensor_tensor(low, squares, high, ALU.subtract).then_inc(hidden_ready, 1)
                residual(f"down{part}")

            norm("pool", 0, G_2A)
            count_t, one_t = heads_scratch[:, 1536:1792], heads_scratch[:, 1792:2048]
            then(dve.memset(one_t, 1.0))
            then(dve.tensor_tensor_scan(count_t, one_t, one_t, 0.0, ALU.mult, ALU.add))
            for n, win in enumerate(POOL_WINDOWS):
                then(dve.tensor_scalar(pair_tile(44 + n, 1), count_t, float(win), None, ALU.min))
                then(dve.reciprocal(pair_tile(44 + n, 1), pair_tile(44 + n, 1)))
            keep("pool_in", tiles(0))
            dve.wait_ge(evacuated, PLAN["pool_qm"].g0)
            ping = [heads_scratch[:, c:c + 3 * T].rearrange("p (m t) -> p m t", m=3) for c in (0, 3 * T)]
            for n, win in enumerate(POOL_WINDOWS):
                u = proj[:, 3 * n:3 * n + 3, :]
                src = u
                for s in range(n + 1):
                    d = 1 << s
                    dst = ping[s % 2]
                    dve.tensor_copy(dst[:, :, 0:d], src[:, :, 0:d])
                    then(dve.tensor_tensor(dst[:, :, d:T], src[:, :, d:T], src[:, :, 0:T - d], ALU.add))
                    src = dst
                rc = spread(proj[:, 44 + n:45 + n, :], 1, 3)
                then(dve.tensor_tensor(src, src, rc, ALU.mult))
                then(dve.tensor_tensor(proj[:, 32 + 3 * n:35 + 3 * n, :], src, u, ALU.subtract))
            keep("pool_qm", tiles(24))
            attend(MEM0, units_of("pool_zm"), {"pool_zm": tiles(28)})
            split_tiles("pooled", (32, 35, 38, 41), 3)
            dve.wait_ge(silu_ready, 4)
            for j in range(4):
                g = PLAN["pool_mix"].g0 + j
                dve.wait_ge(units_used, PLAN["pool_mix"].made(j))
                for f in range(3):
                    t = 3 * j + f
                    last = dve.scalar_tensor_tensor(out=proj[:, 12 + t, :],
                                                    in0=bank[2 * (g % 2) + f // 2][:, (f % 2) * T:(f % 2) * T + T],
                                                    scalar=gains[:, 1, G_POOL.start + t:G_POOL.start + t + 1],
                                                    in1=proj[:, 12 + t, :], op0=ALU.mult, op1=ALU.mult)
                last.then_inc(evacuated, 1)
            dve.wait_ge(evacuated, PLAN["out0"].g0)
            split_tiles("pool_y", (12, 16, 20))
            split_gated("pool_y", 3, ((24, 28, 4),))
            residual("out0")

            norm("kv", 1, G_KV)
            then(dve.tensor_copy(kept_rstd, rstd[:, 0, 0:T]))
            keep("cmp_kv", tiles(0))
            keep("sel_k", tiles(8))
            keep("sel_v", rows(sel_v))
            keep("win_k", tiles(16))
            keep("win_v", rows(win_v))
            dve.wait_ge(misc_in, 32)
            dve.tensor_copy(rstd[0:1, 0, 0:T], pos_i[:, :]).then_inc(rope_pos, 1)
            dve.wait_ge(rope_pos, 2)
            col = stats[0:ROT, 0, 8:9]
            then(dve.tensor_copy(col, bank[6][0:ROT, 0:1]))
            ang, turns = rope_s[:, :], rope_c[:, :]
            then(dve.tensor_scalar(ang, bank[5][0:ROT, 0:T], col, None, ALU.mult))
            then(dve.tensor_scalar(turns, ang, 0.15915494309189535, 12582912.0, ALU.mult, ALU.add))
            then(dve.tensor_scalar(turns, turns, 12582912.0, None, ALU.subtract))
            for part in TWO_PI_PARTS:
                then(dve.scalar_tensor_tensor(out=ang, in0=turns, scalar=-part, in1=ang, op0=ALU.mult, op1=ALU.add))
            then(dve.tensor_scalar(ang, ang, 3.1415925, -3.1415925, ALU.min, ALU.max))
            then(dve.tensor_scalar(turns, ang, -1.0, None, ALU.mult))
            dve.tensor_tensor(turns, turns, ang, ALU.max).then_inc(rope_angle, 1)
            dve.wait_ge(rope_sin, 2)
            dve.sem_inc(rope_tables, 1)

            def rotate(n):
                x, tiles_, t_from = ROPE_TURNS[n]
                if t_from is None:
                    c = spread(rope_c[:, :].rearrange("p (m t) -> p m t", m=1), 1, 2)
                    s = spread(rope_s[:, :].rearrange("p (m t) -> p m t", m=1), 1, 2)
                    view = lambda y: y[0:ROT, 0:2 * T].rearrange("p (m t) -> p m t", m=2)
                else:
                    c, s = (spread(y[:, t_from:T:CMP_STRIDE].rearrange("p (m t) -> p m t", m=1), 1, 4)
                            for y in (rope_c, rope_s))
                    view = lambda y: y[0:ROT, 0:4 * N_CMP].rearrange("p (m t) -> p m t", m=4)
                b = bank[5 + n % 2]
                a_, b_ = view(rstd[:, 0, :]), view(rstd[:, 1, :])
                if n:
                    dve.wait_ge(rope_done, n)
                dve.wait_ge(rope_swapped, n + 1)
                dve.tensor_tensor(a_, x, c, ALU.mult)
                then(dve.tensor_tensor(b_, view(b), s, ALU.mult))
                dve.tensor_tensor(x, a_, b_, ALU.add).then_inc(rope_done, 1)

            dve.wait_ge(evacuated, PLAN["cmp_hid_k"].g0)
            for n in range(4):
                rotate(n)
            n_blocks = CMP_LEN * 4 * N_CMP
            blocks = heads_scratch[:, 0:n_blocks].rearrange("p (l n) -> p l n", l=CMP_LEN)
            for c in range(2):
                if c:
                    dve.wait_ge(x_ready, x_made["blocks"] + 1)
                for kv in range(4):
                    z = proj[:, 4 * c + kv, :].rearrange("p (m r) -> p r m", r=CMP_STRIDE)
                    for half in range(2):
                        l = slice(CMP_STRIDE * half, CMP_STRIDE * half + CMP_STRIDE)
                        last = dve.tensor_tensor(blocks[:, l, kv * N_CMP:kv * N_CMP + N_CMP],
                                                 z[:, :, half:half + N_CMP],
                                                 spread(pe_cols[:, c, l].rearrange("p (l n) -> p l n", n=1), 2, N_CMP),
                                                 ALU.add)
                then(last)
                split(blocks, zpe(x_high, c), zpe(x_low, c)).then_inc(x_ready, 1)
            for c, name in enumerate(("cmp_hid_k", "cmp_hid_v")):
                dve.wait_ge(hid_act, c + 1)
                dve.sem_inc(evacuated, 1)
            norm("nsa", 0, G_2B, again=True)
            keep("nsa_q", tiles(24))
            dve.wait_ge(cmp_second, 1)
            dve.tensor_copy(vcmp[0:N_CMP, :, :].rearrange("p m d -> p (m d)"), bank[5][0:N_CMP, :])
            dve.tensor_copy(kcmpT[:, 0:4 * N_CMP], bank[7][:, 0:4 * N_CMP]).then_inc(cmp_ready, 1)
            dve.wait_ge(cmp_ready, 1)
            g = PLAN["nsa_gate"]
            dve.wait_ge(units_used, g.made())
            for h in range(TH):
                last = dve.tensor_copy(nsa_gates[:, h, :], bank[2 * (g.g0 % 2) + h][:, 0:36])
            last.then_inc(evacuated, 1)
            for n in range(4, len(ROPE_TURNS)):
                rotate(n)
            dve.wait_ge(silu_ready, 5)
            attend(range(NSA[0], MEM1[-1] + 1), BESIDE_NSA[ROPED:],
                   {"nsa_zq": tiles(36), "nsa_qm": tiles(48), "nsa_zm": tiles(52)})
            split_gated("nsa_y", 0, ((24, 36, 6), (28, 40, 7), (32, 44, 8), (48, 52, 9)))
            residual("out1")

            dve.wait_ge(norm_root, normed[0] + 1)
            for kt in range(KT):
                last = normed_tile(proj[:, kt, :], kt, 1, G_FINAL, rstd[:, 0, 0:T])
                if kt % 4 == 3:
                    last.then_inc(out_ready, 1)
            for n in range(8):
                h, c = n % 2, n // 2
                dve.wait_ge(final_turned, n + 1)
                dve.tensor_copy(tokens[:, h, c * 512:c * 512 + 512], bank[5 + n % 2][:, :]).then_inc(final_kept, 1)


_INS = ['x', 'mem', 'norm_mix', 'w_in', 'hgrn_lb_logits', 'hgrn_onorm', 'attn_qnorm', 'attn_knorm', 'w_out',
        'norm_cross', 'mem_norm', 'wq_x', 'wk_x', 'wv_x', 'wo_x', 'xq_norm', 'xk_norm', 'norm_mlp', 'w_up',
        'w_down', 'mem_2', 'positions_2', 'norm_g_2', 'mem_norm_g_2', 'w_mem_kv_2', 'w_out_2', 'a_w_in_2',
        'a_w_pool_2', 'a_pool_scale_2', 'b_w_in_2', 'kv_norm_g_2', 'w_kv_2', 'cmp_pe_2', 'cmp_w1_2', 'cmp_w2_2',
        'final_g_2']


def kernel(**inputs):
    import numpy as np
    import concourse.bacc as bacc
    from concourse.bass_utils import run_bass_kernel_spmd

    nc = bacc.Bacc("TRN2", target_bir_lowering=False, num_devices=1, dynamic_dma_scratch_size=1024)
    arrays, args = {}, {}
    for name in _INS:
        arr = np.ascontiguousarray(inputs[name])
        arrays[f"in_{name}"] = arr
        args[name] = nc.dram_tensor(f"in_{name}", arr.shape, mybir.dt.from_np(arr.dtype), kind="ExternalInput").ap()
    args["out"] = nc.dram_tensor("out", (1, T, D), F32, kind="ExternalOutput").ap()
    build_program(nc, args)
    r = run_bass_kernel_spmd(nc, [arrays], core_ids=[0])
    return r.results[0]["out"]
```
